# Optimizing a Trainium2 kernel written in Bass

```python
import math
import jax, jax.numpy as jnp
from jax import lax
import numpy as np

D_MODEL = 1024
BATCH = 1
SEQ = 1024
DEPTH = 1

MIX_WIDTH = D_MODEL
HG_HEADS = 4
HG_DK = 128
HG_DV = 128
HG_KEY_WIDTH = HG_HEADS * HG_DK
HG_VAL_WIDTH = HG_HEADS * HG_DV
HG_CHUNK = 64
ATT_HEADS = 8
ATT_KV_HEADS = 2
ATT_GROUP = ATT_HEADS // ATT_KV_HEADS
ATT_HD = 64
ATT_Q_WIDTH = ATT_HEADS * ATT_HD
ATT_KV_WIDTH = ATT_KV_HEADS * ATT_HD
WINDOW = 128
ATT_BLOCK = 128
HG_COLS = 2 * HG_KEY_WIDTH + 2 * HG_VAL_WIDTH
ATT_COLS = ATT_Q_WIDTH + 2 * ATT_KV_WIDTH
IN_COLS = HG_COLS + ATT_COLS
D_FF = 2816
CONV_W = 3
EPS = 1e-6


def rmsnorm(x, w, eps=EPS):
    xf = x.astype(jnp.float32)
    inv = lax.rsqrt(jnp.mean(xf * xf, axis=-1, keepdims=True) + eps)
    return (xf * inv * w.astype(jnp.float32)).astype(x.dtype)

def hgrn2_chunkwise(q, k, v, log_f):
    B, S, H, DK = q.shape
    DV = v.shape[-1]
    n = S // HG_CHUNK

    def to_chunks(a):
        return a.astype(jnp.float32).reshape(B, n, HG_CHUNK, H, a.shape[-1]).transpose(1, 0, 3, 2, 4)

    qc, kc, vc, gc = to_chunks(q), to_chunks(k), to_chunks(v), to_chunks(log_f)
    causal = jnp.tril(jnp.ones((HG_CHUNK, HG_CHUNK), dtype=bool))[:, :, None]

    def step(state, inp):
        qi, ki, vi, gi = inp
        b = jnp.cumsum(gi, axis=2)
        rel = b[:, :, :, None, :] - b[:, :, None, :, :]
        decay = jnp.exp(jnp.where(causal, rel, -jnp.inf))
        scores = jnp.einsum('bhtk,bhsk,bhtsk->bhts', qi, ki, decay)
        intra = jnp.einsum('bhts,bhsv->bhtv', scores, vi)
        inter = jnp.einsum('bhtk,bhkv->bhtv', qi * jnp.exp(b), state)
        b_last = b[:, :, -1:, :]
        new_state = state * jnp.exp(b_last)[:, :, 0, :, None] + jnp.einsum(
            'bhsk,bhsv->bhkv', ki * jnp.exp(b_last - b), vi)
        return new_state, intra + inter

    state0 = jnp.zeros((B, H, DK, DV), jnp.float32)
    _, out = lax.scan(step, state0, (qc, kc, vc, gc))
    return out.transpose(1, 0, 3, 2, 4).reshape(B, S, H, DV)

def sliding_window_attention_with_sinks(q, k, v, sinks):
    B, S = q.shape[0], q.shape[1]
    nb = S // ATT_BLOCK
    scale = 1.0 / math.sqrt(ATT_HD)
    qb = q.astype(jnp.float32).reshape(B, nb, ATT_BLOCK, ATT_KV_HEADS, ATT_GROUP, ATT_HD)

    def band_keys(a):
        ap = jnp.pad(a.astype(jnp.float32), ((0, 0), (ATT_BLOCK, 0), (0, 0), (0, 0)))
        ap = ap.reshape(B, nb + 1, ATT_BLOCK, ATT_KV_HEADS, ATT_HD)
        return jnp.concatenate([ap[:, :-1], ap[:, 1:]], axis=2)

    kb, vb = band_keys(k), band_keys(v)
    scores = jnp.einsum('bnqhgd,bnkhd->bnhgqk', qb, kb) * scale
    qi = jnp.arange(ATT_BLOCK)[:, None]
    kj = jnp.arange(2 * ATT_BLOCK)[None, :]
    dist = qi + ATT_BLOCK - kj
    band = (dist >= 0) & (dist < WINDOW)
    key_pos = jnp.arange(nb)[:, None] * ATT_BLOCK + jnp.arange(2 * ATT_BLOCK)[None, :] - ATT_BLOCK
    mask = band[None] & (key_pos >= 0)[:, None, :]
    scores = jnp.where(mask[None, :, None, None], scores, -jnp.inf)
    sink = sinks.astype(jnp.float32).reshape(ATT_KV_HEADS, ATT_GROUP)[None, None, :, :, None, None]
    m = jnp.maximum(jnp.max(scores, axis=-1, keepdims=True), sink)
    p = jnp.exp(scores - m)
    denom = jnp.sum(p, axis=-1, keepdims=True) + jnp.exp(sink - m)
    out = jnp.einsum('bnhgqk,bnkhd->bnqhgd', p / denom, vb)
    return out.reshape(B, S, ATT_HEADS * ATT_HD)

def causal_depthwise_conv(a, w, b):
    C = a.shape[-1]
    y = lax.conv_general_dilated(
        a, w[:, None, :].astype(a.dtype), window_strides=(1,), padding=[(CONV_W - 1, 0)],
        dimension_numbers=('NWC', 'WIO', 'NWC'), feature_group_count=C)
    return y + b.astype(a.dtype)

def first_inputs(seed: int = 0) -> dict:
    key = jax.random.key(seed)
    ks = jax.random.split(key, 16)
    f32 = jnp.float32
    nrm = lambda k, shape, s: jax.random.normal(k, shape, f32) * s
    return {
        "x": jax.random.normal(ks[0], (BATCH, SEQ, D_MODEL), f32),
        "norm_mix_w": 1.0 + nrm(ks[1], (DEPTH, D_MODEL), 0.02),
        "w_in": nrm(ks[2], (DEPTH, D_MODEL, IN_COLS), D_MODEL ** -0.5),
        "b_attn": nrm(ks[3], (DEPTH, ATT_COLS), 0.02),
        "lb_logits": nrm(ks[4], (DEPTH + 1, HG_KEY_WIDTH), 0.1),
        "hg_norm_w": 1.0 + nrm(ks[5], (DEPTH, HG_DV), 0.02),
        "sinks": nrm(ks[6], (DEPTH, ATT_HEADS), 0.5),
        "w_out": nrm(ks[7], (DEPTH, MIX_WIDTH, D_MODEL), MIX_WIDTH ** -0.5),
        "norm_ffn_w": 1.0 + nrm(ks[8], (DEPTH, D_MODEL), 0.02),
        "w_gate": nrm(ks[9], (DEPTH, D_MODEL, D_FF), D_MODEL ** -0.5),
        "w_up": nrm(ks[10], (DEPTH, D_MODEL, D_FF), D_MODEL ** -0.5),
        "conv_w": nrm(ks[11], (DEPTH, CONV_W, D_FF), CONV_W ** -0.5),
        "conv_b": nrm(ks[12], (DEPTH, D_FF), 0.02),
        "w_down": nrm(ks[13], (DEPTH, D_FF, D_MODEL), D_FF ** -0.5),
        "final_norm_w": 1.0 + nrm(ks[14], (D_MODEL,), 0.02),
    }

def first_block(x, norm_mix_w, w_in, b_attn, lb_logits, hg_norm_w, sinks, w_out,
              norm_ffn_w, w_gate, w_up, conv_w, conv_b, w_down, final_norm_w):
    B, S, _ = x.shape
    lb_all = jnp.cumsum(jax.nn.softmax(lb_logits.astype(jnp.float32), axis=0), axis=0)[:DEPTH]
    h = x
    for l in range(DEPTH):
        u = rmsnorm(h, norm_mix_w[l])
        proj = u @ w_in[l]
        hq, hf, hi, hg, att = jnp.split(
            proj, [HG_KEY_WIDTH, 2 * HG_KEY_WIDTH, 2 * HG_KEY_WIDTH + HG_VAL_WIDTH, HG_COLS], axis=-1)
        lb = lb_all[l]
        f = lb + (1.0 - lb) * jax.nn.sigmoid(hf.astype(jnp.float32))
        log_f = jnp.log(f).reshape(B, S, HG_HEADS, HG_DK)
        k_hg = (1.0 - f).reshape(B, S, HG_HEADS, HG_DK)
        q_hg = hq.astype(jnp.float32).reshape(B, S, HG_HEADS, HG_DK) * (HG_DK ** -0.5)
        v_hg = hi.reshape(B, S, HG_HEADS, HG_DV)
        o_hg = hgrn2_chunkwise(q_hg, k_hg, v_hg, log_f)
        o_hg = rmsnorm(o_hg, hg_norm_w[l]).reshape(B, S, HG_VAL_WIDTH)
        o_hg = (o_hg * jax.nn.silu(hg.astype(jnp.float32))).astype(h.dtype)
        att = att + b_attn[l]
        aq, ak, av = jnp.split(att, [ATT_Q_WIDTH, ATT_Q_WIDTH + ATT_KV_WIDTH], axis=-1)
        o_att = sliding_window_attention_with_sinks(
            aq.reshape(B, S, ATT_HEADS, ATT_HD),
            ak.reshape(B, S, ATT_KV_HEADS, ATT_HD),
            av.reshape(B, S, ATT_KV_HEADS, ATT_HD),
            sinks[l]).astype(h.dtype)
        mix = jnp.concatenate([o_hg, o_att], axis=-1)
        h = h + mix @ w_out[l]
        v = rmsnorm(h, norm_ffn_w[l])
        gate = causal_depthwise_conv(v @ w_gate[l], conv_w[l], conv_b[l])
        h = h + (jax.nn.silu(gate) * (v @ w_up[l])) @ w_down[l]
    return rmsnorm(h, final_norm_w)


POOL_WINDOWS = (2, 4, 8, 16)
N_POOL_GROUPS = len(POOL_WINDOWS)
POOL_GROUP_DIM = D_MODEL // 8
POOL_W = N_POOL_GROUPS * POOL_GROUP_DIM
FOX_HEADS = 8
FOX_HEAD_DIM = 64
FOX_W = FOX_HEADS * FOX_HEAD_DIM
Q_BLOCK = 128
OFF_POOL = 0
OFF_Q = OFF_POOL + POOL_W
OFF_K = OFF_Q + FOX_W
OFF_V = OFF_K + FOX_W
OFF_F = OFF_V + FOX_W
OFF_GP = OFF_F + FOX_HEADS
OFF_GF = OFF_GP + D_MODEL
IN_W = OFF_GF + D_MODEL
N_MEM = 256
X_HEADS = 4
X_HEAD_DIM = 128
X_W = X_HEADS * X_HEAD_DIM
CONV_WIDTH = 3
RMS_EPS = 1e-6


def rms_norm(x, g):
    xf = x.astype(jnp.float32)
    y = xf * lax.rsqrt(jnp.mean(xf * xf, axis=-1, keepdims=True) + RMS_EPS)
    return (y * g.astype(jnp.float32)).astype(x.dtype)

def shift_right(z, n):
    return jnp.pad(z, ((0, 0), (n, 0), (0, 0)))[:, : z.shape[1]]

def pool_mixer(u, pool_w, pool_scale):
    B, S, _ = u.shape
    uf = u.astype(jnp.float32)
    cs = jnp.cumsum(uf, axis=1)
    t = jnp.arange(S)
    outs = []
    for g, w in enumerate(POOL_WINDOWS):
        sl = slice(g * POOL_GROUP_DIM, (g + 1) * POOL_GROUP_DIM)
        csg = cs[..., sl]
        cnt = jnp.minimum(t + 1, w).astype(jnp.float32)[None, :, None]
        outs.append((csg - shift_right(csg, w)) / cnt - uf[..., sl])
    pooled = jnp.stack(outs, axis=2).astype(u.dtype)
    mixed = jnp.einsum("bsgc,gcd->bsgd", pooled, pool_w).reshape(B, S, POOL_W)
    return mixed * pool_scale

def fox_attention(q, k, v, log_f):
    B, S, H, Dh = q.shape
    nb = S // Q_BLOCK
    scale = 1.0 / math.sqrt(Dh)
    cT = jnp.cumsum(log_f.astype(jnp.float32), axis=1).transpose(0, 2, 1)
    qb = q.reshape(B, nb, Q_BLOCK, H, Dh).transpose(1, 0, 2, 3, 4)
    cb = cT.reshape(B, H, nb, Q_BLOCK).transpose(2, 0, 1, 3)
    kpos = jnp.arange(S)

    def one_block(args):
        qi, ci, bi = args
        s = jnp.einsum("bqhd,bkhd->bhqk", qi, k, preferred_element_type=jnp.float32) * scale
        s = s + ci[..., :, None] - cT[:, :, None, :]
        qpos = bi * Q_BLOCK + jnp.arange(Q_BLOCK)
        s = jnp.where(kpos[None, :] <= qpos[:, None], s, -jnp.inf)
        p = jax.nn.softmax(s, axis=-1)
        return jnp.einsum("bhqk,bkhd->bqhd", p.astype(v.dtype), v)

    out = lax.map(one_block, (qb, cb, jnp.arange(nb)))
    return out.transpose(1, 0, 2, 3, 4).reshape(B, S, H * Dh)

def mem_attention(h, mem_n, w_xq, w_xkv, w_xo):
    B, S, _ = h.shape
    M = mem_n.shape[1]
    q = (h @ w_xq).reshape(B, S, X_HEADS, X_HEAD_DIM)
    kv = mem_n @ w_xkv
    k = kv[..., :X_W].reshape(B, M, X_HEADS, X_HEAD_DIM)
    v = kv[..., X_W:].reshape(B, M, X_HEADS, X_HEAD_DIM)
    s = jnp.einsum("bqhd,bmhd->bhqm", q, k, preferred_element_type=jnp.float32) / math.sqrt(X_HEAD_DIM)
    p = jax.nn.softmax(s, axis=-1)
    o = jnp.einsum("bhqm,bmhd->bqhd", p.astype(v.dtype), v).reshape(B, S, X_W)
    return o @ w_xo

def conv_ffn(h, w_up, conv_w, conv_b, w_down):
    z = h @ w_up
    zc = conv_w[2] * z + conv_w[1] * shift_right(z, 1) + conv_w[0] * shift_right(z, 2) + conv_b
    g, u = zc[..., :D_FF], zc[..., D_FF:]
    return (jax.nn.gelu(g, approximate=True) * u) @ w_down

def second_inputs(seed: int = 0) -> dict:
    key = jax.random.key(seed)
    ks = jax.random.split(key, 32)
    L, D = DEPTH, D_MODEL
    f32 = jnp.float32

    def nrm(k, shape, fan_in):
        return jax.random.normal(k, shape, f32) * (fan_in ** -0.5)

    def gain(k):
        return 1.0 + 0.05 * jax.random.normal(k, (L, D), f32)

    b_forget = (jnp.linspace(1.0, 5.0, FOX_HEADS, dtype=f32)[None, :]
                + 0.1 * jax.random.normal(ks[5], (L, FOX_HEADS), f32))
    return {
        "x": jax.random.normal(ks[0], (BATCH, SEQ, D), f32),
        "mem": jax.random.normal(ks[1], (BATCH, N_MEM, D), f32),
        "mix_pre_g": gain(ks[2]),
        "mix_post_g": gain(ks[3]),
        "w_in": nrm(ks[4], (L, D, IN_W), D),
        "b_forget": b_forget,
        "pool_w": nrm(ks[6], (L, N_POOL_GROUPS, POOL_GROUP_DIM, POOL_GROUP_DIM), POOL_GROUP_DIM),
        "pool_scale": 1.0 + 0.1 * jax.random.normal(ks[7], (L, POOL_W), f32),
        "w_pool_br": nrm(ks[8], (L, POOL_W, D), POOL_W),
        "w_fox_br": nrm(ks[9], (L, FOX_W, D), FOX_W),
        "w_mix_out": nrm(ks[10], (L, D, D), D),
        "xa_pre_g": gain(ks[11]),
        "xa_post_g": gain(ks[12]),
        "mem_g": gain(ks[13]),
        "w_xq": nrm(ks[14], (L, D, X_W), D),
        "w_xkv": nrm(ks[15], (L, D, 2 * X_W), D),
        "w_xo": nrm(ks[16], (L, X_W, D), X_W),
        "ffn_pre_g": gain(ks[17]),
        "ffn_post_g": gain(ks[18]),
        "w_up": nrm(ks[19], (L, D, 2 * D_FF), D),
        "conv_w": nrm(ks[20], (L, CONV_WIDTH, 2 * D_FF), CONV_WIDTH),
        "conv_b": 0.01 * jax.random.normal(ks[21], (L, 2 * D_FF), f32),
        "w_down": nrm(ks[22], (L, D_FF, D), D_FF),
    }

def second_block(x, mem, mix_pre_g, mix_post_g, w_in, b_forget, pool_w, pool_scale,
              w_pool_br, w_fox_br, w_mix_out, xa_pre_g, xa_post_g, mem_g, w_xq, w_xkv,
              w_xo, ffn_pre_g, ffn_post_g, w_up, conv_w, conv_b, w_down):
    B, S, _ = x.shape
    for l in range(DEPTH):
        h = rms_norm(x, mix_pre_g[l])
        z = h @ w_in[l]
        u_pool = z[..., OFF_POOL:OFF_Q]
        q = z[..., OFF_Q:OFF_K].reshape(B, S, FOX_HEADS, FOX_HEAD_DIM)
        k = z[..., OFF_K:OFF_V].reshape(B, S, FOX_HEADS, FOX_HEAD_DIM)
        v = z[..., OFF_V:OFF_F].reshape(B, S, FOX_HEADS, FOX_HEAD_DIM)
        log_f = jax.nn.log_sigmoid((z[..., OFF_F:OFF_GP] + b_forget[l]).astype(jnp.float32))
        gate_pool = jax.nn.sigmoid(z[..., OFF_GP:OFF_GF])
        gate_fox = jax.nn.sigmoid(z[..., OFF_GF:])
        y_pool = pool_mixer(u_pool, pool_w[l], pool_scale[l]) @ w_pool_br[l]
        y_fox = fox_attention(q, k, v, log_f) @ w_fox_br[l]
        merged = gate_pool * y_pool + gate_fox * y_fox
        x = x + rms_norm(merged @ w_mix_out[l], mix_post_g[l])
        h = rms_norm(x, xa_pre_g[l])
        mem_n = rms_norm(mem, mem_g[l])
        x = x + rms_norm(mem_attention(h, mem_n, w_xq[l], w_xkv[l], w_xo[l]), xa_post_g[l])
        h = rms_norm(x, ffn_pre_g[l])
        x = x + rms_norm(conv_ffn(h, w_up[l], conv_w[l], conv_b[l], w_down[l]), ffn_post_g[l])
    return x


def setup_inputs(seed=0):
    out = dict(first_inputs(seed))
    for name, value in second_inputs(seed + 1).items():
        if name != "x":
            out[name + "_2"] = value
    return out


def reference(
    x, norm_mix_w, w_in, b_attn, lb_logits, hg_norm_w, sinks, w_out, norm_ffn_w, w_gate, w_up,
    conv_w, conv_b, w_down, final_norm_w, mem_2, mix_pre_g_2, mix_post_g_2, w_in_2, b_forget_2,
    pool_w_2, pool_scale_2, w_pool_br_2, w_fox_br_2, w_mix_out_2, xa_pre_g_2, xa_post_g_2,
    mem_g_2, w_xq_2, w_xkv_2, w_xo_2, ffn_pre_g_2, ffn_post_g_2, w_up_2, conv_w_2, conv_b_2,
    w_down_2,
):
    x = first_block(
        x, norm_mix_w, w_in, b_attn, lb_logits, hg_norm_w, sinks, w_out, norm_ffn_w, w_gate,
        w_up, conv_w, conv_b, w_down, final_norm_w,
    )
    return second_block(
        x, mem_2, mix_pre_g_2, mix_post_g_2, w_in_2, b_forget_2, pool_w_2, pool_scale_2,
        w_pool_br_2, w_fox_br_2, w_mix_out_2, xa_pre_g_2, xa_post_g_2, mem_g_2, w_xq_2, w_xkv_2,
        w_xo_2, ffn_pre_g_2, ffn_post_g_2, w_up_2, conv_w_2, conv_b_2, w_down_2,
    )


_drawn_inputs = setup_inputs


def setup_inputs(seed=0):
    import zlib

    import numpy as np

    out = dict(_drawn_inputs(seed))
    spreads = {}
    factors = {'b_attn': 3.208,
     'hg_norm_w': 4.715,
     'sinks': 8.0,
     'norm_ffn_w': 3.562,
     'conv_b': 4.933,
     'conv_b_2': 8.0}
    for name, (base, spread) in spreads.items():
        noise = np.random.default_rng([zlib.crc32(name.encode()), seed]).standard_normal(out[name].shape)
        drawn = base * np.exp(spread * noise) if base else spread * noise
        out[name] = __import__('jax').numpy.asarray(drawn.astype(out[name].dtype))
    for name, factor in factors.items():
        out[name] = (out[name] * factor).astype(out[name].dtype)
    return out
```

```python
from contextlib import ExitStack

import concourse.bass as bass
from concourse import mybir

F32 = mybir.dt.float32
F32R = mybir.dt.float32r
BF16 = mybir.dt.bfloat16
I32 = mybir.dt.int32
U8 = mybir.dt.uint8
ALU = mybir.AluOpType
ACT = mybir.ActivationFunctionType
AX = mybir.AxisListType

P = 128
T = 1024
D = 1024
KT = D // P
HALF = 512
CH = 256
DFF = 2816
FG = DFF // CH
NBLK = T // P
MEM = 256
EPS = 1e-6
NEG = -1e30
HG = 4
LEVELS = 7
HG_SCALE = 128 ** -0.5

PARAM_ROWS = [
    [("norm_mix_w", 8), ("norm_ffn_w", 8), ("final_norm_w", 8), ("mix_pre_g_2", 8), ("mix_post_g_2", 8),
     ("xa_pre_g_2", 8), ("xa_post_g_2", 8), ("mem_g_2", 8), ("ffn_pre_g_2", 8), ("ffn_post_g_2", 8),
     ("pool_scale_2", 4), ("lb_logits", 8), ("hg_norm_w", 1), ("b_attn", 5)],
    [("conv_w", 66), ("conv_b", 22)],
    [("conv_w_2a", 88)],
    [("conv_w_2b", 44), ("conv_b_2", 44)],
]
PCOL = {}
for _t, _rows in enumerate(PARAM_ROWS):
    _at = 0
    for _name, _n in _rows:
        PCOL[_name] = (_t, _at, _n)
        _at += _n
N_CONSTS = 27
N_PARAM_DMAS = sum(len(r) for r in PARAM_ROWS)


def weight_segments(a):
    def tiles(w):
        return w.rearrange("o (k p) n -> p (o k) n", p=P)

    w_in, w_out, w_gate, w_up = (tiles(a[n]) for n in ("w_in", "w_out", "w_gate", "w_up"))
    w_down, w_in2, w_up2, w_down2 = (tiles(a[n]) for n in ("w_down", "w_in_2", "w_up_2", "w_down_2"))
    w_pool, w_fox, w_mix = (tiles(a[n]) for n in ("w_pool_br_2", "w_fox_br_2", "w_mix_out_2"))
    w_xq, w_xkv, w_xo = (tiles(a[n]) for n in ("w_xq_2", "w_xkv_2", "w_xo_2"))

    def cols(w, base, step, n=CH):
        return lambda i: w[:, :, bass.ds(i * step + base, n)]

    def rows(w, step):
        return lambda i: w[:, bass.ds(i * step, step), :]

    return {
        "mem_k": (1, [(0, cols(w_xkv, 0, 0)), (1, cols(w_xkv, 256, 0))]),
        "mem_v": (1, [(0, cols(w_xkv, 512, 0)), (1, cols(w_xkv, 768, 0))]),
        "in1_gates": (2, [(0, cols(w_in, 512, CH)), (1, cols(w_in, 1536, CH))]),
        "in1_q": (2, [(0, cols(w_in, 0, CH)), (1, cols(w_in, 2048, CH))]),
        "in1_v": (1, [(0, cols(w_in, 1024, 0)), (1, cols(w_in, 1280, 0)), (2, cols(w_in, 2560, 0))]),
        "out1": (2, [(0, cols(w_out, 0, 512)), (1, cols(w_out, 256, 512))]),
        "ffn1": (FG, [(0, cols(w_gate, 0, CH)), (1, cols(w_up, 0, CH)), (2, rows(w_down, 2))]),
        "in2_f": (1, [(2, cols(w_in2, 2048, 0, P))]),
        "in2_pqk": (3, [(0, cols(w_in2, 0, 512)), (1, cols(w_in2, 256, 512))]),
        "in2_gates": (4, [(0, cols(w_in2, 2056, 512)), (1, cols(w_in2, 2312, 512))]),
        "in2_v": (1, [(0, cols(w_in2, 1536, 0)), (1, cols(w_in2, 1792, 0))]),
        "branches": (2, [(0, cols(w_pool, 0, 512, 512)), (1, cols(w_fox, 0, 512, 512))]),
        "mix": (2, [(0, cols(w_mix, 0, 512)), (1, cols(w_mix, 256, 512))]),
        "xq": (1, [(0, cols(w_xq, 0, 0)), (1, cols(w_xq, 256, 0))]),
        "xo": (1, [(0, cols(w_xo, 0, 0, 512)), (1, cols(w_xo, 512, 0, 512))]),
        "ffn2": (FG, [(0, cols(w_up2, 0, CH)), (1, cols(w_up2, DFF, CH)), (2, rows(w_down2, 2))]),
    }


def segment_bases(segments):
    used, out = [0, 0, 0], {}
    for name, (iters, chunks) in segments.items():
        out[name] = list(used)
        for slot, _ in chunks:
            used[slot] += iters
    return out


def program(nc, a, out):
    segments = weight_segments(a)
    bases = segment_bases(segments)

    def use(name, pos, i):
        slot = segments[name][1][pos][0]
        assert [s for s, _ in segments[name][1]].count(slot) == 1
        return bases[name][slot] + i

    def iterate(e, n, body):
        if n == 1:
            body(0)
        else:
            with e.Fori(0, n) as i:
                body(i)

    with ExitStack() as ctx:
        def sb(name, shape, dt=F32):
            return ctx.enter_context(nc.sbuf_tensor(name, shape, dt))

        def sem(name):
            return ctx.enter_context(nc.semaphore(name))

        def dram(name, shape):
            return nc.dram_tensor(name, shape, F32, kind="Internal").ap()

        XT = sb("XT", [P, KT, T])
        UH = sb("UH", [P, KT, T], F32R)
        UL = sb("UL", [P, KT, T], F32R)
        raw = [sb(f"raw{s}", [P, 2048]) for s in range(2)]
        wh = [sb(f"wh{s}", [P, 2048], F32R) for s in range(3)]
        wl = [sb(f"wl{s}", [P, 2048], F32R) for s in range(3)]
        SC = sb("SC", [P, 6144])
        aH = sb("aH", [P, 2, T], F32R)
        aL = sb("aL", [P, 2, T], F32R)
        prm = sb("prm", [P, 4, P])
        ident = sb("ident", [P, P])
        ones = sb("ones", [P, P])
        bmask = sb("bmask", [P, 3, P], BF16)
        identb = sb("identb", [P, P], BF16)
        lvl = sb("lvl", [P, LEVELS, P], U8)
        small = sb("small", [P, 104])
        eps = small[:, 0:1]
        nsink = small[:, 8:16]
        lb = small[:, 16:20]
        omlb = small[:, 20:24]
        psink = small[:, 76:84]
        binv = small[:, 72:73]
        invt = small[:, 84:100]
        sm = small[:, 24:64]
        XTf = XT[:].rearrange("p k t -> p (k t)")
        PS = ctx.enter_context(nc.psum_tensor("PS", [P, 8, HALF], F32))

        def pair(n):
            return PS[:, 2 * n:2 * n + 2, :].rearrange("p b n -> p (b n)")

        def sc(at, n):
            return SC[:, at:at + n]

        def pc(name, j=0):
            t, at, _ = PCOL[name]
            return prm[:, t, at + j:at + j + 1]

        xres = dram("xres", (D, T))
        zq1 = dram("zq1", (HG * P, T))
        zf1 = dram("zf1", (HG * P, T))
        zg1 = dram("zg1", (HG * P, T))
        aq1 = dram("aq1", (512, T))
        ak1 = dram("ak1", (128, T))
        v1 = dram("v1", (T, 640 + 128))
        zpqk = dram("zpqk", (1536, T))
        zgate = dram("zgate", (2048, T))
        fc = dram("fc", (8, T))
        fnc = dram("fnc", (8, T))
        onesd = dram("onesd", (1, T))
        v2 = dram("v2", (T, 512))
        mk = dram("mk", (512, MEM))
        mv = dram("mv", (MEM, 512))
        xq = dram("xq", (512, T))

        raw_loaded = [sem(f"raw_loaded{s}") for s in range(3)]
        hi_done = [sem(f"hi_done{s}") for s in range(3)]
        w_ready = [sem(f"w_ready{s}") for s in range(3)]
        w_free = [sem(f"w_free{s}") for s in range(3)]
        pe_stage, act_stage, dve_stage = sem("pe_stage"), sem("act_stage"), sem("dve_stage")
        consts_ready = sem("consts_ready")
        passed = {e.engine: sem(f"passed_{n}") for n, e in (("act", nc.scalar), ("dve", nc.vector), ("pool", nc.gpsimd), ("sp", nc.sync))}

        shared = {}

        class Count:
            def __init__(self, semaphore, base):
                self.sem, self.base = semaphore, base

            def __call__(self, value):
                return self.sem, self.base + value

        stages = []

        class Stage:
            def __init__(self, name):
                self.name = name
                self.index = len(stages) + 1
                stages.append(self)
                self.setup()

            def count(self, what, total):
                name = f"{type(self).__name__.lower()}_{what}"
                if name not in shared:
                    shared[name] = [sem(name), 0]
                semaphore, base = shared[name]
                shared[name][1] += total
                return Count(semaphore, base)

            def setup(self): pass
            def tensor(self, pe): pass
            def scalar(self, act): pass
            def vector(self, dve): pass

            def after(self, e):
                if self.index > 1:
                    e.wait_ge(pe_stage, self.index - 1)
                    e.wait_ge(act_stage, self.index - 1)
                    e.wait_ge(dve_stage, self.index - 1)


        def apart(e):
            e.sem_inc(passed[e.engine], 1)

        def feature_tiles(pe, seg, pos, i, full, free, n, kt=KT, ntok=T, nf=2, u0=0, u_ready=None,
                          banks=0, ):
            slot = segments[seg][1][pos][0]
            width = nf * P
            pe.wait_ge(w_ready[slot], use(seg, pos, i) + 2)
            H = wh[slot][:, 0:kt * width].rearrange("p (k n) -> p k n", k=kt)
            L = wl[slot][:, 0:kt * width].rearrange("p (k n) -> p k n", k=kt)
            step = min(ntok, HALF)
            for f in range(nf):
                pe.wait_ge(*free(n + f + 1))
                ps = pair((banks + f) % 2)
                cols = slice(f * P, f * P + P)
                for k in range(kt):
                    if u_ready is not None and f == 0:
                        pe.wait_ge(u_ready, k + 1)
                    for j, (w, u) in enumerate(((H, UH), (H, UL), (L, UH))):
                        for h in range(ntok // step):
                            mm = pe.matmul(ps[:, h * step:(h + 1) * step], w[:, k, cols],
                                           u[:, u0 + k, h * step:(h + 1) * step],
                                           start=(k == 0 and j == 0), stop=(k == kt - 1 and j == 2))
                mm.then_inc(full.sem, 1)
            pe.drain().then_inc(w_free[slot], 1)

        def token_tiles(pe, seg, pos, full, free, n, ntt, bias_row=None, width=CH, c0=0):
            slot = segments[seg][1][pos][0]
            pe.wait_ge(w_ready[slot], use(seg, pos, 0) + 2)
            H = wh[slot][:].rearrange("p (k n) -> p k n", k=KT)
            L = wl[slot][:].rearrange("p (k n) -> p k n", k=KT)
            for t in range(ntt):
                pe.wait_ge(*free(n + t + 1))
                ps = PS[:, 4 + (n + t) % 4, 0:width]
                for k in range(KT):
                    for j, (w, u) in enumerate(((H, UH), (L, UH), (H, UL))):
                        mm = pe.matmul(ps, u[:, k, t * P:(t + 1) * P], w[:, k, c0:c0 + width],
                                  start=(k == 0 and j == 0),
                                  stop=(k == KT - 1 and j == 2 and bias_row is None))
                if bias_row is not None:
                    mm = pe.matmul(ps, ones[0:1, :], bias_row, start=False, stop=True)
                mm.then_inc(full.sem, 1)

        def free_slot(pe, seg, pos):
            pe.drain().then_inc(w_free[segments[seg][1][pos][0]], 1)


        class Setup(Stage):
            def setup(self):
                self.prm_loaded, self.p_full, self.v = self.count("prm_loaded", 0), self.count("p_full", 1), self.count("v", 0)

            def scalar(self, act):
                prow = XTf[:, 0:512].rearrange("p (t n) -> p t n", t=4)
                act.wait_ge(consts_ready, 1)
                for t, names in enumerate(PARAM_ROWS):
                    for name, n in names:
                        _, at, _ = PCOL[name]
                        if name == "conv_w_2a":
                            src = a["conv_w_2"].rearrange("o c (m p) -> (o c m) p", p=P)[0:88]
                        elif name == "conv_w_2b":
                            src = a["conv_w_2"].rearrange("o c (m p) -> (o c m) p", p=P)[88:132]
                        elif name == "conv_w":
                            src = a[name].rearrange("o c (m p) -> (o c m) p", p=P)
                        elif len(a[name].shape) == 1:
                            src = a[name].rearrange("(m p) -> m p", p=P)
                        else:
                            src = a[name].rearrange("o (m p) -> (o m) p", p=P)[0:n]
                        act.dma_start(prow[at:at + n, t, :], src).then_inc(self.prm_loaded.sem, 16)
                act.dma_start(small[0:1, 64:72], a["sinks"]).then_inc(self.prm_loaded.sem, 16)
                act.dma_start(small[0:8, 72:73], a["b_forget_2"].rearrange("o n -> n o")).then_inc(self.prm_loaded.sem, 16)

            def tensor(self, pe):
                for s in range(3):
                    pe.sem_inc(w_free[s], 1)
                pe.wait_ge(consts_ready, N_CONSTS)
                pe.wait_ge(*self.prm_loaded(16 * (N_PARAM_DMAS + 2)))
                for t in range(4):
                    pe.transpose(PS[:, 6, t * P:(t + 1) * P], XTf[:, t * P:(t + 1) * P], ident[:])
                pe.matmul(PS[:, 7, 0:8], ones[0:1, :], small[0:1, 64:72], start=True, stop=True).then_inc(self.p_full.sem, 1)

            def vector(self, dve):
                n = [0]

                def done(ins):
                    n[0] += 1
                    ins.then_inc(self.v.sem, 1)
                    dve.wait_ge(*self.v(n[0]))

                dve.wait_ge(consts_ready, N_CONSTS)
                si, ti = SC[:, 0:P].bitcast(I32), SC[:, P:2 * P].bitcast(I32)
                xi, xf, tri, lm = SC[:, 2 * P:3 * P].bitcast(I32), sc(3 * P, P), sc(4 * P, P), sc(5 * P, P)
                done(dve.tensor_tensor(xi, si, ti, ALU.bitwise_xor))
                done(dve.tensor_copy(xf, xi))
                done(dve.tensor_tensor(tri, ti, si, ALU.is_gt))
                done(dve.tensor_tensor(xf, xf, tri, ALU.mult))
                for l in range(LEVELS):
                    m = float(1 << l)
                    done(dve.tensor_scalar(tri, xf, m, None, ALU.is_ge))
                    done(dve.scalar_tensor_tensor(out=lm, in0=xf, scalar=2 * m, in1=tri, op0=ALU.is_lt, op1=ALU.mult))
                    done(dve.tensor_copy(lvl[:, l, :], lm))
                dve.wait_ge(*self.p_full(1))
                done(dve.tensor_copy(prm[:].rearrange("p t n -> p (t n)"), PS[:, 6, :]))
                done(dve.tensor_scalar(nsink, PS[:, 7, 0:8], -1.0, None, ALU.mult))
                done(dve.tensor_scalar(psink, PS[:, 7, 0:8], 1.0, None, ALU.mult))
                _, at, _ = PCOL["lb_logits"]
                l0, l1 = prm[:, 0, at:at + 4], prm[:, 0, at + 4:at + 8]
                done(dve.tensor_tensor(sm[:, 0:4], l0, l1, ALU.max))
                done(dve.tensor_tensor(sm[:, 4:8], l0, sm[:, 0:4], ALU.subtract))
                done(dve.tensor_tensor(sm[:, 8:12], l1, sm[:, 0:4], ALU.subtract))

        class TurnIn(Stage):
            def __init__(self, name, src, dst, n, store):
                self.src, self.dst, self.n, self.store = src, dst, n, store
                super().__init__(name)

            def setup(self):
                parts = max(1, self.n // HALF)
                self.loaded, self.full, self.free = self.count("loaded", 16 * parts), self.count("full", parts * KT), self.count("free", parts * KT)
                self.stored = self.count("stored", 16 * self.store)

            def scalar(self, act):
                parts = max(1, self.n // HALF)
                nb = min(4, self.n // P)
                rows = self.src.rearrange("(h b p) n -> h p b n", p=P, b=nb)
                act.dma_start(sc(0, nb * D).rearrange("p (b n) -> p b n", b=nb), rows[0]).then_inc(self.loaded.sem, 16)
                for h in range(parts):
                    for k in range(KT):
                        n = h * KT + k
                        act.wait_ge(*self.full(n + 1))
                        act.activation(self.dst[:, k, h * HALF:h * HALF + nb * P], PS[:, n % 2, 0:nb * P],
                                       ACT.Copy).then_inc(self.free.sem, 1)
                    if h + 1 < parts:
                        act.dma_start(sc(0, nb * D).rearrange("p (b n) -> p b n", b=nb), rows[h + 1]).then_inc(self.loaded.sem, 16)
                if self.store:
                    act.wait_ge(*self.free(parts * KT))
                    act.dma_start(xres.rearrange("(k p) t -> p k t", p=P), XT[:]).then_inc(self.stored.sem, 16)
                    act.wait_ge(*self.stored(16))

            def tensor(self, pe):
                parts, nb = max(1, self.n // HALF), min(4, self.n // P)
                for h in range(parts):
                    pe.wait_ge(*self.loaded(16 * (h + 1)))
                    for k in range(KT):
                        n = h * KT + k
                        if n >= 2:
                            pe.wait_ge(*self.free(n - 1))
                        for b in range(nb):
                            tr = pe.transpose(PS[:, n % 2, b * P:(b + 1) * P], sc(b * D + k * P, P), ident[:])
                        tr.then_inc(self.full.sem, 1)

        class SetupBound(Stage):
            def setup(self):
                self.e, self.v = self.count("e", 1), self.count("v", 4)

            def scalar(self, act):
                act.activation(sm[:, 12:20], sm[:, 4:12], ACT.Exp).then_inc(self.e.sem, 1)

            def vector(self, dve):
                dve.wait_ge(*self.e(1))
                dve.tensor_tensor(sm[:, 20:24], sm[:, 12:16], sm[:, 16:20], ALU.add).then_inc(self.v.sem, 1)
                dve.wait_ge(*self.v(1))
                dve.reciprocal(sm[:, 24:28], sm[:, 20:24]).then_inc(self.v.sem, 1)
                dve.wait_ge(*self.v(2))
                dve.tensor_tensor(lb, sm[:, 12:16], sm[:, 24:28], ALU.mult).then_inc(self.v.sem, 1)
                dve.tensor_tensor(omlb, sm[:, 16:20], sm[:, 24:28], ALU.mult).then_inc(self.v.sem, 1)


        class Norm(Stage):
            def __init__(self, name, weight, mode, src=None, n=T, store=False):
                self.weight, self.mode, self.n, self.store = weight, mode, n, store
                self.src = XT if src is None else src
                super().__init__(name)

            def setup(self):
                split = self.mode == "split"
                self.sq_ready, self.sq_used = self.count("sq_ready", KT), self.count("sq_used", KT)
                self.ln, self.rstd_ready = self.count("ln", 1), self.count("rstd", 1)
                self.u_ready = self.count("u", 0 if self.mode == "inplace" else KT)
                self.hi_ready, self.lo_ready = self.count("hi", KT * split), self.count("lo", KT * split)
                self.res = self.count("res", 16 * (self.mode == "post"))
                self.xn, self.stored = self.count("xn", KT * (not split)), self.count("stored", 16 * self.store)
                n = self.n
                self.sq = [sc(0, n), sc(T, n)]
                self.lnv, self.rstd = sc(2 * T, n), sc(3 * T, n)
                self.u = [sc(4 * T, n), sc(5 * T, n)]

            def scalar(self, act):
                if self.mode == "post":
                    act.dma_start(UH[:].bitcast(F32), xres.rearrange("(k p) t -> p k t", p=P)).then_inc(self.res.sem, 16)
                for k in range(KT):
                    if k >= 2:
                        act.wait_ge(*self.sq_used(k - 1))
                    act.activation(self.sq[k % 2], self.src[:, k, :], ACT.Square).then_inc(self.sq_ready.sem, 1)
                act.wait_ge(*self.sq_used(KT))
                act.activation(self.lnv, PS[:, 0:2, :].rearrange("p b n -> p (b n)")[:, 0:self.n], ACT.Ln,
                               bias=eps, scale=1.0 / D).then_inc(self.ln.sem, 1)
                act.wait_ge(*self.ln(1))
                act.activation(self.rstd, self.lnv, ACT.Exp, scale=-0.5).then_inc(self.rstd_ready.sem, 1)
                if self.mode == "split":
                    for k in range(KT):
                        act.wait_ge(*self.u_ready(k + 1))
                        act.activation(UH[:, k, 0:self.n], self.u[k % 2], ACT.Copy).then_inc(self.hi_ready.sem, 1)
                if self.store:
                    act.wait_ge(*self.xn(KT))
                    act.dma_start(xres.rearrange("(k p) t -> p k t", p=P), XT[:]).then_inc(self.stored.sem, 16)
                    act.wait_ge(*self.stored(16))

            def tensor(self, pe):
                step = min(self.n, HALF)
                for k in range(KT):
                    pe.wait_ge(*self.sq_ready(k + 1))
                    for h in range(self.n // step):
                        mm = pe.matmul(PS[:, h, 0:step], ones[:], self.sq[k % 2][:, h * step:(h + 1) * step],
                                       start=k == 0, stop=k == KT - 1)
                    mm.then_inc(self.sq_used.sem, 1)

            def vector(self, dve):
                dve.wait_ge(*self.rstd_ready(1))
                if self.mode == "post":
                    dve.wait_ge(*self.res(16))

                def lo(k):
                    dve.wait_ge(*self.hi_ready(k + 1))
                    dve.tensor_tensor(UL[:, k, 0:self.n], self.u[k % 2], UH[:, k, 0:self.n].bitcast(F32),
                                      ALU.subtract).then_inc(self.lo_ready.sem, 1)

                def add(k):
                    dve.wait_ge(*self.u_ready(k + 1))
                    dve.tensor_tensor(XT[:, k, :], self.u[k % 2], UH[:, k, :].bitcast(F32), ALU.add).then_inc(self.xn.sem, 1)

                for k in range(KT):
                    if self.mode == "inplace":
                        dve.scalar_tensor_tensor(out=XT[:, k, :], in0=XT[:, k, :], scalar=pc(self.weight, k), in1=self.rstd,
                                                 op0=ALU.mult, op1=ALU.mult).then_inc(self.xn.sem, 1)
                        continue
                    if k >= 2:
                        dve.wait_ge(*(self.lo_ready if self.mode == "split" else self.xn)(k - 1))
                    dve.scalar_tensor_tensor(out=self.u[k % 2], in0=self.src[:, k, :], scalar=pc(self.weight, k),
                                             in1=self.rstd, op0=ALU.mult, op1=ALU.mult).then_inc(self.u_ready.sem, 1)
                    if k >= 1:
                        (lo if self.mode == "split" else add)(k - 1)
                if self.mode != "inplace":
                    (lo if self.mode == "split" else add)(KT - 1)


        class Project(Stage):
            def __init__(self, name, loops, ntok=T, u0=0, kt=KT):
                self.loops, self.ntok, self.u0, self.kt = loops, ntok, u0, kt
                super().__init__(name)

            def setup(self):
                n = sum(segments[seg][0] * sum(c[2] for c in chunks) for seg, chunks in self.loops)
                self.full, self.free, self.z_done = self.count("full", n), self.count("free", n + 2), self.count("z_done", n)
                self.z_stored = [self.count(f"z_stored{s}", 16 * ((n + 1 - s) // 2) + 16) for s in range(2)]
                self.z = [sc(0, self.ntok), sc(T, self.ntok)]

            def tensor(self, pe):
                n = 0
                for seg, chunks in self.loops:
                    iters = segments[seg][0]

                    def body(i):
                        for pos in range(len(chunks)):
                            nf = chunks[pos][2]
                            feature_tiles(pe, seg, pos, i, self.full, self.free, n + (i * per + pos * 2), nf=nf,
                                          ntok=self.ntok, u0=self.u0, kt=self.kt)
                    per = sum(c[2] for c in chunks)
                    iterate(pe, iters, body)
                    n += iters * per

            def scalar(self, act):
                act.sem_inc(self.free.sem, 2)
                for s in range(2):
                    act.sem_inc(self.z_stored[s].sem, 16)
                n = 0
                for seg, chunks in self.loops:
                    iters = segments[seg][0]
                    per = sum(c[2] for c in chunks)
                    assert per % 2 == 0 or iters == 1

                    def body(i):
                        for pos, (finish, where, nf) in enumerate(chunks):
                            for f in range(nf):
                                t = pos * 2 + f
                                s = (n + t) % 2
                                act.wait_ge(*self.full(n + (i * per + t) + 1))
                                uses = (n + t) // 2 + i * (per // 2)
                                act.wait_ge(*self.z_stored[s](16 * uses + 16))
                                apart(act)
                                finish(act, self.z[s], pair(f % 2)[:, 0:self.ntok], i, f, self.free)
                                act.drain().then_inc(self.z_done.sem, 1)
                                act.wait_ge(*self.z_done(n + (i * per + t) + 1))
                                act.dma_start(where(i, f), self.z[s]).then_inc(self.z_stored[s].sem, 16)
                    iterate(act, iters, body)
                    n += iters * per
                for s in range(2):
                    act.wait_ge(*self.z_stored[s](16 * ((n + 1 - s) // 2) + 16))

        def finish_with(func, bias=None, scale=1.0):
            def finish(act, o, ps, i, f, free):
                kw = {"bias": bias(i, f)} if bias else {}
                act.activation(o, ps, func, scale=scale, **kw).then_inc(free.sem, 1)
            return finish

        def rows_at(z, base, step):
            return lambda i, f: z[bass.ds(i * step + (base + f * P), P), :]

        class ProjectTokens(Stage):
            def __init__(self, name, dest, jobs, ntt=NBLK, key=None):
                self.dest, self.jobs, self.ntt, self.key = dest, jobs, ntt, key
                super().__init__(name)

            def setup(self):
                n, key = len(self.jobs) * self.ntt, 1 if self.key else 0
                self.full, self.free = self.count("full", n), self.count("free", n + 4)
                self.stored = self.count("stored", 16 * (len(self.jobs) + key))
                self.kfull, self.kdone, self.brow = self.count("kfull", key), self.count("kdone", key), self.count("brow", 16 * key)

            def tensor(self, pe):
                n = 0
                for seg, pos, c0, width, where, bias in self.jobs:
                    if bias:
                        pe.wait_ge(*self.brow(16))
                    token_tiles(pe, seg, pos, self.full, self.free, n, self.ntt, width=width, c0=c0,
                                bias_row=SC[0:1, 0:P] if bias else None)
                    if self.key and self.key[0:2] == (seg, pos):
                        slot = segments[seg][1][pos][0]
                        H = wh[slot][:].rearrange("p (k n) -> p k n", k=KT)
                        L = wl[slot][:].rearrange("p (k n) -> p k n", k=KT)
                        for k in range(KT):
                            for j, (w, u) in enumerate(((H, UH), (H, UL), (L, UH))):
                                for h in range(2):
                                    pe.matmul(PS[:, h, :], w[:, k, 0:P], u[:, k, h * HALF:(h + 1) * HALF],
                                              start=(k == 0 and j == 0), stop=(k == KT - 1 and j == 2))
                        pe.drain().then_inc(self.kfull.sem, 1)
                    free_slot(pe, seg, pos)
                    n += self.ntt

            def scalar(self, act):
                if any(j[5] for j in self.jobs):
                    act.dma_start(SC[0:1, 0:P], a["b_attn"][0:1, 640:768]).then_inc(self.brow.sem, 16)
                act.sem_inc(self.free.sem, 4)
                n = 0
                for q, (seg, pos, c0, width, where, bias) in enumerate(self.jobs):
                    st = XTf[:, (q % 2) * 2048:(q % 2) * 2048 + self.ntt * width].rearrange("p (t n) -> p t n", n=width)
                    if q >= 2:
                        act.wait_ge(*self.stored(16 * q))
                    for t in range(self.ntt):
                        act.wait_ge(*self.full(n + 1))
                        act.activation(st[:, t, :], PS[:, 4 + n % 4, 0:width], ACT.Copy).then_inc(self.free.sem, 1)
                        n += 1
                    act.wait_ge(*self.free(n + 4))
                    act.dma_start(self.dest[:, where:where + width].rearrange("(t p) n -> p t n", p=P), st).then_inc(self.stored.sem, 16)
                if self.key:
                    act.wait_ge(*self.kfull(1))
                    act.activation(sc(T, T), pair(0), ACT.Identity, bias=self.key[3]).then_inc(self.kdone.sem, 1)
                    act.wait_ge(*self.kdone(1))
                    act.dma_start(self.key[2], sc(T, T)).then_inc(self.stored.sem, 16)
                act.wait_ge(*self.stored(16 * (len(self.jobs) + (1 if self.key else 0))))


        class OutProduct(Stage):
            def __init__(self, name, seg, nf, kt, residual):
                self.seg, self.nf, self.kt, self.residual = seg, nf, kt, residual
                super().__init__(name)

            def setup(self):
                self.full, self.free, self.res = self.count("full", KT), self.count("free", KT + 2), self.count("res", 16 * self.residual)

            def tensor(self, pe):
                iters = segments[self.seg][0]
                iterate(pe, iters, lambda i: [
                    feature_tiles(pe, self.seg, pos, i, self.full, self.free, i * (2 * self.nf) + pos * self.nf, nf=self.nf, kt=self.kt)
                    for pos in range(2)])

            def scalar(self, act):
                if self.residual:
                    act.dma_start(XT[:], xres.rearrange("(k p) t -> p k t", p=P)).then_inc(self.res.sem, 16)

            def vector(self, dve):
                dve.sem_inc(self.free.sem, 2)
                if self.residual:
                    dve.wait_ge(*self.res(16))

                def body(i):
                    for t in range(2 * self.nf):
                        dve.wait_ge(*self.full(i * (2 * self.nf) + t + 1))
                        x = XTf[:, bass.ds(i * (2 * self.nf * T) + t * T, T)]
                        if self.residual:
                            dve.tensor_tensor(x, pair(t % 2), x, ALU.add).then_inc(self.free.sem, 1)
                        else:
                            dve.tensor_copy(x, pair(t % 2)).then_inc(self.free.sem, 1)
                iterate(dve, segments[self.seg][0], body)


        class FFN(Stage):
            def __init__(self, name, seg, second):
                self.seg, self.second = seg, second
                super().__init__(name)

            def setup(self):
                s, n = self.count, 2 * FG
                self.g_full, self.u_full, self.y_full = s("g_full", n), s("u_full", n), s("y_full", FG * KT)
                self.ps_free, self.y_free = s("ps_free", 2 * n + 2), s("y_free", FG * KT + 2)
                self.tap, self.c1, self.c2, self.gate, self.prod = s("tap", n), s("c1", n), s("c2", n), s("gate", n), s("prod", n + 1)
                self.hi, self.a_ready = s("hi", n), s("a_ready", n + 1)
                self.utap, self.u1, self.u2 = (s(x, n * self.second) for x in ("utap", "u1", "u2"))
                self.g_free, self.cleared = s("g_free", n + 2), s("cleared", 1 * self.second)
                self.AH = aH[:]
                self.AL = aL[:]
                self.g = [sc(0, T), sc(T, T)]
                self.t = sc(2 * T, T)
                self.p = sc(3 * T, T)

            def half_group(self, pe, g, pos, full):
                slot = segments[self.seg][1][pos][0]
                pe.wait_ge(w_ready[slot], use(self.seg, pos, g) + 2)
                H = wh[slot][:].rearrange("p (k n) -> p k n", k=KT)
                L = wl[slot][:].rearrange("p (k n) -> p k n", k=KT)
                for f in range(2):
                    pe.wait_ge(*self.ps_free(g * 4 + (pos * 2 + f + 1)))
                    for k in range(KT):
                        for j, (w, u) in enumerate(((H, UH), (H, UL), (L, UH))):
                            for h in range(2):
                                mm = pe.matmul(PS[:, 2 * f + h, :], w[:, k, f * P:(f + 1) * P], u[:, k, h * HALF:(h + 1) * HALF],
                                               start=(k == 0 and j == 0), stop=(k == KT - 1 and j == 2))
                    mm.then_inc(full.sem, 1)
                pe.drain().then_inc(w_free[slot], 1)

            def down(self, pe, g):
                pe.wait_ge(w_ready[2], use(self.seg, 2, g) + 2)
                pe.wait_ge(*self.a_ready(g * 2 + 3))
                H = wh[2][:].rearrange("p (k n) -> p k n", k=2)
                L = wl[2][:].rearrange("p (k n) -> p k n", k=2)
                for m in range(KT):
                    pe.wait_ge(*self.y_free(g * KT + (m + 1)))
                    for k in range(2):
                        for j, (w, u) in enumerate(((H, self.AH), (H, self.AL), (L, self.AH))):
                            for h in range(2):
                                mm = pe.matmul(PS[:, 4 + 2 * (m % 2) + h, :], w[:, k, m * P:(m + 1) * P],
                                               u[:, k, h * HALF:(h + 1) * HALF],
                                               start=(k == 0 and j == 0), stop=(k == 1 and j == 2))
                    mm.then_inc(self.y_full.sem, 1)
                pe.drain().then_inc(w_free[2], 1)

            def tensor(self, pe):
                self.half_group(pe, 0, 0, self.g_full)
                self.half_group(pe, 0, 1, self.u_full)
                with pe.Fori(0, FG - 1) as g:
                    self.half_group(pe, g + 1, 0, self.g_full)
                    self.down(pe, g)
                    self.half_group(pe, g + 1, 1, self.u_full)
                self.down(pe, FG - 1)

            def taps(self, g, f, col0):
                def col(name, base):
                    t, at, _ = PCOL[name]
                    return prm[:, t, bass.ds(g * 2 + (at + base + f + col0), 1)]
                if self.second:
                    return col("conv_w_2a", 0), col("conv_w_2a", 44), col("conv_w_2b", 0), col("conv_b_2", 0)
                return col("conv_w", 0), col("conv_w", 22), col("conv_w", 44), col("conv_b", 0)

            def scalar(self, act):
                def gates(g):
                    for f in range(2):
                        n = g * 2 + f
                        _, _, w2, b = self.taps(g, f, 0)
                        act.wait_ge(*self.g_full(n + 1))
                        act.wait_ge(*self.g_free(n + 1))
                        apart(act)
                        act.activation(self.g[f], pair(f), ACT.Identity, bias=b, scale=w2).then_inc(self.tap.sem, 1)
                        act.wait_ge(*self.c2(n + 1))
                        act.activation(self.g[f], self.g[f], ACT.Gelu_apprx_tanh if self.second else ACT.Silu).then_inc(self.gate.sem, 1)

                def ups(g):
                    for f in range(2):
                        n = g * 2 + f
                        if self.second:
                            _, _, w2, b = self.taps(g, f, 22)
                            act.wait_ge(*self.u_full(n + 1))
                            act.wait_ge(*self.prod(n + 1))
                            apart(act)
                            act.activation(self.t, pair(f), ACT.Identity, bias=b, scale=w2).then_inc(self.utap.sem, 1)
                        act.wait_ge(*self.prod(n + 2))
                        act.activation(self.AH[:, f, :], self.p, ACT.Copy).then_inc(self.hi.sem, 1)

                with act.Fori(0, FG) as g:
                    gates(g)
                    ups(g)

            def vector(self, dve):
                dve.sem_inc(self.ps_free.sem, 2)
                dve.sem_inc(self.y_free.sem, 2)
                dve.sem_inc(self.g_free.sem, 2)
                dve.sem_inc(self.prod.sem, 1)
                dve.sem_inc(self.a_ready.sem, 1)
                if self.second:
                    dve.memset(XTf, 0.0).then_inc(self.cleared.sem, 1)
                    dve.wait_ge(*self.cleared(1))

                def older(o, ps, w0, w1, ready, n, s1, s2, free):
                    dve.wait_ge(*ready(n + 1))
                    dve.scalar_tensor_tensor(out=o[:, 1:T], in0=ps[:, 0:T - 1], scalar=w1, in1=o[:, 1:T],
                                             op0=ALU.mult, op1=ALU.add).then_inc(s1.sem, 1)
                    dve.wait_ge(*s1(n + 1))
                    dve.scalar_tensor_tensor(out=o[:, 2:T], in0=ps[:, 0:T - 2], scalar=w0, in1=o[:, 2:T],
                                             op0=ALU.mult, op1=ALU.add).then_inc(s2.sem, 1)
                    if free is not None:
                        dve.wait_ge(*s2(n + 1))
                        dve.sem_inc(free.sem, 1)

                def gates(g):
                    for f in range(2):
                        w0, w1, _, _ = self.taps(g, f, 0)
                        older(self.g[f], pair(f), w0, w1, self.tap, g * 2 + f, self.c1, self.c2, self.ps_free)

                def ups(g):
                    for f in range(2):
                        n = g * 2 + f
                        if self.second:
                            w0, w1, _, _ = self.taps(g, f, 22)
                            older(self.t, pair(f), w0, w1, self.utap, n, self.u1, self.u2, self.ps_free)
                            up = self.t
                        else:
                            dve.wait_ge(*self.u_full(n + 1))
                            up = pair(f)
                        dve.wait_ge(*self.gate(n + 1))
                        dve.wait_ge(*self.a_ready(n + 1))
                        dve.tensor_tensor(self.p, up, self.g[f], ALU.mult).then_inc(self.prod.sem, 1)
                        dve.wait_ge(*self.prod(n + 2))
                        if not self.second:
                            dve.sem_inc(self.ps_free.sem, 1)
                        dve.sem_inc(self.g_free.sem, 1)
                        dve.wait_ge(*self.hi(n + 1))
                        dve.tensor_tensor(self.AL[:, f, :], self.p, self.AH[:, f, :].bitcast(F32), ALU.subtract).then_inc(self.a_ready.sem, 1)

                def add(g):
                    for m in range(KT):
                        dve.wait_ge(*self.y_full(g * KT + (m + 1)))
                        dve.tensor_tensor(XT[:, m, :], pair(2 + m % 2), XT[:, m, :], ALU.add).then_inc(self.y_free.sem, 1)

                gates(0)
                ups(0)
                with dve.Fori(0, FG - 1) as g:
                    gates(g + 1)
                    add(g)
                    ups(g + 1)
                add(FG - 1)

        class Split(Stage):
            def setup(self):
                self.hi = self.count("hi", KT)

            def scalar(self, act):
                for k in range(KT):
                    act.activation(UH[:, k, :], XT[:, k, :], ACT.Copy).then_inc(self.hi.sem, 1)

            def vector(self, dve):
                for k in range(KT):
                    dve.wait_ge(*self.hi(k + 1))
                    dve.tensor_tensor(UL[:, k, :], XT[:, k, :], UH[:, k, :].bitcast(F32), ALU.subtract)


        class Attend(Stage):
            def __init__(self, name, heads, rows, dv, scale, keys, loads, n_loads, sinks=False):
                self.heads, self.rows, self.dv, self.scale = heads, rows, dv, scale
                self.keys, self.loads, self.n_loads, self.sinks = keys, loads, n_loads, sinks
                super().__init__(name)

            def setup(self):
                s, n = self.count, self.heads * NBLK
                self.loaded = [s(f"loaded{j}", 16 * self.n_loads * self.heads // 2) for j in range(2)]
                self.s_full, self.exp_done = s("s_full", n), s("exp_done", n + 2)
                self.pt_full, self.pt_copied = s("pt_full", n + 2), s("pt_copied", n + 1)
                self.o_full, self.o_free = s("o_full", n + 16), s("o_free", n + 2)
                self.m_ready, self.mx, self.den, self.inv = s("m_ready", n), s("mx", n), s("den", n * self.sinks), s("inv", n)
                self.Q = [XTf[:, 0:T], sc(5120, T)]
                self.K = [XTf[:, 1024 + 1152 * j:1024 + 1152 * j + T] for j in range(2)]
                self.V = [sc(4096 + 512 * j, 512) for j in range(2)]
                self.O = XTf[:, 3328:3328 + 4096].rearrange("p (b n) -> p b n", b=NBLK)
                self.Pb = [sc(0, T), sc(T, T)]
                self.PT = [sc(2 * T, T), sc(3 * T, T)]

            def sync(self, sp):
                self.after(sp)
                with sp.Fori(0, self.heads // 2) as i:
                    for s in range(2):
                        sp.wait_ge(*self.o_full(i * 16 + 8 * (s + 1)))
                        apart(sp)
                        self.loads(sp, i * 2 + s, s, self)

            def tensor(self, pe):
                pe.sem_inc(self.pt_full.sem, 2)
                pe.sem_inc(self.o_full.sem, 16)

                def scores(i, t):
                    s, b = t // 8, t % 8
                    k0, nk, masks = self.keys(b)
                    if b == 0:
                        pe.wait_ge(*self.loaded[s](i * (16 * self.n_loads) + 16 * self.n_loads))
                    pe.wait_ge(*self.exp_done(i * 16 + (t + 1)))
                    ps = pair(t % 2)
                    last = nk * P
                    for c in range(0, last, HALF):
                        e = min(c + HALF, last)
                        inside = [m for m in masks if c <= m[0] * P < e]
                        for j, (kb, m) in enumerate(inside):
                            pe.matmul(ps[:, kb * P:(kb + 1) * P], identb[:], bmask[:, m, :], start=j == 0,
                                      stop=False, skip_group_check=True)
                        mm = pe.matmul(ps[:, c:e], self.Q[s][0:self.rows, b * P:(b + 1) * P],
                                       self.K[s][0:self.rows, k0 * P + c:k0 * P + e], start=not inside, stop=True,
                                       skip_group_check=True)
                    mm.then_inc(self.s_full.sem, 1)

                def turn(i, u):
                    nk = self.keys(u % 8)[1]
                    pe.wait_ge(*self.exp_done(i * 16 + (u + 3)))
                    pe.wait_ge(*self.pt_copied(i * 16 + (u + 1)))
                    for j in range(nk):
                        tr = pe.transpose(pair(2)[:, j * P:(j + 1) * P], self.Pb[u % 2][:, j * P:(j + 1) * P], ident[:])
                    tr.then_inc(self.pt_full.sem, 1)

                def values(i, u):
                    s, b = u // 8, u % 8
                    k0, nk, _ = self.keys(b)
                    V = self.V[s].rearrange("p (b n) -> p b n", n=self.dv)
                    pe.wait_ge(*self.pt_copied(i * 16 + (u + 2)))
                    pe.wait_ge(*self.o_free(i * 16 + (u + 1)))
                    for j in range(nk):
                        mm = pe.matmul(PS[:, 6 + u % 2, 0:self.dv], self.PT[u % 2][:, j * P:(j + 1) * P],
                                       V[:, k0 + j, :], start=j == 0, stop=j == nk - 1)
                    mm.then_inc(self.o_full.sem, 1)

                with pe.Fori(0, self.heads // 2) as i:
                    for t in range(18):
                        if t < 16:
                            scores(i, t)
                        if 1 <= t <= 16:
                            turn(i, t - 1)
                        if t >= 2:
                            values(i, t - 2)

            def scalar(self, act):
                act.sem_inc(self.exp_done.sem, 2)
                act.sem_inc(self.pt_copied.sem, 1)
                with act.Fori(0, self.heads // 2) as i:
                    for t in range(17):
                        if t < 16:
                            nk = self.keys(t % 8)[1]
                            act.wait_ge(*self.m_ready(i * 16 + (t + 1)))
                            act.wait_ge(*self.pt_full(i * 16 + (t + 1)))
                            apart(act)
                            if self.sinks:
                                act.activation(sm[:, 8 + t % 4:9 + t % 4], sm[:, 4 + t % 4:5 + t % 4], ACT.Exp,
                                               bias=psink[:, bass.ds(i * 2 + t // 8, 1)])
                            act.activation(self.Pb[t % 2][:, 0:nk * P], pair(t % 2)[:, 0:nk * P], ACT.Exp,
                                           bias=sm[:, 4 + t % 4:5 + t % 4], scale=self.scale,
                                           accum_out=sm[:, 12 + t % 4:13 + t % 4]).then_inc(self.exp_done.sem, 1)
                        if t >= 1:
                            u = t - 1
                            nk = self.keys(u % 8)[1]
                            act.wait_ge(*self.pt_full(i * 16 + (u + 3)))
                            act.wait_ge(*self.o_full(i * 16 + (u + 15)))
                            act.activation(self.PT[u % 2][:, 0:nk * P], pair(2)[:, 0:nk * P], ACT.Copy)\
                               .then_inc(self.pt_copied.sem, 1)

            def vector(self, dve):
                dve.sem_inc(self.o_free.sem, 2)

                def maximum(i, t):
                    nk = self.keys(t % 8)[1]
                    dve.wait_ge(*self.s_full(i * 16 + (t + 1)))
                    dve.reduce_max(sm[:, t % 4:t % 4 + 1], pair(t % 2)[:, 0:nk * P], AX.X).then_inc(self.mx.sem, 1)
                    dve.wait_ge(*self.mx(i * 16 + (t + 1)))
                    o, x = sm[:, 4 + t % 4:5 + t % 4], sm[:, t % 4:t % 4 + 1]
                    if self.sinks:
                        dve.tensor_scalar(o, x, -self.scale, nsink[:, bass.ds(i * 2 + t // 8, 1)], ALU.mult, ALU.min)\
                           .then_inc(self.m_ready.sem, 1)
                    else:
                        dve.tensor_scalar(o, x, -self.scale, None, ALU.mult).then_inc(self.m_ready.sem, 1)

                def output(i, u):
                    s, b = u // 8, u % 8
                    j = u % 4
                    den = sm[:, 12 + j:13 + j]
                    dve.wait_ge(*self.o_full(i * 16 + (u + 17)))
                    if self.sinks:
                        dve.tensor_tensor(sm[:, 16 + j:17 + j], den, sm[:, 8 + j:9 + j], ALU.add).then_inc(self.den.sem, 1)
                        dve.wait_ge(*self.den(i * 16 + (u + 1)))
                        den = sm[:, 16 + j:17 + j]
                    dve.reciprocal(sm[:, 20 + j:21 + j], den).then_inc(self.inv.sem, 1)
                    dve.wait_ge(*self.inv(i * 16 + (u + 1)))
                    dve.tensor_scalar(self.O[:, b, bass.ds(i * (2 * self.dv) + s * self.dv, self.dv)],
                                      PS[:, 6 + u % 2, 0:self.dv], sm[:, 20 + j:21 + j], None, ALU.mult)\
                       .then_inc(self.o_free.sem, 1)

                with dve.Fori(0, self.heads // 2) as i:
                    for t in range(18):
                        if t < 16:
                            maximum(i, t)
                        if t >= 2:
                            output(i, t - 2)

        class TurnHeads(Stage):
            def __init__(self, name, src, u0):
                self.src, self.u0 = src, u0
                super().__init__(name)

            def setup(self):
                self.full, self.hi, self.free = self.count("full", 4), self.count("hi", 4), self.count("free", 4)

            def tensor(self, pe):
                for k in range(4):
                    if k >= 2:
                        pe.wait_ge(*self.free(k - 1))
                    for b in range(NBLK):
                        tr = pe.transpose(pair(k % 2)[:, b * P:(b + 1) * P], self.src[:, b, k * P:(k + 1) * P], ident[:])
                    tr.then_inc(self.full.sem, 1)

            def scalar(self, act):
                for k in range(4):
                    act.wait_ge(*self.full(k + 1))
                    act.activation(UH[:, self.u0 + k, :], pair(k % 2), ACT.Copy).then_inc(self.hi.sem, 1)

            def vector(self, dve):
                for k in range(4):
                    dve.wait_ge(*self.hi(k + 1))
                    dve.tensor_tensor(UL[:, self.u0 + k, :], pair(k % 2), UH[:, self.u0 + k, :].bitcast(F32),
                                      ALU.subtract).then_inc(self.free.sem, 1)


        class HGRN(Stage):
            def setup(self):
                def s(what):
                    return self.count(what, 0)
                self.loaded, self.head_done = s("loaded"), s("head_done")
                self.fk, self.lnf, self.scan = s("fk"), s("lnf"), s("scan")
                self.dd, self.ex, self.mr, self.pl, self.pr = s("dd"), s("ex"), s("mr"), s("pl"), s("pr")
                self.e0, self.q0, self.de, self.ke, self.ee = s("e0"), s("q0"), s("de"), s("ke"), s("ee")
                self.tk, self.kc, self.kv, self.st, self.oo = s("tk"), s("kc"), s("kv"), s("st"), s("oo")
                self.sq, self.ss, self.l2, self.r2, self.n1, self.n2, self.hi = (s(x) for x in ("sq", "ss", "l2", "r2", "n1", "n2", "hi"))

                def x(n):
                    return XTf[:, n * T:(n + 1) * T]
                self.q, self.f, self.g, self.v, self.b, self.k = (x(n) for n in range(6))
                self.E = [x(6), sc(T, T)]
                self.M = [x(7), sc(2 * T, T)]
                self.ST = sc(0, T)
                self.KE, self.KET, self.Q0, self.S, self.o = sc(T, T), sc(2 * T, T), sc(3 * T, T), sc(4 * T, T), sc(5 * T, T)

            def sync(self, sp):
                self.after(sp)
                with sp.Fori(0, HG) as i:
                    sp.wait_ge(*self.head_done(i + 1))
                    apart(sp)
                    for dst, src in ((self.q, zq1), (self.f, zf1), (self.g, zg1)):
                        sp.dma_start(dst, src[bass.ds(i * P, P), :]).then_inc(self.loaded.sem, 16)
                    sp.dma_start(self.v.rearrange("p (c n) -> p c n", c=NBLK),
                                 v1.rearrange("(c p) n -> p c n", p=P)[:, :, bass.ds(i * P, P)]).then_inc(self.loaded.sem, 16)

            def tensor(self, pe):
                def c(t, n):
                    return t[:, n * P:(n + 1) * P]
                with pe.Fori(0, HG) as i:
                    pe.wait_ge(*self.fk(i * 2 + 2))
                    for n in range(NBLK):
                        mm = pe.matmul(c(pair(1), n), c(self.k, n), c(self.q, n), start=True, stop=True)
                    mm.then_inc(self.pl.sem, 1)
                    for l in range(LEVELS):
                        pe.wait_ge(*self.mr(i * LEVELS + (l + 1)))
                        if l >= 1:
                            pe.wait_ge(*self.pr(i * 8 + l))
                        for n in range(NBLK):
                            mm = pe.matmul(c(pair(l % 2), n), c(self.M[l % 2], n), c(self.M[l % 2], n), start=True, stop=True)
                        mm.then_inc(self.pl.sem, 1)
                    pe.wait_ge(*self.ke(i + 1))
                    for n in range(NBLK):
                        mm = pe.transpose(c(pair(2), n), c(self.KE, n), ident[:])
                    mm.then_inc(self.tk.sem, 1)
                    pe.wait_ge(*self.kc(i + 1))
                    for n in range(NBLK):
                        mm = pe.matmul(c(pair(3), n), c(self.KET, n), c(self.v, n), start=True, stop=True)
                    mm.then_inc(self.kv.sem, 1)
                    pe.wait_ge(*self.pr(i * 8 + 8))
                    pe.wait_ge(*self.st(i * 7 + 7))
                    pe.wait_ge(*self.q0(i + 1))
                    for n in range(NBLK):
                        mm = pe.matmul(c(pair(0), n), c(self.v, n), c(self.ST, n), start=True, stop=n == 0)
                        if n:
                            mm = pe.matmul(c(pair(0), n), c(self.S, n), c(self.Q0, n), start=False, stop=True)
                    mm.then_inc(self.oo.sem, 1)
                    pe.wait_ge(*self.sq(i + 1))
                    for h in range(2):
                        mm = pe.matmul(PS[:, 2 + h, :], ones[:], self.o[:, h * HALF:(h + 1) * HALF], start=True, stop=True)
                    mm.then_inc(self.ss.sem, 1)

            def scalar(self, act):
                with act.Fori(0, HG) as i:
                    act.wait_ge(*self.fk(i * 2 + 1))
                    act.activation(self.E[0], self.f, ACT.Ln).then_inc(self.lnf.sem, 1)
                    for l in range(LEVELS):
                        act.wait_ge(*self.dd(i * 14 + 2 * (l + 1)))
                        act.activation(self.E[l % 2], self.E[l % 2], ACT.Exp).then_inc(self.ex.sem, 1)
                    act.wait_ge(*self.mr(i * LEVELS + LEVELS))
                    act.activation(self.E[0], self.b, ACT.Exp).then_inc(self.e0.sem, 1)
                    act.wait_ge(*self.de(i + 1))
                    act.activation(self.KE, self.KE, ACT.Exp).then_inc(self.ee.sem, 1)
                    act.wait_ge(*self.tk(i + 1))
                    act.activation(self.KET, pair(2), ACT.Copy).then_inc(self.kc.sem, 1)
                    act.wait_ge(*self.oo(i + 1))
                    act.activation(self.o, pair(0), ACT.Square).then_inc(self.sq.sem, 1)
                    act.wait_ge(*self.ss(i + 1))
                    act.activation(self.E[1], pair(1), ACT.Ln, bias=eps, scale=1.0 / P).then_inc(self.l2.sem, 1)
                    act.wait_ge(*self.l2(i + 1))
                    act.activation(self.E[1], self.E[1], ACT.Exp, scale=-0.5).then_inc(self.r2.sem, 1)
                    act.wait_ge(*self.n2(i + 1))
                    apart(act)
                    act.activation(UH[:, bass.ds(i, 1), :], self.M[0], ACT.Copy).then_inc(self.hi.sem, 1)

            def vector(self, dve):
                dve.sem_inc(self.head_done.sem, 1)

                def halves(t, m):
                    v = t.rearrange("p (n h m) -> p n h m", h=2, m=m)
                    return v[:, :, 0, :], v[:, :, 1, :]

                with dve.Fori(0, HG) as i:
                    dve.wait_ge(*self.loaded(i * 64 + 64))
                    dve.tensor_scalar(self.f, self.f, omlb[:, bass.ds(i, 1)], lb[:, bass.ds(i, 1)], ALU.mult, ALU.add)\
                       .then_inc(self.fk.sem, 1)
                    dve.wait_ge(*self.fk(i * 2 + 1))
                    dve.tensor_scalar(self.k, self.f, -1.0, 1.0, ALU.mult, ALU.add).then_inc(self.fk.sem, 1)
                    dve.wait_ge(*self.lnf(i + 1))
                    for n in range(NBLK):
                        s = slice(n * P, (n + 1) * P)
                        dve.tensor_tensor_scan(self.b[:, s], ones[:], self.E[0][:, s], 0.0, ALU.mult, ALU.add).then_inc(self.scan.sem, 1)
                    dve.wait_ge(*self.scan(i * 8 + 8))

                    def exponents(l):
                        m = 64 >> l
                        b0, b1 = halves(self.b, m)
                        e0, e1 = halves(self.E[l % 2], m)
                        ref = b0[:, :, m - 1:m].to_broadcast([P, T // (2 * m), m])
                        if l >= 2:
                            dve.wait_ge(*self.mr(i * LEVELS + (l - 1)))
                        dve.tensor_tensor(e0, ref, b0, ALU.subtract).then_inc(self.dd.sem, 1)
                        dve.tensor_tensor(e1, b1, ref, ALU.subtract).then_inc(self.dd.sem, 1)

                    def decayed(l):
                        m = 64 >> l
                        e0, e1 = halves(self.E[l % 2], m)
                        m0, m1 = halves(self.M[l % 2], m)
                        k0, _ = halves(self.k, m)
                        _, q1 = halves(self.q, m)
                        dve.wait_ge(*self.ex(i * LEVELS + (l + 1)))
                        if l >= 2:
                            dve.wait_ge(*self.pl(i * 8 + l))
                        dve.tensor_tensor(m0, k0, e0, ALU.mult)
                        dve.tensor_tensor(m1, q1, e1, ALU.mult).then_inc(self.mr.sem, 1)

                    def placed(l):
                        dve.wait_ge(*self.pl(i * 8 + (l + 2)))
                        dve.wait_ge(*self.pr(i * 8 + (l + 1)))
                        mask = lvl[:, 6 - l:7 - l, :].to_broadcast([P, NBLK, P])
                        apart(dve)
                        dve.copy_predicated(self.ST.rearrange("p (n t) -> p n t", n=NBLK), mask,
                                            pair(l % 2).rearrange("p (n t) -> p n t", n=NBLK)).then_inc(self.pr.sem, 1)

                    exponents(0)
                    dve.wait_ge(*self.pl(i * 8 + 1))
                    dve.tensor_tensor(self.ST.rearrange("p (n t) -> p n t", n=NBLK),
                                      pair(1).rearrange("p (n t) -> p n t", n=NBLK),
                                      ident[:].rearrange("p (o t) -> p o t", o=1).to_broadcast([P, NBLK, P]), ALU.mult).then_inc(self.pr.sem, 1)
                    for l in range(LEVELS):
                        if l + 1 < LEVELS:
                            exponents(l + 1)
                        decayed(l)
                        if l >= 1:
                            placed(l - 1)
                    bc = self.b.rearrange("p (n t) -> p n t", n=NBLK)
                    dve.wait_ge(*self.pl(i * 8 + 7))
                    dve.tensor_tensor(self.KE.rearrange("p (n t) -> p n t", n=NBLK),
                                      bc[:, :, P - 1:P].to_broadcast([P, NBLK, P]), bc, ALU.subtract).then_inc(self.de.sem, 1)
                    placed(LEVELS - 1)
                    dve.wait_ge(*self.ee(i + 1))
                    dve.tensor_tensor(self.KE, self.k, self.KE, ALU.mult).then_inc(self.ke.sem, 1)
                    dve.wait_ge(*self.e0(i + 1))
                    dve.tensor_tensor(self.Q0, self.q, self.E[0], ALU.mult).then_inc(self.q0.sem, 1)
                    dve.wait_ge(*self.kv(i + 1))
                    for n in range(NBLK - 1):
                        s0, s1 = slice(n * P, (n + 1) * P), slice((n + 1) * P, (n + 2) * P)
                        if n == 0:
                            dve.tensor_copy(self.S[:, s1], pair(3)[:, s0]).then_inc(self.st.sem, 1)
                        else:
                            dve.wait_ge(*self.st(i * 7 + n))
                            dve.scalar_tensor_tensor(out=self.S[:, s1], in0=self.S[:, s0], scalar=self.E[0][:, (n + 1) * P - 1:(n + 1) * P],
                                                     in1=pair(3)[:, s0], op0=ALU.mult, op1=ALU.add).then_inc(self.st.sem, 1)
                    dve.wait_ge(*self.r2(i + 1))
                    dve.scalar_tensor_tensor(out=self.o, in0=pair(0), scalar=pc("hg_norm_w"), in1=self.E[1],
                                             op0=ALU.mult, op1=ALU.mult).then_inc(self.n1.sem, 1)
                    dve.wait_ge(*self.n1(i + 1))
                    dve.tensor_tensor(self.M[0], self.o, self.g, ALU.mult).then_inc(self.n2.sem, 1)
                    dve.wait_ge(*self.hi(i + 1))
                    dve.tensor_tensor(UL[:, bass.ds(i, 1), :], self.M[0], UH[:, bass.ds(i, 1), :].bitcast(F32), ALU.subtract)\
                       .then_inc(self.head_done.sem, 1)


        class Forget(Stage):
            def setup(self):
                def s(what):
                    return self.count(what, 0)
                self.full, self.free, self.x, self.a1, self.st = s("full"), s("free"), s("x"), s("a1"), s("st")

            def tensor(self, pe):
                feature_tiles(pe, "in2_f", 0, 0, self.full, self.free, 0, nf=1)

            def scalar(self, act):
                x, t = sc(0, T)[0:8, :], sc(T, T)[0:8, :]
                act.wait_ge(*self.x(1))
                for n, (func, src, kw) in enumerate(((ACT.Abs, x, {}), (ACT.Exp, t, {"scale": -1.0}),
                                                     (ACT.Ln, t, {"bias": ones[0:8, 0:1]}))):
                    act.activation(t, src, func, **kw).then_inc(self.a1.sem, 1)
                    act.wait_ge(*self.a1(n + 1))
                act.wait_ge(*self.x(5))
                act.dma_start(fc, sc(2 * T, T)[0:8, :]).then_inc(self.st.sem, 16)
                act.dma_start(fnc, sc(3 * T, T)[0:8, :]).then_inc(self.st.sem, 16)
                act.dma_start(onesd, sc(4 * T, T)[0:1, :]).then_inc(self.st.sem, 16)
                act.wait_ge(*self.st(48))

            def vector(self, dve):
                dve.sem_inc(self.free.sem, 1)
                x, t, c = sc(0, T)[0:8, :], sc(T, T)[0:8, :], sc(2 * T, T)[0:8, :]
                one = sc(4 * T, T)[0:8, :]
                dve.memset(one, 1.0).then_inc(self.free.sem, 1)
                dve.wait_ge(*self.full(1))
                dve.tensor_scalar(x, pair(0)[0:8, :], binv[0:8, :], None, ALU.add).then_inc(self.x.sem, 1)
                dve.wait_ge(*self.a1(3))
                dve.wait_ge(*self.x(1))
                dve.scalar_tensor_tensor(out=t, in0=x, scalar=0.0, in1=t, op0=ALU.min, op1=ALU.subtract).then_inc(self.x.sem, 1)
                dve.wait_ge(*self.x(2))
                dve.wait_ge(*self.free(2))
                dve.tensor_tensor_scan(c, one, t, 0.0, ALU.mult, ALU.add).then_inc(self.x.sem, 1)
                dve.wait_ge(*self.x(3))
                dve.tensor_scalar(sc(3 * T, T)[0:8, :], c, -8.0, None, ALU.mult).then_inc(self.x.sem, 1)
                dve.wait_ge(*self.x(4))
                dve.tensor_scalar(c, c, 8.0, None, ALU.mult).then_inc(self.x.sem, 1)

        class Pooling(Stage):
            def setup(self):
                def s(what):
                    return self.count(what, 0)
                self.loaded, self.v, self.pooled, self.full, self.hi, self.free = (s(x) for x in ("loaded", "v", "pooled", "full", "hi", "free"))

            def scalar(self, act):
                act.dma_start(XT[:, 0:4, :], zpqk[0:512, :].rearrange("(k p) t -> p k t", p=P)).then_inc(self.loaded.sem, 16)
                act.dma_start(XT[:, 6, 0:512].rearrange("p (g n) -> p g n", g=4), a["pool_w_2"].rearrange("o g p n -> p (o g) n")).then_inc(self.loaded.sem, 16)
                for g in range(4):
                    act.wait_ge(*self.full(g + 1))
                    act.activation(UH[:, g, :], pair(g % 2), ACT.Copy, scale=pc("pool_scale_2", g)).then_inc(self.hi.sem, 1)

            def tensor(self, pe):
                for g in range(4):
                    pe.wait_ge(*self.pooled(g + 1))
                    if g >= 2:
                        pe.wait_ge(*self.free(g - 1))
                    for h in range(2):
                        mm = pe.matmul(pair(g % 2)[:, h * HALF:(h + 1) * HALF], XT[:, 6, g * P:(g + 1) * P],
                                       sc((2 + g % 2) * T + h * HALF, HALF), start=True, stop=True)
                    mm.then_inc(self.full.sem, 1)

            def vector(self, dve):
                n = [0]

                def done(ins):
                    n[0] += 1
                    ins.then_inc(self.v.sem, 1)
                    dve.wait_ge(*self.v(n[0]))

                def split(g):
                    dve.wait_ge(*self.hi(g + 1))
                    dve.scalar_tensor_tensor(out=UL[:, g, :], in0=pair(g % 2), scalar=pc("pool_scale_2", g),
                                             in1=UH[:, g, :].bitcast(F32), op0=ALU.mult, op1=ALU.subtract).then_inc(self.free.sem, 1)

                dve.wait_ge(*self.loaded(32))
                for g in range(4):
                    w = 2 << g
                    u, cur = XT[:, g, :], XT[:, g, :]
                    for j in range(g + 1):
                        step, nxt = 1 << j, sc((j % 2) * T, T)
                        done(dve.tensor_copy(nxt[:, 0:step], cur[:, 0:step]))
                        done(dve.tensor_tensor(nxt[:, step:T], cur[:, step:T], cur[:, 0:T - step], ALU.add))
                        cur = nxt
                    o = sc((2 + g % 2) * T, T)
                    if g >= 2:
                        dve.wait_ge(*self.full(g - 1))
                    done(dve.scalar_tensor_tensor(out=o[:, w:T], in0=cur[:, w:T], scalar=1.0 / w, in1=u[:, w:T],
                                                  op0=ALU.mult, op1=ALU.subtract))
                    done(dve.tensor_tensor(o[:, 0:w], cur[:, 0:w], invt[:, 0:w], ALU.mult))
                    dve.tensor_tensor(o[:, 0:w], o[:, 0:w], u[:, 0:w], ALU.subtract).then_inc(self.pooled.sem, 1)
                    if g >= 1:
                        split(g - 1)
                split(3)

        class Branches(Stage):
            def setup(self):
                def s(what):
                    return self.count(what, 0)
                self.full, self.free, self.m, self.sum, self.loaded = s("full"), s("free"), s("m"), s("sum"), [s("loaded0"), s("loaded1")]

            def tensor(self, pe):
                with pe.Fori(0, 2) as i:
                    for pos in range(2):
                        pe.wait_ge(w_ready[pos], use("branches", pos, i) + 2)
                    for f in range(4):
                        for pos in range(2):
                            H = wh[pos][:].rearrange("p (k n) -> p k n", k=4)
                            L = wl[pos][:].rearrange("p (k n) -> p k n", k=4)
                            pe.wait_ge(*self.free(i * 8 + (f * 2 + pos + 1)))
                            for k in range(4):
                                for j, (w, u) in enumerate(((H, UH), (H, UL), (L, UH))):
                                    for h in range(2):
                                        mm = pe.matmul(PS[:, 2 * pos + h, :], w[:, k, f * P:(f + 1) * P],
                                                       u[:, 4 * pos + k, h * HALF:(h + 1) * HALF],
                                                       start=(k == 0 and j == 0), stop=(k == 3 and j == 2))
                            mm.then_inc(self.full.sem, 1)
                    for pos in range(2):
                        pe.drain().then_inc(w_free[pos], 1)

            def scalar(self, act):
                with act.Fori(0, 4) as i:
                    for s in range(2):
                        act.wait_ge(*self.sum(i * 2 + (s + 1)))
                        for j in range(2):
                            act.dma_start(sc((2 * s + j) * T, T), zgate[bass.ds(i * 256 + (s * P + j * D), P), :])\
                               .then_inc(self.loaded[s].sem, 16)

            def vector(self, dve):
                dve.sem_inc(self.free.sem, 2)
                dve.sem_inc(self.sum.sem, 2)
                with dve.Fori(0, 4) as i:
                    for s in range(2):
                        dve.wait_ge(*self.loaded[s](i * 32 + 32))
                        ga, gb = sc(2 * s * T, T), sc((2 * s + 1) * T, T)
                        for j, g in enumerate((ga, gb)):
                            dve.wait_ge(*self.full(i * 4 + (2 * s + j + 1)))
                            dve.tensor_tensor(g, pair(j), g, ALU.mult).then_inc(self.free.sem, 1)
                        dve.wait_ge(*self.free(i * 4 + (2 * s + 4)))
                        dve.tensor_tensor(XTf[:, bass.ds(i * (2 * T) + s * T, T)], ga, gb, ALU.add).then_inc(self.sum.sem, 1)

        class TurnOut(Stage):
            def setup(self):
                self.full, self.free = self.count("full", 0), self.count("free", 0)
                self.st = [self.count(f"st{j}", 0) for j in range(4)]

            def tensor(self, pe):
                for b in range(NBLK):
                    if b >= 2:
                        pe.wait_ge(*self.free(b - 1))
                    for k in range(KT):
                        tr = pe.transpose(pair(b % 2)[:, k * P:(k + 1) * P], XT[:, k, b * P:(b + 1) * P], ident[:])
                    tr.then_inc(self.full.sem, 1)

            def scalar(self, act):
                for b in range(NBLK):
                    act.wait_ge(*self.full(b + 1))
                    if b >= 4:
                        act.wait_ge(*self.st[b % 4](16))
                    act.activation(sc((b % 4) * T, T), pair(b % 2), ACT.Copy).then_inc(self.free.sem, 1)
                    act.wait_ge(*self.free(b + 1))
                    act.dma_start(out[b * P:(b + 1) * P, :], sc((b % 4) * T, T)).then_inc(self.st[b % 4].sem, 16)
                for j in range(4):
                    act.wait_ge(*self.st[j](32))

        pid, battn = ACT.Identity, PCOL["b_attn"][1]

        def attn_bias(i, f):
            return prm[:, 0, bass.ds(i * 2 + (battn + f), 1)]

        def copy(scale=1.0):
            return finish_with(ACT.Copy, scale=scale)

        def window_keys(b):
            return (0, 1, [(0, 1)]) if b == 0 else (b - 1, 2, [(0, 0), (1, 1)])

        def window_loads(sp, h, s, st):
            kv = h // 4
            sp.dma_start(st.Q[s][0:64, :], aq1[bass.ds(h * 64, 64), :]).then_inc(st.loaded[s].sem, 16)
            sp.dma_start(st.K[s][0:64, :], ak1[bass.ds(kv * 64, 64), :]).then_inc(st.loaded[s].sem, 16)
            sp.dma_start(st.V[s].rearrange("p (b n) -> p b n", n=64),
                         v1.rearrange("(b p) n -> p b n", p=P)[:, :, bass.ds(kv * 64 + 512, 64)]).then_inc(st.loaded[s].sem, 16)

        def fox_loads(sp, h, s, st):
            q, k, ld = st.Q[s], st.K[s], st.loaded[s]
            sp.dma_start(q[0:64, :], zpqk[bass.ds(h * 64 + 512, 64), :]).then_inc(ld.sem, 16)
            sp.dma_start(q[64:65, :], fc[bass.ds(h, 1), :]).then_inc(ld.sem, 16)
            sp.dma_start(q[65:66, :], onesd[:, :]).then_inc(ld.sem, 16)
            sp.dma_start(k[0:64, :], zpqk[bass.ds(h * 64 + 1024, 64), :]).then_inc(ld.sem, 16)
            sp.dma_start(k[64:65, :], onesd[:, :]).then_inc(ld.sem, 16)
            sp.dma_start(k[65:66, :], fnc[bass.ds(h, 1), :]).then_inc(ld.sem, 16)
            sp.dma_start(st.V[s].rearrange("p (b n) -> p b n", n=64),
                         v2.rearrange("(b p) n -> p b n", p=P)[:, :, bass.ds(h * 64, 64)]).then_inc(ld.sem, 16)

        def mem_loads(sp, h, s, st):
            sp.dma_start(st.Q[s], xq[bass.ds(h * P, P), :]).then_inc(st.loaded[s].sem, 16)
            sp.dma_start(st.K[s][:, 0:MEM], mk[bass.ds(h * P, P), :]).then_inc(st.loaded[s].sem, 16)
            sp.dma_start(st.V[s][:, 0:256].rearrange("p (b n) -> p b n", n=P),
                         mv.rearrange("(b p) n -> p b n", p=P)[:, :, bass.ds(h * P, P)]).then_inc(st.loaded[s].sem, 16)

        memT = XTf[:, 4096:6144].rearrange("p (k t) -> p k t", k=KT)
        Setup("setup")
        SetupBound("bound")
        TurnIn("turn_mem", a["mem_2"].rearrange("o t n -> (o t) n"), memT, MEM, False)
        Norm("norm_mem", "mem_g_2", "split", src=memT, n=MEM)
        Project("mem_k", [("mem_k", [(copy(), rows_at(mk, 0, 0), 2), (copy(), rows_at(mk, 256, 0), 2)])], ntok=MEM)
        ProjectTokens("mem_v", mv, [("mem_v", 0, 0, CH, 0, False), ("mem_v", 1, 0, CH, 256, False)], ntt=2)
        TurnIn("turn_x", a["x"].rearrange("o t n -> (o t) n"), XT, T, True)
        Norm("norm_mix", "norm_mix_w", "split")
        Project("in1", [("in1_gates", [(finish_with(ACT.Sigmoid), rows_at(zf1, 0, CH), 2), (finish_with(ACT.Silu), rows_at(zg1, 0, CH), 2)]),
                        ("in1_q", [(copy(HG_SCALE), rows_at(zq1, 0, CH), 2), (finish_with(pid, attn_bias), rows_at(aq1, 0, CH), 2)])])
        ProjectTokens("in1_v", v1, [("in1_v", 0, 0, CH, 0, False), ("in1_v", 1, 0, CH, 256, False), ("in1_v", 2, P, P, 512, True)],
                      key=("in1_v", 2, ak1, pc("b_attn", 4)))
        window = Attend("window", 8, 64, 64, 0.125, window_keys, window_loads, 3, sinks=True)
        TurnHeads("turn_window", window.O, 4)
        hgrn = HGRN("hgrn")
        OutProduct("out1", "out1", 2, KT, True)
        Norm("norm_ffn1", "norm_ffn_w", "split")
        FFN("ffn1", "ffn1", False)
        Norm("final", "final_norm_w", "inplace", store=True)
        Norm("norm_mix2", "mix_pre_g_2", "split")
        Forget("forget")
        Project("in2", [("in2_pqk", [(copy(), rows_at(zpqk, 0, 512), 2), (copy(), rows_at(zpqk, 256, 512), 2)]),
                        ("in2_gates", [(finish_with(ACT.Sigmoid), rows_at(zgate, 0, 512), 2), (finish_with(ACT.Sigmoid), rows_at(zgate, 256, 512), 2)])])
        ProjectTokens("in2_v", v2, [("in2_v", 0, 0, CH, 0, False), ("in2_v", 1, 0, CH, 256, False)])
        fox = Attend("fox", 8, 66, 64, 0.125, lambda b: (0, b + 1, [(b, 1)]), fox_loads, 7)
        TurnHeads("turn_fox", fox.O, 4)
        Pooling("pooling")
        Branches("branches")
        Split("split_merged")
        OutProduct("mix", "mix", 2, KT, False)
        Norm("post_mix", "mix_post_g_2", "post", store=True)
        Norm("norm_xa", "xa_pre_g_2", "split")
        Project("xq", [("xq", [(copy(), rows_at(xq, 0, 0), 2), (copy(), rows_at(xq, 256, 0), 2)])])
        memory = Attend("memory", 4, P, P, P ** -0.5, lambda b: (0, 2, []), mem_loads, 3)
        TurnHeads("turn_memory", memory.O, 0)
        OutProduct("xo", "xo", 4, 4, False)
        Norm("post_xa", "xa_post_g_2", "post", store=True)
        Norm("norm_ffn2", "ffn_pre_g_2", "split")
        FFN("ffn2", "ffn2", True)
        Norm("post_ffn", "ffn_post_g_2", "post")
        TurnOut("turn_out")

        groups = [["mem_k", "mem_v", "in1_gates", "in1_q", "in1_v"], window, hgrn,
                  ["out1", "ffn1", "in2_f", "in2_pqk", "in2_gates", "in2_v"], fox,
                  ["branches", "mix", "xq"], memory, ["xo", "ffn2"]]
        assert [g for group in groups if isinstance(group, list) for g in group] == list(segments)

        block = ctx.enter_context(nc.Block())

        @block.sync
        def _(sp):
            for group in groups:
                if isinstance(group, Stage):
                    group.sync(sp)
                    continue
                for seg in group:
                    iters, chunks = segments[seg]

                    def body(i):
                        seen = set()
                        for slot, src in chunks:
                            for other in ((0, 2) if slot != 1 else (1,)):
                                used = bases[seg][other] + ((1 if other in seen else 0) if other in [c[0] for c in chunks] else 0)
                                if other in [c[0] for c in chunks]:
                                    sp.wait_ge(w_ready[other], i + (used + 1))
                                    apart(sp)
                                else:
                                    sp.wait_ge(w_ready[other], used + 1)
                            ap = src(i)
                            k, n = ap.shape[1], ap.shape[2]
                            sp.dma_start(raw[slot % 2][:, 0:k * n].rearrange("p (k n) -> p k n", k=k), ap)\
                              .then_inc(raw_loaded[slot], 16)
                            seen.add(slot)
                    iterate(sp, iters, body)

        @block.gpsimd
        def _(pool):
            n = 0

            def const(ins):
                ins.then_inc(consts_ready, 1)

            prow = XTf[:, 0:512]
            const(pool.memset(prow, 0.0))
            for s in range(3):
                pool.sem_inc(w_ready[s], 1)
            const(pool.memset(ident[:], 0.0))
            const(pool.memset(ones[:], 1.0))
            const(pool.memset(bmask[:].rearrange("p a n -> p (a n)"), 0.0))
            const(pool.memset(eps, EPS))
            for t in range(16):
                const(pool.memset(invt[:, t:t + 1], 1.0 / (t + 1)))
            const(pool.iota(SC[:, 0:P].bitcast(I32), pattern=[[0, P]], base=0, channel_multiplier=1))
            const(pool.iota(SC[:, P:2 * P].bitcast(I32), pattern=[[1, P]], base=0, channel_multiplier=0))
            pool.wait_ge(consts_ready, 23)
            const(pool.affine_select(out=ident[:], in_=ident[:], compare_op=ALU.not_equal, fill=1.0, base=0,
                                     pattern=[[-1, P]], channel_multiplier=1))
            const(pool.affine_select(out=bmask[:, 0, :], in_=bmask[:, 0, :], compare_op=ALU.is_gt, fill=NEG, base=0,
                                     pattern=[[1, P]], channel_multiplier=-1))
            const(pool.affine_select(out=bmask[:, 1, :], in_=bmask[:, 1, :], compare_op=ALU.is_ge, fill=NEG, base=0,
                                     pattern=[[-1, P]], channel_multiplier=1))
            pool.wait_ge(consts_ready, 26)
            const(pool.tensor_copy(identb[:], ident[:]))
            for seg, (iters, chunks) in segments.items():
                def body(i):
                    for pos, (slot, src) in enumerate(chunks):
                        ap = src(i)
                        m = ap.shape[1] * ap.shape[2]
                        u = use(seg, pos, i)
                        pool.wait_ge(raw_loaded[slot], u * 16 + 16)
                        pool.wait_ge(w_free[slot], u + 1)
                        apart(pool)
                        pool.tensor_copy(wh[slot][:, 0:m], raw[slot % 2][:, 0:m]).then_inc(hi_done[slot], 1)
                        pool.wait_ge(hi_done[slot], u + 1)
                        pool.tensor_tensor(wl[slot][:, 0:m], raw[slot % 2][:, 0:m], wh[slot][:, 0:m].bitcast(F32),
                                           ALU.subtract).then_inc(w_ready[slot], 1)
                iterate(pool, iters, body)

        def run(e, method, own):
            for stage in stages:
                stage.after(e)
                part = {"tensor": stage.tensor, "scalar": stage.scalar, "vector": stage.vector}[method]
                part(e)
                e.drain().then_inc(own, 1)

        @block.tensor
        def _(pe):
            run(pe, "tensor", pe_stage)

        @block.scalar
        def _(act):
            run(act, "scalar", act_stage)

        @block.vector
        def _(dve):
            run(dve, "vector", dve_stage)


def kernel(**inputs):
    import numpy as np
    import concourse.bacc as bacc
    from concourse.bass_utils import run_bass_kernel_spmd

    nc = bacc.Bacc("TRN2", target_bir_lowering=False, num_devices=1)
    arrays, aps = {}, {}
    for name, value in inputs.items():
        v = np.ascontiguousarray(value)
        arrays["in_" + name] = v
        aps[name] = nc.dram_tensor("in_" + name, v.shape, mybir.dt.from_np(v.dtype), kind="ExternalInput").ap()
    out = nc.dram_tensor("out", (1, T, D), F32, kind="ExternalOutput").ap()
    program(nc, aps, out.rearrange("o t n -> (o t) n"))
    r = run_bass_kernel_spmd(nc, [arrays], core_ids=[0])
    return r.results[0]["out"]
```

```python
from contextlib import ExitStack

import concourse.bass as bass
from concourse import mybir

F32 = mybir.dt.float32
F32R = mybir.dt.float32r
BF16 = mybir.dt.bfloat16
I32 = mybir.dt.int32
U8 = mybir.dt.uint8
ALU = mybir.AluOpType
ACT = mybir.ActivationFunctionType
AX = mybir.AxisListType

P = 128
T = 1024
D = 1024
KT = D // P
HALF = 512
CH = 256
DFF = 2816
FG = DFF // CH
NBLK = T // P
MEM = 256
EPS = 1e-6
NEG = -1e30
HG = 4
LEVELS = 7
HG_SCALE = 128 ** -0.5

PARAM_ROWS = [
    [("norm_mix_w", 8), ("norm_ffn_w", 8), ("final_norm_w", 8), ("mix_pre_g_2", 8), ("mix_post_g_2", 8),
     ("xa_pre_g_2", 8), ("xa_post_g_2", 8), ("mem_g_2", 8), ("ffn_pre_g_2", 8), ("ffn_post_g_2", 8),
     ("pool_scale_2", 4), ("lb_logits", 8), ("hg_norm_w", 1), ("b_attn", 5)],
    [("conv_w", 66), ("conv_b", 22)],
    [("conv_w_2a", 88)],
    [("conv_w_2b", 44), ("conv_b_2", 44)],
]
PCOL = {}
for _t, _rows in enumerate(PARAM_ROWS):
    _at = 0
    for _name, _n in _rows:
        PCOL[_name] = (_t, _at, _n)
        _at += _n
N_CONSTS = 27
N_PARAM_DMAS = sum(len(r) for r in PARAM_ROWS)


def weight_segments(a):
    def tiles(w):
        return w.rearrange("o (k p) n -> p (o k) n", p=P)

    w_in, w_out, w_gate, w_up = (tiles(a[n]) for n in ("w_in", "w_out", "w_gate", "w_up"))
    w_down, w_in2, w_up2, w_down2 = (tiles(a[n]) for n in ("w_down", "w_in_2", "w_up_2", "w_down_2"))
    w_pool, w_fox, w_mix = (tiles(a[n]) for n in ("w_pool_br_2", "w_fox_br_2", "w_mix_out_2"))
    w_xq, w_xkv, w_xo = (tiles(a[n]) for n in ("w_xq_2", "w_xkv_2", "w_xo_2"))

    def cols(w, base, step, n=CH):
        return lambda i: w[:, :, bass.ds(i * step + base, n)]

    def rows(w, base):
        return lambda i: w[:, bass.ds(i * 2 + base, 2), :]

    return {
        "mem_k": (1, [(0, cols(w_xkv, 0, 0)), (1, cols(w_xkv, 256, 0))]),
        "mem_v": (1, [(0, cols(w_xkv, 512, 0)), (1, cols(w_xkv, 768, 0))]),
        "in1_gates": (2, [(0, cols(w_in, 512, CH)), (1, cols(w_in, 1536, CH))]),
        "in1_q": (2, [(0, cols(w_in, 0, CH)), (1, cols(w_in, 2048, CH))]),
        "in1_v": (1, [(0, cols(w_in, 1024, 0)), (1, cols(w_in, 1280, 0)), (2, cols(w_in, 2560, 0))]),
        "out1": (2, [(0, cols(w_out, 0, 512)), (1, cols(w_out, 256, 512))]),
        "ffn1_head": (1, [(0, cols(w_gate, 0, 0)), (1, cols(w_up, 0, 0))]),
        "ffn1": (FG - 1, [(0, cols(w_gate, CH, CH)), (2, rows(w_down, 0)), (1, cols(w_up, CH, CH))]),
        "ffn1_tail": (1, [(2, rows(w_down, 2 * (FG - 1)))]),
        "in2_pqk": (3, [(0, cols(w_in2, 0, 512)), (1, cols(w_in2, 256, 512))]),
        "in2_gates": (4, [(0, cols(w_in2, 2056, 512)), (1, cols(w_in2, 2312, 512))]),
        "in2_v": (1, [(0, cols(w_in2, 1536, 0)), (1, cols(w_in2, 1792, 0))]),
        "in2_f": (1, [(2, cols(w_in2, 2048, 0, P))]),
        "branches": (2, [(0, cols(w_pool, 0, 512, 512)), (1, cols(w_fox, 0, 512, 512))]),
        "mix": (2, [(0, cols(w_mix, 0, 512)), (1, cols(w_mix, 256, 512))]),
        "xq": (1, [(0, cols(w_xq, 0, 0)), (1, cols(w_xq, 256, 0))]),
        "xo": (1, [(0, cols(w_xo, 0, 0, 512)), (1, cols(w_xo, 512, 0, 512))]),
        "ffn2_head": (1, [(0, cols(w_up2, 0, 0)), (1, cols(w_up2, DFF, 0))]),
        "ffn2": (FG - 1, [(0, cols(w_up2, CH, CH)), (2, rows(w_down2, 0)), (1, cols(w_up2, DFF + CH, CH))]),
        "ffn2_tail": (1, [(2, rows(w_down2, 2 * (FG - 1)))]),
    }


def segment_bases(segments):
    used, out = [0, 0, 0], {}
    for name, (iters, chunks) in segments.items():
        out[name] = list(used)
        for slot, _ in chunks:
            used[slot] += iters
    return out


def program(nc, a, out):
    segments = weight_segments(a)
    bases = segment_bases(segments)

    def use(name, pos, i):
        slot = segments[name][1][pos][0]
        assert [s for s, _ in segments[name][1]].count(slot) == 1
        return bases[name][slot] + i

    def loop(e, n):
        return nc.Fori(0, n, engines=(e.engine,), hint_back_edge=True)

    def iterate(e, n, body):
        if n == 1:
            body(0)
        else:
            with loop(e, n) as i:
                body(i)

    with ExitStack() as ctx:
        def sb(name, shape, dt=F32):
            return ctx.enter_context(nc.sbuf_tensor(name, shape, dt))

        def sem(name):
            return ctx.enter_context(nc.semaphore(name))

        def dram(name, shape):
            return nc.dram_tensor(name, shape, F32, kind="Internal").ap()

        XT = sb("XT", [P, KT, T])
        UH = sb("UH", [P, KT, T], F32R)
        UL = sb("UL", [P, KT, T], F32R)
        raw = [sb(f"raw{s}", [P, 2048]) for s in range(2)]
        wh = [sb(f"wh{s}", [P, 2048], F32R) for s in range(3)]
        wl = [sb(f"wl{s}", [P, 2048], F32R) for s in range(3)]
        SC = sb("SC", [P, 6144])
        aH = sb("aH", [P, 2, T], F32R)
        aL = sb("aL", [P, 2, T], F32R)
        prm = sb("prm", [P, 4, P])
        ident = sb("ident", [P, P])
        ones = sb("ones", [P, P])
        bmask = sb("bmask", [P, 3, P], BF16)
        identb = sb("identb", [P, P], BF16)
        lvl = sb("lvl", [P, LEVELS, P], U8)
        small = sb("small", [P, 104])
        eps = small[:, 0:1]
        nsink = small[:, 8:16]
        lb = small[:, 16:20]
        omlb = small[:, 20:24]
        psink = small[:, 76:84]
        binv = small[:, 72:73]
        invt = small[:, 84:100]
        sm = small[:, 24:64]
        XTf = XT[:].rearrange("p k t -> p (k t)")
        PS = ctx.enter_context(nc.psum_tensor("PS", [P, 8, HALF], F32))

        def pair(n):
            return PS[:, 2 * n:2 * n + 2, :].rearrange("p b n -> p (b n)")

        def sc(at, n):
            return SC[:, at:at + n]

        def pc(name, j=0):
            t, at, _ = PCOL[name]
            return prm[:, t, at + j:at + j + 1]

        xres = dram("xres", (D, T))
        zq1 = dram("zq1", (HG * P, T))
        zf1 = dram("zf1", (HG * P, T))
        zg1 = dram("zg1", (HG * P, T))
        aq1 = dram("aq1", (512, T))
        ak1 = dram("ak1", (128, T))
        v1 = dram("v1", (T, 640 + 128))
        zpqk = dram("zpqk", (1536, T))
        zgate = dram("zgate", (2048, T))
        fc = dram("fc", (8, T))
        fnc = dram("fnc", (8, T))
        onesd = dram("onesd", (1, T))
        v2 = dram("v2", (T, 512))
        mk = dram("mk", (512, MEM))
        mv = dram("mv", (MEM, 512))
        xq = dram("xq", (512, T))

        raw_loaded = [sem(f"raw_loaded{s}") for s in range(3)]
        hi_done = [sem(f"hi_done{s}") for s in range(3)]
        w_ready = [sem(f"w_ready{s}") for s in range(3)]
        w_free = [sem(f"w_free{s}") for s in range(3)]
        pe_stage, act_stage, dve_stage = sem("pe_stage"), sem("act_stage"), sem("dve_stage")
        consts_ready = sem("consts_ready")
        passed = {e.engine: sem(f"passed_{n}") for n, e in (("act", nc.scalar), ("dve", nc.vector), ("pool", nc.gpsimd), ("sp", nc.sync))}

        shared = {}

        class Count:
            def __init__(self, semaphore, base):
                self.sem, self.base = semaphore, base

            def __call__(self, value):
                return self.sem, self.base + value

        stages = []

        class Stage:
            def __init__(self, name):
                self.name = name
                self.index = len(stages) + 1
                stages.append(self)
                self.setup()

            def count(self, what, total):
                name = f"{type(self).__name__.lower()}_{what}"
                if name not in shared:
                    shared[name] = [sem(name), 0]
                semaphore, base = shared[name]
                shared[name][1] += total
                return Count(semaphore, base)

            def setup(self): pass
            def ready(self, k): return None
            def tensor(self, pe): pass
            def scalar(self, act): pass
            def vector(self, dve): pass

            follows = False

            def after(self, e):
                if self.index > 1 and not self.follows:
                    e.wait_ge(pe_stage, self.index - 1)
                    e.wait_ge(act_stage, self.index - 1)
                    e.wait_ge(dve_stage, self.index - 1)


        def apart(e):
            e.sem_inc(passed[e.engine], 1)

        def warm_up(pe, n):
            for _ in range(n):
                pe.matmul(PS[:, 7, 0:3 * P], identb[:], bmask[:].rearrange("p a n -> p (a n)"), start=True, stop=True)

        def rotated(e, iters, per, parts):
            depth = max(lag for lag, _ in parts)

            def step(i, t, last=False):
                for lag, part in parts:
                    if 0 <= t - lag < per:
                        part(i, t - lag)
                    elif t - lag >= per and not last:
                        part(i + 1, t - lag - per)
            for t in range(depth):
                step(0, t)
            if iters > 2:
                with loop(e, iters - 1) as i:
                    for t in range(depth, per + depth):
                        step(i, t)
            else:
                for t in range(depth, per + depth):
                    step(0, t)
            for t in range(depth, per + depth):
                step(iters - 1, t, last=True)

        def feature_tiles(pe, seg, pos, i, full, free, n, kt=KT, ntok=T, nf=2, u0=0, u_ready=None):
            slot = segments[seg][1][pos][0]
            width = nf * P
            pe.wait_ge(w_ready[slot], use(seg, pos, i) + 2)
            H = wh[slot][:, 0:kt * width].rearrange("p (k n) -> p k n", k=kt)
            L = wl[slot][:, 0:kt * width].rearrange("p (k n) -> p k n", k=kt)
            step = min(ntok, HALF)

            def product(f, k, b):
                for j, (w, u) in enumerate(((H, UH), (H, UL), (L, UH))):
                    for h in range(ntok // step):
                        mm = pe.matmul(pair(b)[:, h * step:(h + 1) * step], w[:, k, f * P:f * P + P],
                                       u[:, u0 + k, h * step:(h + 1) * step],
                                       start=(k == 0 and j == 0), stop=(k == kt - 1 and j == 2))
                if k == kt - 1:
                    mm.then_inc(full.sem, 1)

            if nf == 2:
                pe.wait_ge(*free(n + 2))
                for k in range(kt):
                    if u_ready is not None:
                        pe.wait_ge(*u_ready(k + 1))
                    for f in range(2):
                        product(f, k, 2 * pos + f)
            else:
                for f in range(nf):
                    pe.wait_ge(*free(n + f + 1))
                    for k in range(kt):
                        product(f, k, f % 2)
            pe.drain().then_inc(w_free[slot], 1)

        def token_tiles(pe, seg, pos, full, free, n, ntt, bias_row=None, width=CH, c0=0):
            slot = segments[seg][1][pos][0]
            pe.wait_ge(w_ready[slot], use(seg, pos, 0) + 2)
            H = wh[slot][:].rearrange("p (k n) -> p k n", k=KT)
            L = wl[slot][:].rearrange("p (k n) -> p k n", k=KT)
            for t in range(ntt):
                pe.wait_ge(*free(n + t + 1))
                ps = PS[:, 4 + (n + t) % 4, 0:width]
                for k in range(KT):
                    for j, (w, u) in enumerate(((H, UH), (L, UH), (H, UL))):
                        mm = pe.matmul(ps, u[:, k, t * P:(t + 1) * P], w[:, k, c0:c0 + width],
                                  start=(k == 0 and j == 0),
                                  stop=(k == KT - 1 and j == 2 and bias_row is None))
                if bias_row is not None:
                    mm = pe.matmul(ps, ones[0:1, :], bias_row, start=False, stop=True)
                mm.then_inc(full.sem, 1)

        def free_slot(pe, seg, pos):
            pe.drain().then_inc(w_free[segments[seg][1][pos][0]], 1)


        class Setup(Stage):
            def setup(self):
                self.prm_loaded, self.p_full, self.v = self.count("prm_loaded", 0), self.count("p_full", 1), self.count("v", 0)

            def scalar(self, act):
                prow = XTf[:, 0:512].rearrange("p (t n) -> p t n", t=4)
                act.wait_ge(consts_ready, 1)
                for t, names in enumerate(PARAM_ROWS):
                    for name, n in names:
                        _, at, _ = PCOL[name]
                        if name == "conv_w_2a":
                            src = a["conv_w_2"].rearrange("o c (m p) -> (o c m) p", p=P)[0:88]
                        elif name == "conv_w_2b":
                            src = a["conv_w_2"].rearrange("o c (m p) -> (o c m) p", p=P)[88:132]
                        elif name == "conv_w":
                            src = a[name].rearrange("o c (m p) -> (o c m) p", p=P)
                        elif len(a[name].shape) == 1:
                            src = a[name].rearrange("(m p) -> m p", p=P)
                        else:
                            src = a[name].rearrange("o (m p) -> (o m) p", p=P)[0:n]
                        act.dma_start(prow[at:at + n, t, :], src).then_inc(self.prm_loaded.sem, 16)
                act.dma_start(small[0:1, 64:72], a["sinks"]).then_inc(self.prm_loaded.sem, 16)
                act.dma_start(small[0:8, 72:73], a["b_forget_2"].rearrange("o n -> n o")).then_inc(self.prm_loaded.sem, 16)

            def tensor(self, pe):
                for s in range(3):
                    pe.sem_inc(w_free[s], 1)
                pe.wait_ge(consts_ready, N_CONSTS)
                pe.wait_ge(*self.prm_loaded(16 * (N_PARAM_DMAS + 2)))
                for t in range(4):
                    pe.transpose(PS[:, 6, t * P:(t + 1) * P], XTf[:, t * P:(t + 1) * P], ident[:])
                pe.matmul(PS[:, 7, 0:8], ones[0:1, :], small[0:1, 64:72], start=True, stop=True).then_inc(self.p_full.sem, 1)

            def vector(self, dve):
                n = [0]

                def done(ins):
                    n[0] += 1
                    ins.then_inc(self.v.sem, 1)
                    dve.wait_ge(*self.v(n[0]))

                dve.wait_ge(consts_ready, N_CONSTS)
                si, ti = SC[:, 0:P].bitcast(I32), SC[:, P:2 * P].bitcast(I32)
                xi, xf, tri, lm = SC[:, 2 * P:3 * P].bitcast(I32), sc(3 * P, P), sc(4 * P, P), sc(5 * P, P)
                done(dve.tensor_tensor(xi, si, ti, ALU.bitwise_xor))
                done(dve.tensor_copy(xf, xi))
                done(dve.tensor_tensor(tri, ti, si, ALU.is_gt))
                done(dve.tensor_tensor(xf, xf, tri, ALU.mult))
                for l in range(LEVELS):
                    m = float(1 << l)
                    done(dve.tensor_scalar(tri, xf, m, None, ALU.is_ge))
                    done(dve.scalar_tensor_tensor(out=lm, in0=xf, scalar=2 * m, in1=tri, op0=ALU.is_lt, op1=ALU.mult))
                    done(dve.tensor_copy(lvl[:, l, :], lm))
                dve.wait_ge(*self.p_full(1))
                done(dve.tensor_copy(prm[:].rearrange("p t n -> p (t n)"), PS[:, 6, :]))
                done(dve.tensor_scalar(nsink, PS[:, 7, 0:8], -1.0, None, ALU.mult))
                done(dve.tensor_scalar(psink, PS[:, 7, 0:8], 1.0, None, ALU.mult))
                _, at, _ = PCOL["lb_logits"]
                l0, l1 = prm[:, 0, at:at + 4], prm[:, 0, at + 4:at + 8]
                done(dve.tensor_tensor(sm[:, 0:4], l0, l1, ALU.max))
                done(dve.tensor_tensor(sm[:, 4:8], l0, sm[:, 0:4], ALU.subtract))
                done(dve.tensor_tensor(sm[:, 8:12], l1, sm[:, 0:4], ALU.subtract))

        class TurnIn(Stage):
            def __init__(self, name, src, dst, n):
                self.src, self.dst, self.n = src, dst, n
                super().__init__(name)

            def setup(self):
                parts = max(1, self.n // HALF)
                self.loaded, self.full, self.free = self.count("loaded", 16 * parts), self.count("full", parts * KT), self.count("free", parts * KT)
                
            def scalar(self, act):
                parts = max(1, self.n // HALF)
                nb = min(4, self.n // P)
                rows = self.src.rearrange("(h b p) n -> h p b n", p=P, b=nb)
                act.dma_start(sc(0, nb * D).rearrange("p (b n) -> p b n", b=nb), rows[0]).then_inc(self.loaded.sem, 16)
                for h in range(parts):
                    for k in range(KT):
                        n = h * KT + k
                        act.wait_ge(*self.full(n + 1))
                        act.activation(self.dst[:, k, h * HALF:h * HALF + nb * P], PS[:, n % 2, 0:nb * P],
                                       ACT.Copy).then_inc(self.free.sem, 1)
                    if h + 1 < parts:
                        act.dma_start(sc(0, nb * D).rearrange("p (b n) -> p b n", b=nb), rows[h + 1]).then_inc(self.loaded.sem, 16)

            def ready(self, k):
                return self.free(max(1, self.n // HALF) * KT)

            def tensor(self, pe):
                parts, nb = max(1, self.n // HALF), min(4, self.n // P)
                for h in range(parts):
                    pe.wait_ge(*self.loaded(16 * (h + 1)))
                    for k in range(KT):
                        n = h * KT + k
                        if n >= 2:
                            pe.wait_ge(*self.free(n - 1))
                        for b in range(nb):
                            tr = pe.transpose(PS[:, n % 2, b * P:(b + 1) * P], sc(b * D + k * P, P), ident[:])
                        tr.then_inc(self.full.sem, 1)

        class SetupBound(Stage):
            def setup(self):
                self.e, self.v = self.count("e", 1), self.count("v", 4)

            def scalar(self, act):
                act.activation(sm[:, 12:20], sm[:, 4:12], ACT.Exp).then_inc(self.e.sem, 1)

            def vector(self, dve):
                dve.wait_ge(*self.e(1))
                dve.tensor_tensor(sm[:, 20:24], sm[:, 12:16], sm[:, 16:20], ALU.add).then_inc(self.v.sem, 1)
                dve.wait_ge(*self.v(1))
                dve.reciprocal(sm[:, 24:28], sm[:, 20:24]).then_inc(self.v.sem, 1)
                dve.wait_ge(*self.v(2))
                dve.tensor_tensor(lb, sm[:, 12:16], sm[:, 24:28], ALU.mult).then_inc(self.v.sem, 1)
                dve.tensor_tensor(omlb, sm[:, 16:20], sm[:, 24:28], ALU.mult).then_inc(self.v.sem, 1)


        class Norm(Stage):
            def __init__(self, name, weight, mode, src=None, n=T, store=False, before=None, fused=False):
                self.weight, self.mode, self.n, self.store = weight, mode, n, store
                self.src = XT if src is None else src
                self.before, self.fused = before, fused
                self.sums_on_pe = isinstance(before, Norm)
                self.follows = before is not None
                if before is not None and not self.sums_on_pe:
                    before.norm_after = self
                super().__init__(name)

            def setup(self):
                split = self.mode == "split"
                self.sq_ready, self.acc = self.count("sq_ready", KT), self.count("acc", 0 if self.sums_on_pe else KT - 1)
                self.sq_used = self.count("sq_used", KT if self.sums_on_pe else 1)
                self.ln, self.rstd_ready = self.count("ln", 1), self.count("rstd", 1)
                self.u_ready = self.count("u", 0 if self.mode == "inplace" else KT)
                self.hi_ready, self.lo_ready = self.count("hi", KT * split), self.count("lo", KT * split)
                self.res = self.count("res", 16 * (self.mode == "post"))
                self.xn, self.stored = self.count("xn", KT * (not split)), self.count("stored", 16 * self.store)
                n = self.n
                self.sq = [sc(0, n), sc(T, n)]
                self.lnv, self.rstd = sc(2 * T, n), sc(3 * T, n)
                self.sum = self.lnv
                self.u = [sc(4 * T, n), sc(5 * T, n)]

            def ready(self, k):
                return self.xn(k + 1)

            def scalar(self, act):
                for k in range(KT):
                    if self.before is not None:
                        act.wait_ge(*self.before.ready(k))
                    if k >= 2:
                        act.wait_ge(*(self.sq_used(k - 1) if self.sums_on_pe else self.acc(max(1, k - 2))))
                    act.activation(self.sq[k % 2], self.src[:, k, :], ACT.Square).then_inc(self.sq_ready.sem, 1)
                if self.mode == "post":
                    act.dma_start(UH[:].bitcast(F32), xres.rearrange("(k p) t -> p k t", p=P)).then_inc(self.res.sem, 16)
                if self.store:
                    act.dma_start(xres.rearrange("(k p) t -> p k t", p=P), XT[:]).then_inc(self.stored.sem, 16)
                act.wait_ge(*self.sq_used(KT if self.sums_on_pe else 1))
                act.activation(self.lnv, pair(0)[:, 0:self.n], ACT.Ln, bias=eps, scale=1.0 / D).then_inc(self.ln.sem, 1)
                act.wait_ge(*self.ln(1))
                act.activation(self.rstd, self.lnv, ACT.Exp, scale=-0.5).then_inc(self.rstd_ready.sem, 1)
                if self.mode == "split":
                    for k in range(KT):
                        act.wait_ge(*self.u_ready(k + 1))
                        act.activation(UH[:, k, 0:self.n], self.u[k % 2], ACT.Copy).then_inc(self.hi_ready.sem, 1)
                if self.store:
                    act.wait_ge(*self.stored(16))

            def tensor(self, pe):
                step = min(self.n, HALF)
                if not self.sums_on_pe:
                    pe.wait_ge(*self.acc(KT - 1))
                    for h in range(self.n // step):
                        mm = pe.matmul(PS[:, h, 0:step], ones[:], self.sum[:, h * step:(h + 1) * step], start=True, stop=True)
                    mm.then_inc(self.sq_used.sem, 1)
                    if self.mode == "split":
                        warm_up(pe, 20)
                    return
                for k in range(KT):
                    pe.wait_ge(*self.sq_ready(k + 1))
                    for h in range(self.n // step):
                        mm = pe.matmul(PS[:, h, 0:step], ones[:], self.sq[k % 2][:, h * step:(h + 1) * step],
                                       start=k == 0, stop=k == KT - 1)
                    mm.then_inc(self.sq_used.sem, 1)
                if self.mode == "split":
                    warm_up(pe, 20)

            def accumulate(self, dve, k):
                if k == 0:
                    return
                dve.wait_ge(*self.sq_ready(k + 1))
                if k == 1:
                    dve.tensor_tensor(self.sum, self.sq[0], self.sq[1], ALU.add).then_inc(self.acc.sem, 1)
                else:
                    dve.wait_ge(*self.acc(k - 1))
                    dve.tensor_tensor(self.sum, self.sum, self.sq[k % 2], ALU.add).then_inc(self.acc.sem, 1)

            def vector(self, dve):
                if self.fused:
                    self.accumulate(dve, KT - 1)
                elif not self.sums_on_pe:
                    for k in range(KT):
                        self.accumulate(dve, k)
                dve.wait_ge(*self.rstd_ready(1))
                if self.mode == "post":
                    dve.wait_ge(*self.res(16))

                def lo(k):
                    dve.wait_ge(*self.hi_ready(k + 1))
                    dve.tensor_tensor(UL[:, k, 0:self.n], self.u[k % 2], UH[:, k, 0:self.n].bitcast(F32),
                                      ALU.subtract).then_inc(self.lo_ready.sem, 1)

                def add(k):
                    dve.wait_ge(*self.u_ready(k + 1))
                    dve.tensor_tensor(XT[:, k, :], self.u[k % 2], UH[:, k, :].bitcast(F32), ALU.add).then_inc(self.xn.sem, 1)

                for k in range(KT):
                    if self.mode == "inplace":
                        dve.scalar_tensor_tensor(out=XT[:, k, :], in0=XT[:, k, :], scalar=pc(self.weight, k), in1=self.rstd,
                                                 op0=ALU.mult, op1=ALU.mult).then_inc(self.xn.sem, 1)
                        continue
                    if k >= 2:
                        dve.wait_ge(*(self.lo_ready if self.mode == "split" else self.xn)(k - 1))
                    dve.scalar_tensor_tensor(out=self.u[k % 2], in0=self.src[:, k, :], scalar=pc(self.weight, k),
                                             in1=self.rstd, op0=ALU.mult, op1=ALU.mult).then_inc(self.u_ready.sem, 1)
                    if k >= 1:
                        (lo if self.mode == "split" else add)(k - 1)
                if self.mode != "inplace":
                    (lo if self.mode == "split" else add)(KT - 1)


        class Project(Stage):
            def __init__(self, name, loops, ntok=T, u0=0, kt=KT, norm_before=None):
                self.loops, self.ntok, self.u0, self.kt = loops, ntok, u0, kt
                self.norm_before, self.follows = norm_before, norm_before is not None
                super().__init__(name)

            def setup(self):
                n = sum(segments[seg][0] * sum(c[2] for c in chunks) for seg, chunks in self.loops)
                self.full, self.free, self.z_done = self.count("full", n), self.count("free", n + 4), self.count("z_done", n)
                self.z_stored = [self.count(f"z_stored{s}", 16 * ((n + 1 - s) // 2) + 16) for s in range(2)]
                self.z = [sc(0, self.ntok), sc(T, self.ntok)]

            def tensor(self, pe):
                n = 0
                for seg, chunks in self.loops:
                    iters = segments[seg][0]

                    def body(i):
                        for pos in range(len(chunks)):
                            nf = chunks[pos][2]
                            feature_tiles(pe, seg, pos, i, self.full, self.free, n + (i * per + pos * 2), nf=nf,
                                          ntok=self.ntok, u0=self.u0, kt=self.kt, u_ready=self.norm_before.lo_ready if self.norm_before else None)
                    per = sum(c[2] for c in chunks)
                    iterate(pe, iters, body)
                    n += iters * per

            def scalar(self, act):
                act.sem_inc(self.free.sem, 4)
                for s in range(2):
                    act.sem_inc(self.z_stored[s].sem, 16)
                n = 0
                for seg, chunks in self.loops:
                    iters = segments[seg][0]
                    per = sum(c[2] for c in chunks)
                    assert per % 2 == 0 or iters == 1

                    def body(i):
                        for pos, (finish, where, nf) in enumerate(chunks):
                            for f in range(nf):
                                t = pos * 2 + f
                                s = (n + t) % 2
                                act.wait_ge(*self.full(n + (i * per + t) + 1))
                                uses = (n + t) // 2 + i * (per // 2)
                                act.wait_ge(*self.z_stored[s](16 * uses + 16))
                                apart(act)
                                finish(act, self.z[s], pair(2 * pos + f)[:, 0:self.ntok], i, f, self.free)
                                act.drain().then_inc(self.z_done.sem, 1)
                                act.wait_ge(*self.z_done(n + (i * per + t) + 1))
                                act.dma_start(where(i, f), self.z[s]).then_inc(self.z_stored[s].sem, 16)
                    iterate(act, iters, body)
                    n += iters * per
                for s in range(2):
                    act.wait_ge(*self.z_stored[s](16 * ((n + 1 - s) // 2) + 16))

        def finish_with(func, bias=None, scale=1.0):
            def finish(act, o, ps, i, f, free):
                kw = {"bias": bias(i, f)} if bias else {}
                act.activation(o, ps, func, scale=scale, **kw).then_inc(free.sem, 1)
            return finish

        def rows_at(z, base, step):
            return lambda i, f: z[bass.ds(i * step + (base + f * P), P), :]

        class ProjectTokens(Stage):
            def __init__(self, name, dest, jobs, ntt=NBLK, key=None):
                self.dest, self.jobs, self.ntt, self.key = dest, jobs, ntt, key
                super().__init__(name)

            def setup(self):
                n, key = len(self.jobs) * self.ntt, 1 if self.key else 0
                self.full, self.free = self.count("full", n), self.count("free", n + 4)
                self.stored = self.count("stored", 16 * (len(self.jobs) + key))
                self.kfull, self.kdone, self.brow = self.count("kfull", key), self.count("kdone", key), self.count("brow", 16 * key)

            def tensor(self, pe):
                n = 0
                for seg, pos, c0, width, where, bias in self.jobs:
                    if bias:
                        pe.wait_ge(*self.brow(16))
                    token_tiles(pe, seg, pos, self.full, self.free, n, self.ntt, width=width, c0=c0,
                                bias_row=SC[0:1, 0:P] if bias else None)
                    if self.key and self.key[0:2] == (seg, pos):
                        slot = segments[seg][1][pos][0]
                        H = wh[slot][:].rearrange("p (k n) -> p k n", k=KT)
                        L = wl[slot][:].rearrange("p (k n) -> p k n", k=KT)
                        for k in range(KT):
                            for j, (w, u) in enumerate(((H, UH), (H, UL), (L, UH))):
                                for h in range(2):
                                    pe.matmul(PS[:, h, :], w[:, k, 0:P], u[:, k, h * HALF:(h + 1) * HALF],
                                              start=(k == 0 and j == 0), stop=(k == KT - 1 and j == 2))
                        pe.drain().then_inc(self.kfull.sem, 1)
                    free_slot(pe, seg, pos)
                    n += self.ntt

            def scalar(self, act):
                if any(j[5] for j in self.jobs):
                    act.dma_start(SC[0:1, 0:P], a["b_attn"][0:1, 640:768]).then_inc(self.brow.sem, 16)
                act.sem_inc(self.free.sem, 4)
                n = 0
                for q, (seg, pos, c0, width, where, bias) in enumerate(self.jobs):
                    st = XTf[:, (q % 2) * 2048:(q % 2) * 2048 + self.ntt * width].rearrange("p (t n) -> p t n", n=width)
                    if q >= 2:
                        act.wait_ge(*self.stored(16 * q))
                    for t in range(self.ntt):
                        act.wait_ge(*self.full(n + 1))
                        act.activation(st[:, t, :], PS[:, 4 + n % 4, 0:width], ACT.Copy).then_inc(self.free.sem, 1)
                        n += 1
                    act.wait_ge(*self.free(n + 4))
                    act.dma_start(self.dest[:, where:where + width].rearrange("(t p) n -> p t n", p=P), st).then_inc(self.stored.sem, 16)
                if self.key:
                    act.wait_ge(*self.kfull(1))
                    act.activation(sc(T, T), pair(0), ACT.Identity, bias=self.key[3]).then_inc(self.kdone.sem, 1)
                    act.wait_ge(*self.kdone(1))
                    act.dma_start(self.key[2], sc(T, T)).then_inc(self.stored.sem, 16)
                act.wait_ge(*self.stored(16 * (len(self.jobs) + (1 if self.key else 0))))


        class OutProduct(Stage):
            def __init__(self, name, seg, nf, kt, residual):
                self.seg, self.nf, self.kt, self.residual = seg, nf, kt, residual
                super().__init__(name)

            def setup(self):
                self.ahead = 4 if self.nf == 2 else 2
                self.full, self.free, self.res = self.count("full", KT), self.count("free", KT + self.ahead), self.count("res", 16 * self.residual)

            def ready(self, k):
                return self.free(k + 1 + self.ahead)

            def tensor(self, pe):
                iterate(pe, segments[self.seg][0], lambda i: [
                    feature_tiles(pe, self.seg, pos, i, self.full, self.free, i * (2 * self.nf) + pos * self.nf, nf=self.nf, kt=self.kt)
                    for pos in range(2)])

            def scalar(self, act):
                if self.residual:
                    act.dma_start(XT[:], xres.rearrange("(k p) t -> p k t", p=P)).then_inc(self.res.sem, 16)

            def vector(self, dve):
                dve.sem_inc(self.free.sem, self.ahead)
                if self.residual:
                    dve.wait_ge(*self.res(16))
                for t in range(KT):
                    dve.wait_ge(*self.full(t + 1))
                    ps = pair(t % self.ahead)
                    if self.residual:
                        dve.tensor_tensor(XT[:, t, :], ps, XT[:, t, :], ALU.add).then_inc(self.free.sem, 1)
                    else:
                        dve.tensor_copy(XT[:, t, :], ps).then_inc(self.free.sem, 1)
                    if t >= 1:
                        self.norm_after.accumulate(dve, t - 1)


        class FFN(Stage):
            def __init__(self, name, seg, second, norm_before):
                self.seg, self.second = seg, second
                self.norm_before, self.follows = norm_before, True
                super().__init__(name)

            def setup(self):
                s, n = self.count, 2 * FG
                self.g_full, self.u_full, self.y_full = s("g_full", n), s("u_full", n), s("y_full", FG * KT)
                self.ps_free, self.y_free = s("ps_free", 2 * n + 2), s("y_free", FG * KT + 2)
                self.tap, self.c1, self.c2, self.gate, self.prod = s("tap", n), s("c1", n), s("c2", n), s("gate", n), s("prod", n + 1)
                self.hi, self.a_ready = s("hi", n), s("a_ready", n + 1)
                self.utap, self.u1, self.u2 = (s(x, n * self.second) for x in ("utap", "u1", "u2"))
                self.g_free, self.cleared = s("g_free", n + 2), s("cleared", 1 * self.second)
                self.AH = aH[:]
                self.AL = aL[:]
                self.g = [sc(0, T), sc(T, T)]
                self.t = sc(2 * T, T)
                self.p = sc(3 * T, T)

            def ready(self, k):
                return self.y_free(2 + (FG - 1) * KT + k + 1)

            def half_group(self, pe, g, slot, full, u_ready=None):
                pe.wait_ge(w_ready[slot], g + (bases[self.seg + "_head"][slot] + 2))
                H = wh[slot][:].rearrange("p (k n) -> p k n", k=KT)
                L = wl[slot][:].rearrange("p (k n) -> p k n", k=KT)
                if u_ready is not None:
                    pe.wait_ge(*self.ps_free(2))
                    for k in range(KT):
                        pe.wait_ge(*u_ready(k + 1))
                        for f in range(2):
                            for j, (w, u) in enumerate(((H, UH), (H, UL), (L, UH))):
                                for h in range(2):
                                    mm = pe.matmul(PS[:, 2 * f + h, :], w[:, k, f * P:(f + 1) * P], u[:, k, h * HALF:(h + 1) * HALF],
                                                   start=(k == 0 and j == 0), stop=(k == KT - 1 and j == 2))
                            if k == KT - 1:
                                mm.then_inc(full.sem, 1)
                    pe.drain().then_inc(w_free[slot], 1)
                    return
                for f in range(2):
                    pe.wait_ge(*self.ps_free(g * 4 + (slot * 2 + f + 1)))
                    for k in range(KT):
                        for j, (w, u) in enumerate(((H, UH), (H, UL), (L, UH))):
                            for h in range(2):
                                mm = pe.matmul(PS[:, 2 * f + h, :], w[:, k, f * P:(f + 1) * P], u[:, k, h * HALF:(h + 1) * HALF],
                                               start=(k == 0 and j == 0), stop=(k == KT - 1 and j == 2))
                    mm.then_inc(full.sem, 1)
                pe.drain().then_inc(w_free[slot], 1)

            def down(self, pe, g):
                pe.wait_ge(w_ready[2], g + (bases[self.seg][2] + 2))
                pe.wait_ge(*self.a_ready(g * 2 + 3))
                H = wh[2][:].rearrange("p (k n) -> p k n", k=2)
                L = wl[2][:].rearrange("p (k n) -> p k n", k=2)
                for m in range(KT):
                    pe.wait_ge(*self.y_free(g * KT + (m + 1)))
                    for k in range(2):
                        for j, (w, u) in enumerate(((H, self.AH), (H, self.AL), (L, self.AH))):
                            for h in range(2):
                                mm = pe.matmul(PS[:, 4 + 2 * (m % 2) + h, :], w[:, k, m * P:(m + 1) * P],
                                               u[:, k, h * HALF:(h + 1) * HALF],
                                               start=(k == 0 and j == 0), stop=(k == 1 and j == 2))
                    mm.then_inc(self.y_full.sem, 1)
                pe.drain().then_inc(w_free[2], 1)

            def tensor(self, pe):
                self.half_group(pe, 0, 0, self.g_full, self.norm_before.lo_ready)
                self.half_group(pe, 0, 1, self.u_full)
                with loop(pe, FG - 1) as g:
                    self.half_group(pe, g + 1, 0, self.g_full)
                    self.down(pe, g)
                    self.half_group(pe, g + 1, 1, self.u_full)
                self.down(pe, FG - 1)

            def taps(self, g, f, col0):
                def col(name, base):
                    t, at, _ = PCOL[name]
                    return prm[:, t, bass.ds(g * 2 + (at + base + f + col0), 1)]
                if self.second:
                    return col("conv_w_2a", 0), col("conv_w_2a", 44), col("conv_w_2b", 0), col("conv_b_2", 0)
                return col("conv_w", 0), col("conv_w", 22), col("conv_w", 44), col("conv_b", 0)

            def scalar(self, act):
                def gates(g):
                    for f in range(2):
                        n = g * 2 + f
                        _, _, w2, b = self.taps(g, f, 0)
                        act.wait_ge(*self.g_full(n + 1))
                        act.wait_ge(*self.g_free(n + 1))
                        apart(act)
                        act.activation(self.g[f], pair(f), ACT.Identity, bias=b, scale=w2).then_inc(self.tap.sem, 1)
                        act.wait_ge(*self.c2(n + 1))
                        act.activation(self.g[f], self.g[f], ACT.Gelu_apprx_tanh if self.second else ACT.Silu).then_inc(self.gate.sem, 1)

                def ups(g):
                    for f in range(2):
                        n = g * 2 + f
                        if self.second:
                            _, _, w2, b = self.taps(g, f, 22)
                            act.wait_ge(*self.u_full(n + 1))
                            act.wait_ge(*self.prod(n + 1))
                            apart(act)
                            act.activation(self.t, pair(f), ACT.Identity, bias=b, scale=w2).then_inc(self.utap.sem, 1)
                        act.wait_ge(*self.prod(n + 2))
                        act.activation(self.AH[:, f, :], self.p, ACT.Copy).then_inc(self.hi.sem, 1)

                with loop(act, FG) as g:
                    gates(g)
                    ups(g)

            def vector(self, dve):
                dve.wait_ge(*self.norm_before.lo_ready(KT))
                dve.sem_inc(self.ps_free.sem, 2)
                dve.sem_inc(self.y_free.sem, 2)
                dve.sem_inc(self.g_free.sem, 2)
                dve.sem_inc(self.prod.sem, 1)
                dve.sem_inc(self.a_ready.sem, 1)
                if self.second:
                    dve.wait_ge(*self.norm_before.stored(16))
                    dve.memset(XTf, 0.0).then_inc(self.cleared.sem, 1)
                    dve.wait_ge(*self.cleared(1))

                def older(o, ps, w0, w1, ready, n, s1, s2, free):
                    dve.wait_ge(*ready(n + 1))
                    dve.scalar_tensor_tensor(out=o[:, 1:T], in0=ps[:, 0:T - 1], scalar=w1, in1=o[:, 1:T],
                                             op0=ALU.mult, op1=ALU.add).then_inc(s1.sem, 1)
                    dve.wait_ge(*s1(n + 1))
                    dve.scalar_tensor_tensor(out=o[:, 2:T], in0=ps[:, 0:T - 2], scalar=w0, in1=o[:, 2:T],
                                             op0=ALU.mult, op1=ALU.add).then_inc(s2.sem, 1)
                    if free is not None:
                        dve.wait_ge(*s2(n + 1))
                        dve.sem_inc(free.sem, 1)

                def gates(g):
                    for f in range(2):
                        w0, w1, _, _ = self.taps(g, f, 0)
                        older(self.g[f], pair(f), w0, w1, self.tap, g * 2 + f, self.c1, self.c2, self.ps_free)

                def ups(g):
                    for f in range(2):
                        n = g * 2 + f
                        if self.second:
                            w0, w1, _, _ = self.taps(g, f, 22)
                            older(self.t, pair(f), w0, w1, self.utap, n, self.u1, self.u2, self.ps_free)
                            up = self.t
                        else:
                            dve.wait_ge(*self.u_full(n + 1))
                            up = pair(f)
                        dve.wait_ge(*self.gate(n + 1))
                        dve.wait_ge(*self.a_ready(n + 1))
                        dve.tensor_tensor(self.p, up, self.g[f], ALU.mult).then_inc(self.prod.sem, 1)
                        dve.wait_ge(*self.prod(n + 2))
                        if not self.second:
                            dve.sem_inc(self.ps_free.sem, 1)
                        dve.sem_inc(self.g_free.sem, 1)
                        dve.wait_ge(*self.hi(n + 1))
                        dve.tensor_tensor(self.AL[:, f, :], self.p, self.AH[:, f, :].bitcast(F32), ALU.subtract).then_inc(self.a_ready.sem, 1)

                def add(g, norm=None):
                    for m in range(KT):
                        dve.wait_ge(*self.y_full(g * KT + (m + 1)))
                        dve.tensor_tensor(XT[:, m, :], pair(2 + m % 2), XT[:, m, :], ALU.add).then_inc(self.y_free.sem, 1)
                        if norm is not None and m >= 1:
                            norm.accumulate(dve, m - 1)

                gates(0)
                ups(0)
                with loop(dve, FG - 1) as g:
                    gates(g + 1)
                    add(g)
                    ups(g + 1)
                add(FG - 1, self.norm_after)

        class Split(Stage):
            def setup(self):
                self.hi = self.count("hi", KT)

            def scalar(self, act):
                for k in range(KT):
                    act.activation(UH[:, k, :], XT[:, k, :], ACT.Copy).then_inc(self.hi.sem, 1)

            def vector(self, dve):
                for k in range(KT):
                    dve.wait_ge(*self.hi(k + 1))
                    dve.tensor_tensor(UL[:, k, :], XT[:, k, :], UH[:, k, :].bitcast(F32), ALU.subtract)


        class Attend(Stage):
            def __init__(self, name, heads, rows, dv, scale, keys, loads, n_loads, sinks=False):
                self.heads, self.rows, self.dv, self.scale = heads, rows, dv, scale
                self.keys, self.loads, self.n_loads, self.sinks = keys, loads, n_loads, sinks
                super().__init__(name)

            def setup(self):
                s, n = self.count, self.heads * NBLK
                self.loaded = [s(f"loaded{j}", 16 * self.n_loads * self.heads // 2) for j in range(2)]
                self.s_full, self.exp_done = s("s_full", n), s("exp_done", n + 2)
                self.pt_full, self.pt_copied = s("pt_full", n + 2), s("pt_copied", n + 1)
                self.o_full, self.o_free = s("o_full", n + 16), s("o_free", n + 2)
                self.m_ready, self.mx, self.den, self.inv = s("m_ready", n), s("mx", n), s("den", n * self.sinks), s("inv", n)
                self.Q = [XTf[:, 0:T], sc(5120, T)]
                self.K = [XTf[:, 1024 + 1152 * j:1024 + 1152 * j + T] for j in range(2)]
                self.V = [sc(4096 + 512 * j, 512) for j in range(2)]
                self.O = XTf[:, 3328:3328 + 4096].rearrange("p (b n) -> p b n", b=NBLK)
                self.Pb = [sc(0, T), sc(T, T)]
                self.PT = [sc(2 * T, T), sc(3 * T, T)]

            def sync(self, sp):
                self.after(sp)
                with loop(sp, self.heads // 2) as i:
                    for s in range(2):
                        sp.wait_ge(*self.o_full(i * 16 + 8 * (s + 1)))
                        apart(sp)
                        self.loads(sp, i * 2 + s, s, self)

            def tensor(self, pe):
                pe.sem_inc(self.pt_full.sem, 2)
                pe.sem_inc(self.o_full.sem, 16)

                def scores(i, t):
                    s, b = t // 8, t % 8
                    k0, nk, masks = self.keys(b)
                    if b == 0:
                        pe.wait_ge(*self.loaded[s](i * (16 * self.n_loads) + 16 * self.n_loads))
                    pe.wait_ge(*self.exp_done(i * 16 + (t + 1)))
                    ps = pair(t % 2)
                    last = nk * P
                    for c in range(0, last, HALF):
                        e = min(c + HALF, last)
                        inside = [m for m in masks if c <= m[0] * P < e]
                        for j, (kb, m) in enumerate(inside):
                            pe.matmul(ps[:, kb * P:(kb + 1) * P], identb[:], bmask[:, m, :], start=j == 0,
                                      stop=False, skip_group_check=True)
                        mm = pe.matmul(ps[:, c:e], self.Q[s][0:self.rows, b * P:(b + 1) * P],
                                       self.K[s][0:self.rows, k0 * P + c:k0 * P + e], start=not inside, stop=True,
                                       skip_group_check=True)
                    mm.then_inc(self.s_full.sem, 1)

                def turn(i, u):
                    nk = self.keys(u % 8)[1]
                    pe.wait_ge(*self.exp_done(i * 16 + (u + 3)))
                    pe.wait_ge(*self.pt_copied(i * 16 + (u + 1)))
                    for j in range(nk):
                        tr = pe.transpose(pair(2)[:, j * P:(j + 1) * P], self.Pb[u % 2][:, j * P:(j + 1) * P], ident[:])
                    tr.then_inc(self.pt_full.sem, 1)

                def values(i, u):
                    s, b = u // 8, u % 8
                    k0, nk, _ = self.keys(b)
                    V = self.V[s].rearrange("p (b n) -> p b n", n=self.dv)
                    pe.wait_ge(*self.pt_copied(i * 16 + (u + 2)))
                    pe.wait_ge(*self.o_free(i * 16 + (u + 1)))
                    for j in range(nk):
                        mm = pe.matmul(PS[:, 6 + u % 2, 0:self.dv], self.PT[u % 2][:, j * P:(j + 1) * P],
                                       V[:, k0 + j, :], start=j == 0, stop=j == nk - 1)
                    mm.then_inc(self.o_full.sem, 1)

                warm_up(pe, 20)
                rotated(pe, self.heads // 2, 16, [(0, scores), (1, turn), (2, values)])

            def scalar(self, act):
                act.sem_inc(self.exp_done.sem, 2)
                act.sem_inc(self.pt_copied.sem, 1)

                def probs(i, t):
                    nk = self.keys(t % 8)[1]
                    act.wait_ge(*self.m_ready(i * 16 + (t + 1)))
                    act.wait_ge(*self.pt_full(i * 16 + (t + 1)))
                    apart(act)
                    if self.sinks:
                        act.activation(sm[:, 8 + t % 4:9 + t % 4], sm[:, 4 + t % 4:5 + t % 4], ACT.Exp,
                                       bias=psink[:, bass.ds(i * 2 + t // 8, 1)])
                    act.activation(self.Pb[t % 2][:, 0:nk * P], pair(t % 2)[:, 0:nk * P], ACT.Exp,
                                   bias=sm[:, 4 + t % 4:5 + t % 4], scale=self.scale,
                                   accum_out=sm[:, 12 + t % 4:13 + t % 4]).then_inc(self.exp_done.sem, 1)

                def turned(i, u):
                    nk = self.keys(u % 8)[1]
                    act.wait_ge(*self.pt_full(i * 16 + (u + 3)))
                    act.wait_ge(*self.o_full(i * 16 + (u + 15)))
                    act.activation(self.PT[u % 2][:, 0:nk * P], pair(2)[:, 0:nk * P], ACT.Copy)\
                       .then_inc(self.pt_copied.sem, 1)

                rotated(act, self.heads // 2, 16, [(0, probs), (1, turned)])

            def vector(self, dve):
                dve.sem_inc(self.o_free.sem, 2)

                def maximum(i, t):
                    nk = self.keys(t % 8)[1]
                    dve.wait_ge(*self.s_full(i * 16 + (t + 1)))
                    dve.reduce_max(sm[:, t % 4:t % 4 + 1], pair(t % 2)[:, 0:nk * P], AX.X).then_inc(self.mx.sem, 1)
                    dve.wait_ge(*self.mx(i * 16 + (t + 1)))
                    o, x = sm[:, 4 + t % 4:5 + t % 4], sm[:, t % 4:t % 4 + 1]
                    if self.sinks:
                        dve.tensor_scalar(o, x, -self.scale, nsink[:, bass.ds(i * 2 + t // 8, 1)], ALU.mult, ALU.min)\
                           .then_inc(self.m_ready.sem, 1)
                    else:
                        dve.tensor_scalar(o, x, -self.scale, None, ALU.mult).then_inc(self.m_ready.sem, 1)

                def output(i, u):
                    s, b = u // 8, u % 8
                    j = u % 4
                    den = sm[:, 12 + j:13 + j]
                    dve.wait_ge(*self.o_full(i * 16 + (u + 17)))
                    if self.sinks:
                        dve.tensor_tensor(sm[:, 16 + j:17 + j], den, sm[:, 8 + j:9 + j], ALU.add).then_inc(self.den.sem, 1)
                        dve.wait_ge(*self.den(i * 16 + (u + 1)))
                        den = sm[:, 16 + j:17 + j]
                    dve.reciprocal(sm[:, 20 + j:21 + j], den).then_inc(self.inv.sem, 1)
                    dve.wait_ge(*self.inv(i * 16 + (u + 1)))
                    dve.tensor_scalar(self.O[:, b, bass.ds(i * (2 * self.dv) + s * self.dv, self.dv)],
                                      PS[:, 6 + u % 2, 0:self.dv], sm[:, 20 + j:21 + j], None, ALU.mult)\
                       .then_inc(self.o_free.sem, 1)

                rotated(dve, self.heads // 2, 16, [(0, maximum), (2, output)])

        class TurnHeads(Stage):
            def __init__(self, name, src, u0):
                self.src, self.u0 = src, u0
                super().__init__(name)

            def setup(self):
                self.full, self.hi, self.free = self.count("full", 4), self.count("hi", 4), self.count("free", 4)

            def tensor(self, pe):
                for k in range(4):
                    if k >= 2:
                        pe.wait_ge(*self.free(k - 1))
                    for b in range(NBLK):
                        tr = pe.transpose(pair(k % 2)[:, b * P:(b + 1) * P], self.src[:, b, k * P:(k + 1) * P], ident[:])
                    tr.then_inc(self.full.sem, 1)

            def scalar(self, act):
                for k in range(4):
                    act.wait_ge(*self.full(k + 1))
                    act.activation(UH[:, self.u0 + k, :], pair(k % 2), ACT.Copy).then_inc(self.hi.sem, 1)

            def vector(self, dve):
                for k in range(4):
                    dve.wait_ge(*self.hi(k + 1))
                    dve.tensor_tensor(UL[:, self.u0 + k, :], pair(k % 2), UH[:, self.u0 + k, :].bitcast(F32),
                                      ALU.subtract).then_inc(self.free.sem, 1)


        class HGRN(Stage):
            def setup(self):
                def s(what):
                    return self.count(what, 0)
                self.loaded, self.head_done = s("loaded"), s("head_done")
                self.fk, self.lnf, self.scan = s("fk"), s("lnf"), s("scan")
                self.dd, self.ex, self.mr, self.pl, self.pr = s("dd"), s("ex"), s("mr"), s("pl"), s("pr")
                self.e0, self.q0, self.de, self.ke, self.ee = s("e0"), s("q0"), s("de"), s("ke"), s("ee")
                self.tk, self.kc, self.kv, self.st, self.oo = s("tk"), s("kc"), s("kv"), s("st"), s("oo")
                self.sq, self.ss, self.l2, self.r2, self.n1, self.n2, self.hi = (s(x) for x in ("sq", "ss", "l2", "r2", "n1", "n2", "hi"))

                def x(n):
                    return XTf[:, n * T:(n + 1) * T]
                self.q, self.f, self.g, self.v, self.b, self.k = (x(n) for n in range(6))
                self.E = [x(6), sc(T, T)]
                self.M = [x(7), sc(2 * T, T)]
                self.ST = sc(0, T)
                self.KE, self.KET, self.Q0, self.S, self.o = sc(T, T), sc(2 * T, T), sc(3 * T, T), sc(4 * T, T), sc(5 * T, T)

            def sync(self, sp):
                self.after(sp)
                with loop(sp, HG) as i:
                    sp.wait_ge(*self.head_done(i + 1))
                    apart(sp)
                    for dst, src in ((self.q, zq1), (self.f, zf1), (self.g, zg1)):
                        sp.dma_start(dst, src[bass.ds(i * P, P), :]).then_inc(self.loaded.sem, 16)
                    sp.dma_start(self.v.rearrange("p (c n) -> p c n", c=NBLK),
                                 v1.rearrange("(c p) n -> p c n", p=P)[:, :, bass.ds(i * P, P)]).then_inc(self.loaded.sem, 16)

            def tensor(self, pe):
                def c(t, n):
                    return t[:, n * P:(n + 1) * P]
                with loop(pe, HG) as i:
                    pe.wait_ge(*self.fk(i * 2 + 2))
                    for n in range(NBLK):
                        mm = pe.matmul(c(pair(1), n), c(self.k, n), c(self.q, n), start=True, stop=True)
                    mm.then_inc(self.pl.sem, 1)
                    for l in range(LEVELS):
                        pe.wait_ge(*self.mr(i * LEVELS + (l + 1)))
                        if l >= 1:
                            pe.wait_ge(*self.pr(i * 8 + l))
                        for n in range(NBLK):
                            mm = pe.matmul(c(pair(l % 2), n), c(self.M[l % 2], n), c(self.M[l % 2], n), start=True, stop=True)
                        mm.then_inc(self.pl.sem, 1)
                    pe.wait_ge(*self.ke(i + 1))
                    for n in range(NBLK):
                        mm = pe.transpose(c(pair(2), n), c(self.KE, n), ident[:])
                    mm.then_inc(self.tk.sem, 1)
                    pe.wait_ge(*self.kc(i + 1))
                    for n in range(NBLK):
                        mm = pe.matmul(c(pair(3), n), c(self.KET, n), c(self.v, n), start=True, stop=True)
                    mm.then_inc(self.kv.sem, 1)
                    pe.wait_ge(*self.pr(i * 8 + 8))
                    pe.wait_ge(*self.st(i * 7 + 7))
                    pe.wait_ge(*self.q0(i + 1))
                    for n in range(NBLK):
                        mm = pe.matmul(c(pair(0), n), c(self.v, n), c(self.ST, n), start=True, stop=n == 0)
                        if n:
                            mm = pe.matmul(c(pair(0), n), c(self.S, n), c(self.Q0, n), start=False, stop=True)
                    mm.then_inc(self.oo.sem, 1)
                    pe.wait_ge(*self.sq(i + 1))
                    for h in range(2):
                        mm = pe.matmul(PS[:, 2 + h, :], ones[:], self.o[:, h * HALF:(h + 1) * HALF], start=True, stop=True)
                    mm.then_inc(self.ss.sem, 1)

            def scalar(self, act):
                with loop(act, HG) as i:
                    act.wait_ge(*self.fk(i * 2 + 1))
                    act.activation(self.E[0], self.f, ACT.Ln).then_inc(self.lnf.sem, 1)
                    for l in range(LEVELS):
                        act.wait_ge(*self.dd(i * 14 + 2 * (l + 1)))
                        act.activation(self.E[l % 2], self.E[l % 2], ACT.Exp).then_inc(self.ex.sem, 1)
                    act.wait_ge(*self.mr(i * LEVELS + LEVELS))
                    act.activation(self.E[0], self.b, ACT.Exp).then_inc(self.e0.sem, 1)
                    act.wait_ge(*self.de(i + 1))
                    act.activation(self.KE, self.KE, ACT.Exp).then_inc(self.ee.sem, 1)
                    act.wait_ge(*self.tk(i + 1))
                    act.activation(self.KET, pair(2), ACT.Copy).then_inc(self.kc.sem, 1)
                    act.wait_ge(*self.oo(i + 1))
                    act.activation(self.o, pair(0), ACT.Square).then_inc(self.sq.sem, 1)
                    act.wait_ge(*self.ss(i + 1))
                    act.activation(self.E[1], pair(1), ACT.Ln, bias=eps, scale=1.0 / P).then_inc(self.l2.sem, 1)
                    act.wait_ge(*self.l2(i + 1))
                    act.activation(self.E[1], self.E[1], ACT.Exp, scale=-0.5).then_inc(self.r2.sem, 1)
                    act.wait_ge(*self.n2(i + 1))
                    apart(act)
                    act.activation(UH[:, bass.ds(i, 1), :], self.M[0], ACT.Copy).then_inc(self.hi.sem, 1)

            def vector(self, dve):
                dve.sem_inc(self.head_done.sem, 1)

                def halves(t, m):
                    v = t.rearrange("p (n h m) -> p n h m", h=2, m=m)
                    return v[:, :, 0, :], v[:, :, 1, :]

                with loop(dve, HG) as i:
                    dve.wait_ge(*self.loaded(i * 64 + 64))
                    dve.tensor_scalar(self.f, self.f, omlb[:, bass.ds(i, 1)], lb[:, bass.ds(i, 1)], ALU.mult, ALU.add)\
                       .then_inc(self.fk.sem, 1)
                    dve.wait_ge(*self.fk(i * 2 + 1))
                    dve.tensor_scalar(self.k, self.f, -1.0, 1.0, ALU.mult, ALU.add).then_inc(self.fk.sem, 1)
                    dve.wait_ge(*self.lnf(i + 1))
                    for n in range(NBLK):
                        s = slice(n * P, (n + 1) * P)
                        dve.tensor_tensor_scan(self.b[:, s], ones[:], self.E[0][:, s], 0.0, ALU.mult, ALU.add).then_inc(self.scan.sem, 1)
                    dve.wait_ge(*self.scan(i * 8 + 8))

                    def exponents(l):
                        m = 64 >> l
                        b0, b1 = halves(self.b, m)
                        e0, e1 = halves(self.E[l % 2], m)
                        ref = b0[:, :, m - 1:m].to_broadcast([P, T // (2 * m), m])
                        if l >= 2:
                            dve.wait_ge(*self.mr(i * LEVELS + (l - 1)))
                        dve.tensor_tensor(e0, ref, b0, ALU.subtract).then_inc(self.dd.sem, 1)
                        dve.tensor_tensor(e1, b1, ref, ALU.subtract).then_inc(self.dd.sem, 1)

                    def decayed(l):
                        m = 64 >> l
                        e0, e1 = halves(self.E[l % 2], m)
                        m0, m1 = halves(self.M[l % 2], m)
                        k0, _ = halves(self.k, m)
                        _, q1 = halves(self.q, m)
                        dve.wait_ge(*self.ex(i * LEVELS + (l + 1)))
                        if l >= 2:
                            dve.wait_ge(*self.pl(i * 8 + l))
                        dve.tensor_tensor(m0, k0, e0, ALU.mult)
                        dve.tensor_tensor(m1, q1, e1, ALU.mult).then_inc(self.mr.sem, 1)

                    def placed(l):
                        dve.wait_ge(*self.pl(i * 8 + (l + 2)))
                        dve.wait_ge(*self.pr(i * 8 + (l + 1)))
                        mask = lvl[:, 6 - l:7 - l, :].to_broadcast([P, NBLK, P])
                        apart(dve)
                        dve.copy_predicated(self.ST.rearrange("p (n t) -> p n t", n=NBLK), mask,
                                            pair(l % 2).rearrange("p (n t) -> p n t", n=NBLK)).then_inc(self.pr.sem, 1)

                    exponents(0)
                    dve.wait_ge(*self.pl(i * 8 + 1))
                    dve.tensor_tensor(self.ST.rearrange("p (n t) -> p n t", n=NBLK),
                                      pair(1).rearrange("p (n t) -> p n t", n=NBLK),
                                      ident[:].rearrange("p (o t) -> p o t", o=1).to_broadcast([P, NBLK, P]), ALU.mult).then_inc(self.pr.sem, 1)
                    for l in range(LEVELS):
                        if l + 1 < LEVELS:
                            exponents(l + 1)
                        decayed(l)
                        if l >= 1:
                            placed(l - 1)
                    bc = self.b.rearrange("p (n t) -> p n t", n=NBLK)
                    dve.wait_ge(*self.pl(i * 8 + 7))
                    dve.tensor_tensor(self.KE.rearrange("p (n t) -> p n t", n=NBLK),
                                      bc[:, :, P - 1:P].to_broadcast([P, NBLK, P]), bc, ALU.subtract).then_inc(self.de.sem, 1)
                    placed(LEVELS - 1)
                    dve.wait_ge(*self.ee(i + 1))
                    dve.tensor_tensor(self.KE, self.k, self.KE, ALU.mult).then_inc(self.ke.sem, 1)
                    dve.wait_ge(*self.e0(i + 1))
                    dve.tensor_tensor(self.Q0, self.q, self.E[0], ALU.mult).then_inc(self.q0.sem, 1)
                    dve.wait_ge(*self.kv(i + 1))
                    for n in range(NBLK - 1):
                        s0, s1 = slice(n * P, (n + 1) * P), slice((n + 1) * P, (n + 2) * P)
                        if n == 0:
                            dve.tensor_copy(self.S[:, s1], pair(3)[:, s0]).then_inc(self.st.sem, 1)
                        else:
                            dve.wait_ge(*self.st(i * 7 + n))
                            dve.scalar_tensor_tensor(out=self.S[:, s1], in0=self.S[:, s0], scalar=self.E[0][:, (n + 1) * P - 1:(n + 1) * P],
                                                     in1=pair(3)[:, s0], op0=ALU.mult, op1=ALU.add).then_inc(self.st.sem, 1)
                    dve.wait_ge(*self.r2(i + 1))
                    dve.scalar_tensor_tensor(out=self.o, in0=pair(0), scalar=pc("hg_norm_w"), in1=self.E[1],
                                             op0=ALU.mult, op1=ALU.mult).then_inc(self.n1.sem, 1)
                    dve.wait_ge(*self.n1(i + 1))
                    dve.tensor_tensor(self.M[0], self.o, self.g, ALU.mult).then_inc(self.n2.sem, 1)
                    dve.wait_ge(*self.hi(i + 1))
                    dve.tensor_tensor(UL[:, bass.ds(i, 1), :], self.M[0], UH[:, bass.ds(i, 1), :].bitcast(F32), ALU.subtract)\
                       .then_inc(self.head_done.sem, 1)


        class Forget(Stage):
            def setup(self):
                def s(what):
                    return self.count(what, 0)
                self.full, self.free, self.x, self.a1, self.st = s("full"), s("free"), s("x"), s("a1"), s("st")

            def tensor(self, pe):
                feature_tiles(pe, "in2_f", 0, 0, self.full, self.free, 0, nf=1)

            def scalar(self, act):
                x, t = sc(0, T)[0:8, :], sc(T, T)[0:8, :]
                act.wait_ge(*self.x(1))
                for n, (func, src, kw) in enumerate(((ACT.Abs, x, {}), (ACT.Exp, t, {"scale": -1.0}),
                                                     (ACT.Ln, t, {"bias": ones[0:8, 0:1]}))):
                    act.activation(t, src, func, **kw).then_inc(self.a1.sem, 1)
                    act.wait_ge(*self.a1(n + 1))
                act.wait_ge(*self.x(5))
                act.dma_start(fc, sc(2 * T, T)[0:8, :]).then_inc(self.st.sem, 16)
                act.dma_start(fnc, sc(3 * T, T)[0:8, :]).then_inc(self.st.sem, 16)
                act.dma_start(onesd, sc(4 * T, T)[0:1, :]).then_inc(self.st.sem, 16)
                act.wait_ge(*self.st(48))

            def vector(self, dve):
                dve.sem_inc(self.free.sem, 1)
                x, t, c = sc(0, T)[0:8, :], sc(T, T)[0:8, :], sc(2 * T, T)[0:8, :]
                one = sc(4 * T, T)[0:8, :]
                dve.memset(one, 1.0).then_inc(self.free.sem, 1)
                dve.wait_ge(*self.full(1))
                dve.tensor_scalar(x, pair(0)[0:8, :], binv[0:8, :], None, ALU.add).then_inc(self.x.sem, 1)
                dve.wait_ge(*self.a1(3))
                dve.wait_ge(*self.x(1))
                dve.scalar_tensor_tensor(out=t, in0=x, scalar=0.0, in1=t, op0=ALU.min, op1=ALU.subtract).then_inc(self.x.sem, 1)
                dve.wait_ge(*self.x(2))
                dve.wait_ge(*self.free(2))
                dve.tensor_tensor_scan(c, one, t, 0.0, ALU.mult, ALU.add).then_inc(self.x.sem, 1)
                dve.wait_ge(*self.x(3))
                dve.tensor_scalar(sc(3 * T, T)[0:8, :], c, -8.0, None, ALU.mult).then_inc(self.x.sem, 1)
                dve.wait_ge(*self.x(4))
                dve.tensor_scalar(c, c, 8.0, None, ALU.mult).then_inc(self.x.sem, 1)

        class Pooling(Stage):
            def setup(self):
                def s(what):
                    return self.count(what, 0)
                self.loaded, self.v, self.pooled, self.full, self.hi, self.free = (s(x) for x in ("loaded", "v", "pooled", "full", "hi", "free"))

            def scalar(self, act):
                act.dma_start(XT[:, 0:4, :], zpqk[0:512, :].rearrange("(k p) t -> p k t", p=P)).then_inc(self.loaded.sem, 16)
                act.dma_start(XT[:, 6, 0:512].rearrange("p (g n) -> p g n", g=4), a["pool_w_2"].rearrange("o g p n -> p (o g) n")).then_inc(self.loaded.sem, 16)
                for g in range(4):
                    act.wait_ge(*self.full(g + 1))
                    act.activation(UH[:, g, :], pair(g % 2), ACT.Copy, scale=pc("pool_scale_2", g)).then_inc(self.hi.sem, 1)

            def tensor(self, pe):
                for g in range(4):
                    pe.wait_ge(*self.pooled(g + 1))
                    if g >= 2:
                        pe.wait_ge(*self.free(g - 1))
                    for h in range(2):
                        mm = pe.matmul(pair(g % 2)[:, h * HALF:(h + 1) * HALF], XT[:, 6, g * P:(g + 1) * P],
                                       sc((2 + g % 2) * T + h * HALF, HALF), start=True, stop=True)
                    mm.then_inc(self.full.sem, 1)

            def vector(self, dve):
                n = [0]

                def done(ins):
                    n[0] += 1
                    ins.then_inc(self.v.sem, 1)
                    dve.wait_ge(*self.v(n[0]))

                def split(g):
                    dve.wait_ge(*self.hi(g + 1))
                    dve.scalar_tensor_tensor(out=UL[:, g, :], in0=pair(g % 2), scalar=pc("pool_scale_2", g),
                                             in1=UH[:, g, :].bitcast(F32), op0=ALU.mult, op1=ALU.subtract).then_inc(self.free.sem, 1)

                dve.wait_ge(*self.loaded(32))
                for g in range(4):
                    w = 2 << g
                    u, cur = XT[:, g, :], XT[:, g, :]
                    for j in range(g + 1):
                        step, nxt = 1 << j, sc((j % 2) * T, T)
                        done(dve.tensor_copy(nxt[:, 0:step], cur[:, 0:step]))
                        done(dve.tensor_tensor(nxt[:, step:T], cur[:, step:T], cur[:, 0:T - step], ALU.add))
                        cur = nxt
                    o = sc((2 + g % 2) * T, T)
                    if g >= 2:
                        dve.wait_ge(*self.full(g - 1))
                    done(dve.scalar_tensor_tensor(out=o[:, w:T], in0=cur[:, w:T], scalar=1.0 / w, in1=u[:, w:T],
                                                  op0=ALU.mult, op1=ALU.subtract))
                    done(dve.tensor_tensor(o[:, 0:w], cur[:, 0:w], invt[:, 0:w], ALU.mult))
                    dve.tensor_tensor(o[:, 0:w], o[:, 0:w], u[:, 0:w], ALU.subtract).then_inc(self.pooled.sem, 1)
                    if g >= 1:
                        split(g - 1)
                split(3)

        class Branches(Stage):
            def setup(self):
                def s(what):
                    return self.count(what, 0)
                self.full, self.free, self.m, self.sum, self.loaded = s("full"), s("free"), s("m"), s("sum"), [s("loaded0"), s("loaded1")]

            def tensor(self, pe):
                with loop(pe, 2) as i:
                    for pos in range(2):
                        pe.wait_ge(w_ready[pos], use("branches", pos, i) + 2)
                    for f in range(4):
                        for pos in range(2):
                            H = wh[pos][:].rearrange("p (k n) -> p k n", k=4)
                            L = wl[pos][:].rearrange("p (k n) -> p k n", k=4)
                            pe.wait_ge(*self.free(i * 8 + (f * 2 + pos + 1)))
                            for k in range(4):
                                for j, (w, u) in enumerate(((H, UH), (H, UL), (L, UH))):
                                    for h in range(2):
                                        mm = pe.matmul(PS[:, 2 * pos + h, :], w[:, k, f * P:(f + 1) * P],
                                                       u[:, 4 * pos + k, h * HALF:(h + 1) * HALF],
                                                       start=(k == 0 and j == 0), stop=(k == 3 and j == 2))
                            mm.then_inc(self.full.sem, 1)
                    for pos in range(2):
                        pe.drain().then_inc(w_free[pos], 1)

            def scalar(self, act):
                with loop(act, 4) as i:
                    for s in range(2):
                        act.wait_ge(*self.sum(i * 2 + (s + 1)))
                        for j in range(2):
                            act.dma_start(sc((2 * s + j) * T, T), zgate[bass.ds(i * 256 + (s * P + j * D), P), :])\
                               .then_inc(self.loaded[s].sem, 16)

            def vector(self, dve):
                dve.sem_inc(self.free.sem, 2)
                dve.sem_inc(self.sum.sem, 2)
                with loop(dve, 4) as i:
                    for s in range(2):
                        dve.wait_ge(*self.loaded[s](i * 32 + 32))
                        ga, gb = sc(2 * s * T, T), sc((2 * s + 1) * T, T)
                        for j, g in enumerate((ga, gb)):
                            dve.wait_ge(*self.full(i * 4 + (2 * s + j + 1)))
                            dve.tensor_tensor(g, pair(j), g, ALU.mult).then_inc(self.free.sem, 1)
                        dve.wait_ge(*self.free(i * 4 + (2 * s + 4)))
                        dve.tensor_tensor(XTf[:, bass.ds(i * (2 * T) + s * T, T)], ga, gb, ALU.add).then_inc(self.sum.sem, 1)

        class TurnOut(Stage):
            def setup(self):
                self.full, self.free = self.count("full", 0), self.count("free", 0)
                self.st = [self.count(f"st{j}", 0) for j in range(4)]

            def tensor(self, pe):
                for b in range(NBLK):
                    if b >= 2:
                        pe.wait_ge(*self.free(b - 1))
                    for k in range(KT):
                        tr = pe.transpose(pair(b % 2)[:, k * P:(k + 1) * P], XT[:, k, b * P:(b + 1) * P], ident[:])
                    tr.then_inc(self.full.sem, 1)

            def scalar(self, act):
                for b in range(NBLK):
                    act.wait_ge(*self.full(b + 1))
                    if b >= 4:
                        act.wait_ge(*self.st[b % 4](16))
                    act.activation(sc((b % 4) * T, T), pair(b % 2), ACT.Copy).then_inc(self.free.sem, 1)
                    act.wait_ge(*self.free(b + 1))
                    act.dma_start(out[b * P:(b + 1) * P, :], sc((b % 4) * T, T)).then_inc(self.st[b % 4].sem, 16)
                for j in range(4):
                    act.wait_ge(*self.st[j](32))

        pid, battn = ACT.Identity, PCOL["b_attn"][1]

        def attn_bias(i, f):
            return prm[:, 0, bass.ds(i * 2 + (battn + f), 1)]

        def copy(scale=1.0):
            return finish_with(ACT.Copy, scale=scale)

        def window_keys(b):
            return (0, 1, [(0, 1)]) if b == 0 else (b - 1, 2, [(0, 0), (1, 1)])

        def window_loads(sp, h, s, st):
            kv = h // 4
            sp.dma_start(st.Q[s][0:64, :], aq1[bass.ds(h * 64, 64), :]).then_inc(st.loaded[s].sem, 16)
            sp.dma_start(st.K[s][0:64, :], ak1[bass.ds(kv * 64, 64), :]).then_inc(st.loaded[s].sem, 16)
            sp.dma_start(st.V[s].rearrange("p (b n) -> p b n", n=64),
                         v1.rearrange("(b p) n -> p b n", p=P)[:, :, bass.ds(kv * 64 + 512, 64)]).then_inc(st.loaded[s].sem, 16)

        def fox_loads(sp, h, s, st):
            q, k, ld = st.Q[s], st.K[s], st.loaded[s]
            sp.dma_start(q[0:64, :], zpqk[bass.ds(h * 64 + 512, 64), :]).then_inc(ld.sem, 16)
            sp.dma_start(q[64:65, :], fc[bass.ds(h, 1), :]).then_inc(ld.sem, 16)
            sp.dma_start(q[65:66, :], onesd[:, :]).then_inc(ld.sem, 16)
            sp.dma_start(k[0:64, :], zpqk[bass.ds(h * 64 + 1024, 64), :]).then_inc(ld.sem, 16)
            sp.dma_start(k[64:65, :], onesd[:, :]).then_inc(ld.sem, 16)
            sp.dma_start(k[65:66, :], fnc[bass.ds(h, 1), :]).then_inc(ld.sem, 16)
            sp.dma_start(st.V[s].rearrange("p (b n) -> p b n", n=64),
                         v2.rearrange("(b p) n -> p b n", p=P)[:, :, bass.ds(h * 64, 64)]).then_inc(ld.sem, 16)

        def mem_loads(sp, h, s, st):
            sp.dma_start(st.Q[s], xq[bass.ds(h * P, P), :]).then_inc(st.loaded[s].sem, 16)
            sp.dma_start(st.K[s][:, 0:MEM], mk[bass.ds(h * P, P), :]).then_inc(st.loaded[s].sem, 16)
            sp.dma_start(st.V[s][:, 0:256].rearrange("p (b n) -> p b n", n=P),
                         mv.rearrange("(b p) n -> p b n", p=P)[:, :, bass.ds(h * P, P)]).then_inc(st.loaded[s].sem, 16)

        memT = XTf[:, 4096:6144].rearrange("p (k t) -> p k t", k=KT)
        Setup("setup")
        SetupBound("bound")
        turn = TurnIn("turn_mem", a["mem_2"].rearrange("o t n -> (o t) n"), memT, MEM)
        norm = Norm("norm_mem", "mem_g_2", "split", src=memT, n=MEM)
        Project("mem_k", [("mem_k", [(copy(), rows_at(mk, 0, 0), 2), (copy(), rows_at(mk, 256, 0), 2)])], ntok=MEM, norm_before=norm)
        ProjectTokens("mem_v", mv, [("mem_v", 0, 0, CH, 0, False), ("mem_v", 1, 0, CH, 256, False)], ntt=2)
        TurnIn("turn_x", a["x"].rearrange("o t n -> (o t) n"), XT, T)
        norm = Norm("norm_mix", "norm_mix_w", "split", store=True)
        Project("in1", [("in1_gates", [(finish_with(ACT.Sigmoid), rows_at(zf1, 0, CH), 2), (finish_with(ACT.Silu), rows_at(zg1, 0, CH), 2)]),
                        ("in1_q", [(copy(HG_SCALE), rows_at(zq1, 0, CH), 2), (finish_with(pid, attn_bias), rows_at(aq1, 0, CH), 2)])],
                norm_before=norm)
        ProjectTokens("in1_v", v1, [("in1_v", 0, 0, CH, 0, False), ("in1_v", 1, 0, CH, 256, False), ("in1_v", 2, P, P, 512, True)],
                      key=("in1_v", 2, ak1, pc("b_attn", 4)))
        window = Attend("window", 8, 64, 64, 0.125, window_keys, window_loads, 3, sinks=True)
        TurnHeads("turn_window", window.O, 4)
        hgrn = HGRN("hgrn")
        product = OutProduct("out1", "out1", 2, KT, True)
        norm = Norm("norm_ffn1", "norm_ffn_w", "split", before=product, fused=True)
        ffn = FFN("ffn1", "ffn1", False, norm)
        final = Norm("final", "final_norm_w", "inplace", before=ffn, fused=True)
        norm = Norm("norm_mix2", "mix_pre_g_2", "split", before=final, store=True)
        Project("in2", [("in2_pqk", [(copy(), rows_at(zpqk, 0, 512), 2), (copy(), rows_at(zpqk, 256, 512), 2)]),
                        ("in2_gates", [(finish_with(ACT.Sigmoid), rows_at(zgate, 0, 512), 2), (finish_with(ACT.Sigmoid), rows_at(zgate, 256, 512), 2)])],
                norm_before=norm)
        ProjectTokens("in2_v", v2, [("in2_v", 0, 0, CH, 0, False), ("in2_v", 1, 0, CH, 256, False)])
        Forget("forget")
        fox = Attend("fox", 8, 66, 64, 0.125, lambda b: (0, b + 1, [(b, 1)]), fox_loads, 7)
        TurnHeads("turn_fox", fox.O, 4)
        Pooling("pooling")
        Branches("branches")
        Split("split_merged")
        product = OutProduct("mix", "mix", 2, KT, False)
        post = Norm("post_mix", "mix_post_g_2", "post", before=product, fused=True)
        norm = Norm("norm_xa", "xa_pre_g_2", "split", before=post, store=True)
        Project("xq", [("xq", [(copy(), rows_at(xq, 0, 0), 2), (copy(), rows_at(xq, 256, 0), 2)])], norm_before=norm)
        memory = Attend("memory", 4, P, P, P ** -0.5, lambda b: (0, 2, []), mem_loads, 3)
        TurnHeads("turn_memory", memory.O, 0)
        product = OutProduct("xo", "xo", 4, 4, False)
        post = Norm("post_xa", "xa_post_g_2", "post", before=product, fused=True)
        norm = Norm("norm_ffn2", "ffn_pre_g_2", "split", before=post, store=True)
        ffn = FFN("ffn2", "ffn2", True, norm)
        Norm("post_ffn", "ffn_post_g_2", "post", before=ffn, fused=True)
        TurnOut("turn_out")

        groups = [["mem_k", "mem_v", "in1_gates", "in1_q", "in1_v"], window, hgrn,
                  ["out1", "ffn1_head", "ffn1", "ffn1_tail", "in2_pqk", "in2_gates", "in2_v", "in2_f"], fox,
                  ["branches", "mix", "xq"], memory, ["xo", "ffn2_head", "ffn2", "ffn2_tail"]]
        assert [g for group in groups if isinstance(group, list) for g in group] == list(segments)

        block = ctx.enter_context(nc.Block())

        @block.sync
        def _(sp):
            for group in groups:
                if isinstance(group, Stage):
                    group.sync(sp)
                    continue
                for seg in group:
                    iters, chunks = segments[seg]

                    def body(i):
                        seen = set()
                        for slot, src in chunks:
                            for other in ((0, 2) if slot != 1 else (1,)):
                                used = bases[seg][other] + ((1 if other in seen else 0) if other in [c[0] for c in chunks] else 0)
                                if other in [c[0] for c in chunks]:
                                    sp.wait_ge(w_ready[other], i + (used + 1))
                                    apart(sp)
                                else:
                                    sp.wait_ge(w_ready[other], used + 1)
                            ap = src(i)
                            k, n = ap.shape[1], ap.shape[2]
                            sp.dma_start(raw[slot % 2][:, 0:k * n].rearrange("p (k n) -> p k n", k=k), ap)\
                              .then_inc(raw_loaded[slot], 16)
                            seen.add(slot)
                    iterate(sp, iters, body)

        @block.gpsimd
        def _(pool):
            n = 0

            def const(ins):
                ins.then_inc(consts_ready, 1)

            prow = XTf[:, 0:512]
            const(pool.memset(prow, 0.0))
            for s in range(3):
                pool.sem_inc(w_ready[s], 1)
            const(pool.memset(ident[:], 0.0))
            const(pool.memset(ones[:], 1.0))
            const(pool.memset(bmask[:].rearrange("p a n -> p (a n)"), 0.0))
            const(pool.memset(eps, EPS))
            for t in range(16):
                const(pool.memset(invt[:, t:t + 1], 1.0 / (t + 1)))
            const(pool.iota(SC[:, 0:P].bitcast(I32), pattern=[[0, P]], base=0, channel_multiplier=1))
            const(pool.iota(SC[:, P:2 * P].bitcast(I32), pattern=[[1, P]], base=0, channel_multiplier=0))
            pool.wait_ge(consts_ready, 23)
            const(pool.affine_select(out=ident[:], in_=ident[:], compare_op=ALU.not_equal, fill=1.0, base=0,
                                     pattern=[[-1, P]], channel_multiplier=1))
            const(pool.affine_select(out=bmask[:, 0, :], in_=bmask[:, 0, :], compare_op=ALU.is_gt, fill=NEG, base=0,
                                     pattern=[[1, P]], channel_multiplier=-1))
            const(pool.affine_select(out=bmask[:, 1, :], in_=bmask[:, 1, :], compare_op=ALU.is_ge, fill=NEG, base=0,
                                     pattern=[[-1, P]], channel_multiplier=1))
            pool.wait_ge(consts_ready, 26)
            const(pool.tensor_copy(identb[:], ident[:]))
            for seg, (iters, chunks) in segments.items():
                def body(i):
                    for pos, (slot, src) in enumerate(chunks):
                        ap = src(i)
                        m = ap.shape[1] * ap.shape[2]
                        u = use(seg, pos, i)
                        pool.wait_ge(raw_loaded[slot], u * 16 + 16)
                        pool.wait_ge(w_free[slot], u + 1)
                        apart(pool)
                        pool.tensor_copy(wh[slot][:, 0:m], raw[slot % 2][:, 0:m]).then_inc(hi_done[slot], 1)
                        pool.wait_ge(hi_done[slot], u + 1)
                        pool.tensor_tensor(wl[slot][:, 0:m], raw[slot % 2][:, 0:m], wh[slot][:, 0:m].bitcast(F32),
                                           ALU.subtract).then_inc(w_ready[slot], 1)
                iterate(pool, iters, body)

        def run(e, method, own):
            for stage in stages:
                stage.after(e)
                part = {"tensor": stage.tensor, "scalar": stage.scalar, "vector": stage.vector}[method]
                part(e)
                e.drain().then_inc(own, 1)

        @block.tensor
        def _(pe):
            run(pe, "tensor", pe_stage)

        @block.scalar
        def _(act):
            run(act, "scalar", act_stage)

        @block.vector
        def _(dve):
            run(dve, "vector", dve_stage)


def kernel(**inputs):
    import numpy as np
    import concourse.bacc as bacc
    from concourse.bass_utils import run_bass_kernel_spmd

    nc = bacc.Bacc("TRN2", target_bir_lowering=False, num_devices=1)
    arrays, aps = {}, {}
    for name, value in inputs.items():
        v = np.ascontiguousarray(value)
        arrays["in_" + name] = v
        aps[name] = nc.dram_tensor("in_" + name, v.shape, mybir.dt.from_np(v.dtype), kind="ExternalInput").ap()
    out = nc.dram_tensor("out", (1, T, D), F32, kind="ExternalOutput").ap()
    program(nc, aps, out.rearrange("o t n -> (o t) n"))
    r = run_bass_kernel_spmd(nc, [arrays], core_ids=[0])
    return r.results[0]["out"]
```

```python
from contextlib import ExitStack

import concourse.bass as bass
from concourse import mybir

F32 = mybir.dt.float32
F32R = mybir.dt.float32r
BF16 = mybir.dt.bfloat16
I32 = mybir.dt.int32
U8 = mybir.dt.uint8
ALU = mybir.AluOpType
ACT = mybir.ActivationFunctionType
AX = mybir.AxisListType

P = 128
T = 1024
D = 1024
KT = D // P
HALF = 512
CH = 256
DFF = 2816
FG = DFF // CH
NBLK = T // P
MEM = 256
EPS = 1e-6
NEG = -1e30
HG = 4
LEVELS = 7
HG_SCALE = 128 ** -0.5

PARAM_ROWS = [
    [("norm_mix_w", 8), ("norm_ffn_w", 8), ("final_norm_w", 8), ("mix_pre_g_2", 8), ("mix_post_g_2", 8),
     ("xa_pre_g_2", 8), ("xa_post_g_2", 8), ("mem_g_2", 8), ("ffn_pre_g_2", 8), ("ffn_post_g_2", 8),
     ("pool_scale_2", 4), ("lb_logits", 8), ("hg_norm_w", 1), ("b_attn", 5)],
    [("conv_w", 66), ("conv_b", 22)],
    [("conv_w_2a", 88)],
    [("conv_w_2b", 44), ("conv_b_2", 44)],
]
PCOL = {}
for _t, _rows in enumerate(PARAM_ROWS):
    _at = 0
    for _name, _n in _rows:
        PCOL[_name] = (_t, _at, _n)
        _at += _n
N_CONSTS = 27
N_PARAM_DMAS = sum(len(r) for r in PARAM_ROWS)


def weight_segments(a):
    def tiles(w):
        return w.rearrange("o (k p) n -> p (o k) n", p=P)

    w_in, w_out, w_gate, w_up = (tiles(a[n]) for n in ("w_in", "w_out", "w_gate", "w_up"))
    w_down, w_in2, w_up2, w_down2 = (tiles(a[n]) for n in ("w_down", "w_in_2", "w_up_2", "w_down_2"))
    w_pool, w_fox, w_mix = (tiles(a[n]) for n in ("w_pool_br_2", "w_fox_br_2", "w_mix_out_2"))
    w_xq, w_xkv, w_xo = (tiles(a[n]) for n in ("w_xq_2", "w_xkv_2", "w_xo_2"))

    def cols(w, base, step, n=CH):
        return lambda i: w[:, :, bass.ds(i * step + base, n)]

    def rows(w, base):
        return lambda i: w[:, bass.ds(i * 2 + base, 2), :]

    return {
        "mem_k": (1, [(0, cols(w_xkv, 0, 0)), (1, cols(w_xkv, 256, 0))]),
        "mem_v": (1, [(2, cols(w_xkv, 512, 0)), (1, cols(w_xkv, 768, 0))]),
        "in1_gates": (2, [(0, cols(w_in, 512, CH)), (1, cols(w_in, 1536, CH))]),
        "in1_q": (2, [(0, cols(w_in, 0, CH)), (1, cols(w_in, 2048, CH))]),
        "in1_v": (1, [(2, cols(w_in, 1024, 0)), (0, cols(w_in, 2560, 0)), (1, cols(w_in, 1280, 0))]),
        "out1": (2, [(0, cols(w_out, 0, 512)), (1, cols(w_out, 256, 512))]),
        "ffn1_head": (1, [(0, cols(w_gate, 0, 0)), (1, cols(w_up, 0, 0))]),
        "ffn1": (FG - 1, [(0, cols(w_gate, CH, CH)), (2, rows(w_down, 0)), (1, cols(w_up, CH, CH))]),
        "ffn1_tail": (1, [(2, rows(w_down, 2 * (FG - 1)))]),
        "in2_pqk": (3, [(0, cols(w_in2, 0, 512)), (1, cols(w_in2, 256, 512))]),
        "in2_gates": (4, [(0, cols(w_in2, 2056, 512)), (1, cols(w_in2, 2312, 512))]),
        "in2_v": (1, [(2, cols(w_in2, 1536, 0)), (0, cols(w_in2, 1792, 0))]),
        "in2_f": (1, [(1, cols(w_in2, 2048, 0, P))]),
        "branches": (2, [(0, cols(w_pool, 0, 512, 512)), (1, cols(w_fox, 0, 512, 512))]),
        "mix": (2, [(0, cols(w_mix, 0, 512)), (1, cols(w_mix, 256, 512))]),
        "xq": (1, [(0, cols(w_xq, 0, 0)), (1, cols(w_xq, 256, 0))]),
        "xo": (1, [(0, cols(w_xo, 0, 0, 512)), (1, cols(w_xo, 512, 0, 512))]),
        "ffn2_head": (1, [(0, cols(w_up2, 0, 0)), (1, cols(w_up2, DFF, 0))]),
        "ffn2": (FG - 1, [(0, cols(w_up2, CH, CH)), (2, rows(w_down2, 0)), (1, cols(w_up2, DFF + CH, CH))]),
        "ffn2_tail": (1, [(2, rows(w_down2, 2 * (FG - 1)))]),
    }


def segment_bases(segments):
    used, out = [0, 0, 0], {}
    for name, (iters, chunks) in segments.items():
        out[name] = list(used)
        for slot, _ in chunks:
            used[slot] += iters
    return out


def program(nc, a, out):
    segments = weight_segments(a)
    bases = segment_bases(segments)

    def use(name, pos, i):
        slot = segments[name][1][pos][0]
        assert [s for s, _ in segments[name][1]].count(slot) == 1
        return bases[name][slot] + i

    def loop(e, n):
        return nc.Fori(0, n, engines=(e.engine,), hint_back_edge=True)

    def iterate(e, n, body):
        if n == 1:
            body(0)
        else:
            with loop(e, n) as i:
                body(i)

    with ExitStack() as ctx:
        def sb(name, shape, dt=F32):
            return ctx.enter_context(nc.sbuf_tensor(name, shape, dt))

        def sem(name):
            return ctx.enter_context(nc.semaphore(name))

        def dram(name, shape):
            return nc.dram_tensor(name, shape, F32, kind="Internal").ap()

        XT = sb("XT", [P, KT, T])
        UH = sb("UH", [P, KT, T], F32R)
        UL = sb("UL", [P, KT, T], F32R)
        raw = [sb(f"raw{s}", [P, 2048]) for s in range(2)]
        wh = [sb(f"wh{s}", [P, 2048], F32R) for s in range(3)]
        wl = [sb(f"wl{s}", [P, 2048], F32R) for s in range(3)]
        SC = sb("SC", [P, 6144])
        aH = sb("aH", [P, 2, T], F32R)
        aL = sb("aL", [P, 2, T], F32R)
        prm = sb("prm", [P, 4, P])
        ident = sb("ident", [P, P])
        ones = sb("ones", [P, P])
        bmask = sb("bmask", [P, 3, P], BF16)
        identb = sb("identb", [P, P], BF16)
        lvl = sb("lvl", [P, LEVELS, P], U8)
        small = sb("small", [P, 104])
        eps = small[:, 0:1]
        nsink = small[:, 8:16]
        lb = small[:, 16:20]
        omlb = small[:, 20:24]
        psink = small[:, 76:84]
        binv = small[:, 72:73]
        invt = small[:, 84:100]
        sm = small[:, 24:64]
        XTf = XT[:].rearrange("p k t -> p (k t)")
        PS = ctx.enter_context(nc.psum_tensor("PS", [P, 8, HALF], F32))

        def pair(n):
            return PS[:, 2 * n:2 * n + 2, :].rearrange("p b n -> p (b n)")

        def sc(at, n):
            return SC[:, at:at + n]

        def pc(name, j=0):
            t, at, _ = PCOL[name]
            return prm[:, t, at + j:at + j + 1]

        xres = dram("xres", (D, T))
        zq1 = dram("zq1", (HG * P, T))
        zf1 = dram("zf1", (HG * P, T))
        zg1 = dram("zg1", (HG * P, T))
        aq1 = dram("aq1", (512, T))
        ak1 = dram("ak1", (128, T))
        v1 = dram("v1", (T, 640 + 128))
        zpqk = dram("zpqk", (1536, T))
        zgate = dram("zgate", (2048, T))
        fc = dram("fc", (8, T))
        fnc = dram("fnc", (8, T))
        onesd = dram("onesd", (1, T))
        v2 = dram("v2", (T, 512))
        mk = dram("mk", (512, MEM))
        mv = dram("mv", (MEM, 512))
        xq = dram("xq", (512, T))

        raw_loaded = [sem(f"raw_loaded{s}") for s in range(3)]
        hi_done = [sem(f"hi_done{s}") for s in range(3)]
        w_ready = [sem(f"w_ready{s}") for s in range(3)]
        w_free = [sem(f"w_free{s}") for s in range(3)]
        pe_stage, act_stage, dve_stage = sem("pe_stage"), sem("act_stage"), sem("dve_stage")
        consts_ready = sem("consts_ready")
        passed = {e.engine: sem(f"passed_{n}") for n, e in (("act", nc.scalar), ("dve", nc.vector), ("pool", nc.gpsimd), ("sp", nc.sync))}

        shared = {}

        class Count:
            def __init__(self, semaphore, base):
                self.sem, self.base = semaphore, base

            def __call__(self, value):
                return self.sem, self.base + value

        stages = []

        class Stage:
            def __init__(self, name):
                self.name = name
                self.index = len(stages) + 1
                stages.append(self)
                self.setup()

            def count(self, what, total):
                name = f"{type(self).__name__.lower()}_{what}"
                if name not in shared:
                    shared[name] = [sem(name), 0]
                semaphore, base = shared[name]
                shared[name][1] += total
                return Count(semaphore, base)

            def setup(self): pass
            def ready(self, k): return None
            def tensor(self, pe): pass
            def scalar(self, act): pass
            def vector(self, dve): pass

            follows = False

            def after(self, e, back=1):
                if self.index > back and not self.follows:
                    e.wait_ge(pe_stage, self.index - back)
                    e.wait_ge(act_stage, self.index - back)
                    e.wait_ge(dve_stage, self.index - back)


        def apart(e):
            e.sem_inc(passed[e.engine], 1)

        def warm_up(pe, n):
            for _ in range(n):
                pe.matmul(PS[:, 7, 0:3 * P], identb[:], bmask[:].rearrange("p a n -> p (a n)"), start=True, stop=True)

        def rotated(e, iters, per, parts):
            depth = max(lag for lag, _ in parts)

            def step(i, t, last=False):
                for lag, part in parts:
                    if 0 <= t - lag < per:
                        part(i, t - lag)
                    elif t - lag >= per and not last:
                        part(i + 1, t - lag - per)
            for t in range(depth):
                step(0, t)
            if iters > 2:
                with loop(e, iters - 1) as i:
                    for t in range(depth, per + depth):
                        step(i, t)
            else:
                for t in range(depth, per + depth):
                    step(0, t)
            for t in range(depth, per + depth):
                step(iters - 1, t, last=True)

        def feature_tiles(pe, seg, pos, i, full, free, n, kt=KT, ntok=T, nf=2, u0=0, u_ready=None):
            slot = segments[seg][1][pos][0]
            width = nf * P
            pe.wait_ge(w_ready[slot], use(seg, pos, i) + 2)
            H = wh[slot][:, 0:kt * width].rearrange("p (k n) -> p k n", k=kt)
            L = wl[slot][:, 0:kt * width].rearrange("p (k n) -> p k n", k=kt)
            step = min(ntok, HALF)

            def product(f, k, b):
                for j, (w, u) in enumerate(((H, UH), (H, UL), (L, UH))):
                    for h in range(ntok // step):
                        mm = pe.matmul(pair(b)[:, h * step:(h + 1) * step], w[:, k, f * P:f * P + P],
                                       u[:, u0 + k, h * step:(h + 1) * step],
                                       start=(k == 0 and j == 0), stop=(k == kt - 1 and j == 2))
                if k == kt - 1:
                    mm.then_inc(full.sem, 1)

            if nf == 2:
                pe.wait_ge(*free(n + 2))
                for k in range(kt):
                    if u_ready is not None:
                        pe.wait_ge(*u_ready(k + 1))
                    for f in range(2):
                        product(f, k, 2 * pos + f)
            else:
                for f in range(nf):
                    pe.wait_ge(*free(n + f + 1))
                    for k in range(kt):
                        product(f, k, f % 2)
            pe.drain().then_inc(w_free[slot], 1)

        def token_tiles(pe, seg, pos, full, free, n, ntt, bias_row=None, width=CH, c0=0):
            slot = segments[seg][1][pos][0]
            pe.wait_ge(w_ready[slot], use(seg, pos, 0) + 2)
            H = wh[slot][:].rearrange("p (k n) -> p k n", k=KT)
            L = wl[slot][:].rearrange("p (k n) -> p k n", k=KT)
            for t in range(ntt):
                pe.wait_ge(*free(n + t + 1))
                ps = PS[:, 4 + (n + t) % 4, 0:width]
                for k in range(KT):
                    for j, (w, u) in enumerate(((H, UH), (L, UH), (H, UL))):
                        mm = pe.matmul(ps, u[:, k, t * P:(t + 1) * P], w[:, k, c0:c0 + width],
                                  start=(k == 0 and j == 0),
                                  stop=(k == KT - 1 and j == 2 and bias_row is None))
                if bias_row is not None:
                    mm = pe.matmul(ps, ones[0:1, :], bias_row, start=False, stop=True)
                mm.then_inc(full.sem, 1)

        def free_slot(pe, seg, pos):
            pe.drain().then_inc(w_free[segments[seg][1][pos][0]], 1)


        class Setup(Stage):
            def setup(self):
                self.prm_loaded, self.p_full, self.v = self.count("prm_loaded", 0), self.count("p_full", 1), self.count("v", 0)

            def scalar(self, act):
                prow = XTf[:, 0:512].rearrange("p (t n) -> p t n", t=4)
                act.wait_ge(consts_ready, 1)
                for t, names in enumerate(PARAM_ROWS):
                    for name, n in names:
                        _, at, _ = PCOL[name]
                        if name == "conv_w_2a":
                            src = a["conv_w_2"].rearrange("o c (m p) -> (o c m) p", p=P)[0:88]
                        elif name == "conv_w_2b":
                            src = a["conv_w_2"].rearrange("o c (m p) -> (o c m) p", p=P)[88:132]
                        elif name == "conv_w":
                            src = a[name].rearrange("o c (m p) -> (o c m) p", p=P)
                        elif len(a[name].shape) == 1:
                            src = a[name].rearrange("(m p) -> m p", p=P)
                        else:
                            src = a[name].rearrange("o (m p) -> (o m) p", p=P)[0:n]
                        act.dma_start(prow[at:at + n, t, :], src).then_inc(self.prm_loaded.sem, 16)
                act.dma_start(small[0:1, 64:72], a["sinks"]).then_inc(self.prm_loaded.sem, 16)
                act.dma_start(small[0:8, 72:73], a["b_forget_2"].rearrange("o n -> n o")).then_inc(self.prm_loaded.sem, 16)

            def tensor(self, pe):
                for s in range(3):
                    pe.sem_inc(w_free[s], 1)
                pe.wait_ge(consts_ready, N_CONSTS)
                pe.wait_ge(*self.prm_loaded(16 * (N_PARAM_DMAS + 2)))
                for t in range(4):
                    pe.transpose(PS[:, 6, t * P:(t + 1) * P], XTf[:, t * P:(t + 1) * P], ident[:])
                pe.matmul(PS[:, 7, 0:8], ones[0:1, :], small[0:1, 64:72], start=True, stop=True).then_inc(self.p_full.sem, 1)

            def vector(self, dve):
                n = [0]

                def done(ins):
                    n[0] += 1
                    ins.then_inc(self.v.sem, 1)
                    dve.wait_ge(*self.v(n[0]))

                dve.wait_ge(consts_ready, N_CONSTS)
                si, ti = SC[:, 0:P].bitcast(I32), SC[:, P:2 * P].bitcast(I32)
                xi, xf, tri, lm = SC[:, 2 * P:3 * P].bitcast(I32), sc(3 * P, P), sc(4 * P, P), sc(5 * P, P)
                done(dve.tensor_tensor(xi, si, ti, ALU.bitwise_xor))
                done(dve.tensor_copy(xf, xi))
                done(dve.tensor_tensor(tri, ti, si, ALU.is_gt))
                done(dve.tensor_tensor(xf, xf, tri, ALU.mult))
                for l in range(LEVELS):
                    m = float(1 << l)
                    done(dve.tensor_scalar(tri, xf, m, None, ALU.is_ge))
                    done(dve.scalar_tensor_tensor(out=lm, in0=xf, scalar=2 * m, in1=tri, op0=ALU.is_lt, op1=ALU.mult))
                    done(dve.tensor_copy(lvl[:, l, :], lm))
                dve.wait_ge(*self.p_full(1))
                done(dve.tensor_copy(prm[:].rearrange("p t n -> p (t n)"), PS[:, 6, :]))
                done(dve.tensor_scalar(nsink, PS[:, 7, 0:8], -1.0, None, ALU.mult))
                done(dve.tensor_scalar(psink, PS[:, 7, 0:8], 1.0, None, ALU.mult))
                _, at, _ = PCOL["lb_logits"]
                l0, l1 = prm[:, 0, at:at + 4], prm[:, 0, at + 4:at + 8]
                done(dve.tensor_tensor(sm[:, 0:4], l0, l1, ALU.max))
                done(dve.tensor_tensor(sm[:, 4:8], l0, sm[:, 0:4], ALU.subtract))
                done(dve.tensor_tensor(sm[:, 8:12], l1, sm[:, 0:4], ALU.subtract))

        class TurnIn(Stage):
            def __init__(self, name, src, dst, n):
                self.src, self.dst, self.n = src, dst, n
                super().__init__(name)

            def setup(self):
                self.parts = self.n // (2 * P)
                self.full, self.free = self.count("full", self.parts * KT // 2), self.count("free", self.parts * KT // 2)
                self.loaded = [self.count(f"loaded{j}", 16 * len(range(j, self.parts, 3))) for j in range(3)]

            def buffer(self, h):
                at = (4 * T, 0, 2 * T)[h % 3]
                return sc(at, 2 * D).rearrange("p (b n) -> p b n", b=2)

            def load(self, e, h):
                rows = self.src.rearrange("(h b p) n -> h p b n", p=P, b=2)
                e.dma_start(self.buffer(h), rows[h]).then_inc(self.loaded[h % 3].sem, 16)

            def preload(self, act):
                for h in range(min(3, self.parts)):
                    self.load(act, h)
                self.preloaded = True

            preloaded = False

            def scalar(self, act):
                if not self.preloaded:
                    for h in range(min(3, self.parts)):
                        self.load(act, h)
                for h in range(self.parts):
                    for k2 in range(KT // 2):
                        n = h * (KT // 2) + k2
                        act.wait_ge(*self.full(n + 1))
                        act.activation(self.dst[:, 2 * k2:2 * k2 + 2, h * 2 * P:(h + 1) * 2 * P],
                                       PS[:, n % 2, :].rearrange("p (k t) -> p k t", k=2), ACT.Copy).then_inc(self.free.sem, 1)
                    if h + 3 < self.parts:
                        self.load(act, h + 3)

            def ready(self, k):
                return self.free((self.parts - 1) * (KT // 2) + k // 2 + 1)

            def tensor(self, pe):
                for h in range(self.parts):
                    pe.wait_ge(*self.loaded[h % 3](16 * (h // 3 + 1)))
                    for k2 in range(KT // 2):
                        n = h * (KT // 2) + k2
                        if n >= 2:
                            pe.wait_ge(*self.free(n - 1))
                        for k in range(2):
                            for b in range(2):
                                tr = pe.transpose(PS[:, n % 2, (2 * k + b) * P:(2 * k + b + 1) * P],
                                                  self.buffer(h)[:, b, (2 * k2 + k) * P:(2 * k2 + k + 1) * P], ident[:])
                        tr.then_inc(self.full.sem, 1)

        class SetupBound(Stage):
            def setup(self):
                self.e, self.v = self.count("e", 1), self.count("v", 4)

            def scalar(self, act):
                act.activation(sm[:, 12:20], sm[:, 4:12], ACT.Exp).then_inc(self.e.sem, 1)

            def vector(self, dve):
                dve.wait_ge(*self.e(1))
                dve.tensor_tensor(sm[:, 20:24], sm[:, 12:16], sm[:, 16:20], ALU.add).then_inc(self.v.sem, 1)
                dve.wait_ge(*self.v(1))
                dve.reciprocal(sm[:, 24:28], sm[:, 20:24]).then_inc(self.v.sem, 1)
                dve.wait_ge(*self.v(2))
                dve.tensor_tensor(lb, sm[:, 12:16], sm[:, 24:28], ALU.mult).then_inc(self.v.sem, 1)
                dve.tensor_tensor(omlb, sm[:, 16:20], sm[:, 24:28], ALU.mult).then_inc(self.v.sem, 1)


        class Norm(Stage):
            def __init__(self, name, weight, mode, src=None, n=T, store=False, before=None, fused=False):
                self.weight, self.mode, self.n, self.store = weight, mode, n, store
                self.src = XT if src is None else src
                self.before, self.fused = before, fused
                self.sums_on_pe = isinstance(before, Norm)
                self.follows = before is not None
                if before is not None and not self.sums_on_pe:
                    before.norm_after = self
                super().__init__(name)

            def setup(self):
                split = self.mode == "split"
                self.sq_ready, self.acc = self.count("sq_ready", KT), self.count("acc", 0 if self.sums_on_pe else KT - 1)
                self.sq_used = self.count("sq_used", KT if self.sums_on_pe else 1)
                self.ln, self.rstd_ready = self.count("ln", 1), self.count("rstd", 1)
                self.u_ready = self.count("u", 0 if self.mode == "inplace" else KT)
                self.hi_ready, self.lo_ready = self.count("hi", KT * split), self.count("lo", KT * split)
                self.res = self.count("res", 16 * (self.mode == "post"))
                self.xn, self.stored = self.count("xn", KT * (not split)), self.count("stored", 16 * self.store)
                n = self.n
                self.sq = [sc(0, n), sc(T, n)]
                self.lnv, self.rstd = sc(2 * T, n), sc(3 * T, n)
                self.sum = self.lnv
                self.u = [sc(4 * T, n), sc(5 * T, n)]

            def ready(self, k):
                return self.xn(k + 1)

            def scalar(self, act):
                for k in range(KT):
                    if self.mode == "post" and k == self.before.last_use[0]:
                        act.wait_ge(*self.before.last_use[1])
                        act.dma_start(UH[:].bitcast(F32), xres.rearrange("(k p) t -> p k t", p=P)).then_inc(self.res.sem, 16)
                    if self.before is not None:
                        act.wait_ge(*self.before.ready(k))
                    if k >= 2:
                        act.wait_ge(*(self.sq_used(k - 1) if self.sums_on_pe else self.acc(max(1, k - 2))))
                    act.activation(self.sq[k % 2], self.src[:, k, :], ACT.Square).then_inc(self.sq_ready.sem, 1)
                if self.store:
                    act.dma_start(xres.rearrange("(k p) t -> p k t", p=P), XT[:]).then_inc(self.stored.sem, 16)
                act.wait_ge(*self.sq_used(KT if self.sums_on_pe else 1))
                act.activation(self.lnv, pair(0)[:, 0:self.n], ACT.Ln, bias=eps, scale=1.0 / D).then_inc(self.ln.sem, 1)
                act.wait_ge(*self.ln(1))
                act.activation(self.rstd, self.lnv, ACT.Exp, scale=-0.5).then_inc(self.rstd_ready.sem, 1)
                if self.mode == "split":
                    for k in range(KT):
                        act.wait_ge(*self.u_ready(k + 1))
                        act.activation(UH[:, k, 0:self.n], self.u[k % 2], ACT.Copy).then_inc(self.hi_ready.sem, 1)
                if self.store:
                    act.wait_ge(*self.stored(16))

            def tensor(self, pe):
                step = min(self.n, HALF)
                if not self.sums_on_pe:
                    pe.wait_ge(*self.acc(KT - 1))
                    for h in range(self.n // step):
                        mm = pe.matmul(PS[:, h, 0:step], ones[:], self.sum[:, h * step:(h + 1) * step], start=True, stop=True)
                    mm.then_inc(self.sq_used.sem, 1)
                    if self.mode == "split":
                        warm_up(pe, 20)
                    return
                for k in range(KT):
                    pe.wait_ge(*self.sq_ready(k + 1))
                    for h in range(self.n // step):
                        mm = pe.matmul(PS[:, h, 0:step], ones[:], self.sq[k % 2][:, h * step:(h + 1) * step],
                                       start=k == 0, stop=k == KT - 1)
                    mm.then_inc(self.sq_used.sem, 1)
                if self.mode == "split":
                    warm_up(pe, 20)

            def accumulate(self, dve, k):
                if k == 0:
                    return
                dve.wait_ge(*self.sq_ready(k + 1))
                if k == 1:
                    dve.tensor_tensor(self.sum, self.sq[0], self.sq[1], ALU.add).then_inc(self.acc.sem, 1)
                else:
                    dve.wait_ge(*self.acc(k - 1))
                    dve.tensor_tensor(self.sum, self.sum, self.sq[k % 2], ALU.add).then_inc(self.acc.sem, 1)

            def vector(self, dve):
                if self.fused:
                    self.accumulate(dve, KT - 1)
                elif not self.sums_on_pe:
                    for k in range(KT):
                        self.accumulate(dve, k)
                dve.wait_ge(*self.rstd_ready(1))
                if self.mode == "post":
                    dve.wait_ge(*self.res(16))

                def lo(k):
                    dve.wait_ge(*self.hi_ready(k + 1))
                    dve.tensor_tensor(UL[:, k, 0:self.n], self.u[k % 2], UH[:, k, 0:self.n].bitcast(F32),
                                      ALU.subtract).then_inc(self.lo_ready.sem, 1)

                def add(k):
                    dve.wait_ge(*self.u_ready(k + 1))
                    dve.tensor_tensor(XT[:, k, :], self.u[k % 2], UH[:, k, :].bitcast(F32), ALU.add).then_inc(self.xn.sem, 1)

                for k in range(KT):
                    if self.mode == "inplace":
                        dve.scalar_tensor_tensor(out=XT[:, k, :], in0=XT[:, k, :], scalar=pc(self.weight, k), in1=self.rstd,
                                                 op0=ALU.mult, op1=ALU.mult).then_inc(self.xn.sem, 1)
                        continue
                    if k >= 2:
                        dve.wait_ge(*(self.lo_ready if self.mode == "split" else self.xn)(k - 1))
                    dve.scalar_tensor_tensor(out=self.u[k % 2], in0=self.src[:, k, :], scalar=pc(self.weight, k),
                                             in1=self.rstd, op0=ALU.mult, op1=ALU.mult).then_inc(self.u_ready.sem, 1)
                    if k >= 1:
                        (lo if self.mode == "split" else add)(k - 1)
                if self.mode != "inplace":
                    (lo if self.mode == "split" else add)(KT - 1)


        class Project(Stage):
            def __init__(self, name, loops, ntok=T, u0=0, kt=KT, norm_before=None):
                self.loops, self.ntok, self.u0, self.kt = loops, ntok, u0, kt
                self.norm_before, self.follows = norm_before, norm_before is not None
                super().__init__(name)

            def setup(self):
                n = sum(segments[seg][0] * sum(c[2] for c in chunks) for seg, chunks in self.loops)
                self.full, self.free, self.z_done = self.count("full", n), self.count("free", n + 4), self.count("z_done", n)
                self.stores = [len(range(s, n, 4)) for s in range(4)]
                self.z_stored = [self.count(f"z_stored{s}", 16 * self.stores[s] + 16) for s in range(4)]
                self.z = [sc(s * T, self.ntok) for s in range(4)]
                self.all_read = self.free(n + 4)

            def tensor(self, pe):
                n = 0
                for seg, chunks in self.loops:
                    iters = segments[seg][0]

                    def body(i):
                        for pos in range(len(chunks)):
                            nf = chunks[pos][2]
                            feature_tiles(pe, seg, pos, i, self.full, self.free, n + (i * per + pos * 2), nf=nf,
                                          ntok=self.ntok, u0=self.u0, kt=self.kt, u_ready=self.norm_before.lo_ready if self.norm_before else None)
                    per = sum(c[2] for c in chunks)
                    iterate(pe, iters, body)
                    n += iters * per

            def scalar(self, act):
                act.sem_inc(self.free.sem, 4)
                for s in range(4):
                    act.sem_inc(self.z_stored[s].sem, 16)
                n = 0
                for seg, chunks in self.loops:
                    iters = segments[seg][0]
                    per = sum(c[2] for c in chunks)
                    assert per % 4 == 0 or iters == 1

                    def body(i):
                        for pos, (finish, where, nf) in enumerate(chunks):
                            for f in range(nf):
                                t = pos * 2 + f
                                s = (n + t) % 4
                                act.wait_ge(*self.full(n + (i * per + t) + 1))
                                uses = (n + t) // 4 + i * (per // 4)
                                act.wait_ge(*self.z_stored[s](16 * uses + 16))
                                apart(act)
                                finish(act, self.z[s], pair(2 * pos + f)[:, 0:self.ntok], i, f, self.free)
                                act.drain().then_inc(self.z_done.sem, 1)
                                act.wait_ge(*self.z_done(n + (i * per + t) + 1))
                                act.dma_start(where(i, f), self.z[s]).then_inc(self.z_stored[s].sem, 16)
                    iterate(act, iters, body)
                    n += iters * per
                for s in range(4):
                    act.wait_ge(*self.z_stored[s](16 * self.stores[s] + 16))

        def finish_with(func, bias=None, scale=1.0):
            def finish(act, o, ps, i, f, free):
                kw = {"bias": bias(i, f)} if bias else {}
                act.activation(o, ps, func, scale=scale, **kw).then_inc(free.sem, 1)
            return finish

        def rows_at(z, base, step):
            return lambda i, f: z[bass.ds(i * step + (base + f * P), P), :]

        class ProjectTokens(Stage):
            def __init__(self, name, dest, jobs, project, ntt=NBLK, key=None):
                self.dest, self.jobs, self.ntt, self.key = dest, jobs, ntt, key
                self.project, self.follows = project, True
                super().__init__(name)

            def setup(self):
                n, key = len(self.jobs) * self.ntt, 1 if self.key else 0
                self.full, self.free = self.count("full", n), self.count("free", n + 4)
                self.stored = self.count("stored", 16 * (len(self.jobs) + key))
                self.kfull, self.kdone, self.brow = self.count("kfull", key), self.count("kdone", key), self.count("brow", 16 * key)

            def tensor(self, pe):
                pe.wait_ge(*self.project.all_read)
                n = 0
                for seg, pos, c0, width, where, bias in self.jobs:
                    if bias:
                        pe.wait_ge(*self.brow(16))
                    token_tiles(pe, seg, pos, self.full, self.free, n, self.ntt, width=width, c0=c0,
                                bias_row=SC[0:1, 0:P] if bias else None)
                    if self.key and self.key[0:2] == (seg, pos):
                        slot = segments[seg][1][pos][0]
                        H = wh[slot][:].rearrange("p (k n) -> p k n", k=KT)
                        L = wl[slot][:].rearrange("p (k n) -> p k n", k=KT)
                        for k in range(KT):
                            for j, (w, u) in enumerate(((H, UH), (H, UL), (L, UH))):
                                for h in range(2):
                                    pe.matmul(PS[:, h, :], w[:, k, 0:P], u[:, k, h * HALF:(h + 1) * HALF],
                                              start=(k == 0 and j == 0), stop=(k == KT - 1 and j == 2))
                        pe.drain().then_inc(self.kfull.sem, 1)
                    free_slot(pe, seg, pos)
                    n += self.ntt

            turn_after = None

            def scalar(self, act):
                if self.turn_after is not None:
                    self.turn_after.preload(act)
                if any(j[5] for j in self.jobs):
                    act.dma_start(SC[0:1, 0:P], a["b_attn"][0:1, 640:768]).then_inc(self.brow.sem, 16)
                act.sem_inc(self.free.sem, 4)
                n = 0
                for q, (seg, pos, c0, width, where, bias) in enumerate(self.jobs):
                    st = XTf[:, (q % 2) * 2048:(q % 2) * 2048 + self.ntt * width].rearrange("p (t n) -> p t n", n=width)
                    if q >= 2:
                        act.wait_ge(*self.stored(16 * q))
                    for t in range(self.ntt):
                        act.wait_ge(*self.full(n + 1))
                        act.activation(st[:, t, :], PS[:, 4 + n % 4, 0:width], ACT.Copy).then_inc(self.free.sem, 1)
                        n += 1
                    act.wait_ge(*self.free(n + 4))
                    act.dma_start(self.dest[:, where:where + width].rearrange("(t p) n -> p t n", p=P), st).then_inc(self.stored.sem, 16)
                if self.key:
                    act.wait_ge(*self.kfull(1))
                    act.activation(sc(T, T), pair(0), ACT.Identity, bias=self.key[3]).then_inc(self.kdone.sem, 1)
                    act.wait_ge(*self.kdone(1))
                    act.dma_start(self.key[2], sc(T, T)).then_inc(self.stored.sem, 16)
                act.wait_ge(*self.stored(16 * (len(self.jobs) + (1 if self.key else 0))))


        class OutProduct(Stage):
            def __init__(self, name, seg, nf, kt, residual, split_before=None):
                self.seg, self.nf, self.kt, self.residual = seg, nf, kt, residual
                self.split_before, self.follows = split_before, split_before is not None
                super().__init__(name)

            def setup(self):
                self.ahead = 4 if self.nf == 2 else 2
                self.full, self.free, self.res = self.count("full", KT), self.count("free", KT + self.ahead), self.count("res", 16 * self.residual)
                self.last_use = (KT - 2 if self.nf == 2 else KT - 1, self.full(KT))

            def ready(self, k):
                return self.free(k + 1 + self.ahead)

            def tensor(self, pe):
                iterate(pe, segments[self.seg][0], lambda i: [
                    feature_tiles(pe, self.seg, pos, i, self.full, self.free, i * (2 * self.nf) + pos * self.nf, nf=self.nf, kt=self.kt,
                                  u_ready=self.split_before.lo_ready if self.split_before else None)
                    for pos in range(2)])

            def scalar(self, act):
                if self.residual:
                    act.dma_start(XT[:], xres.rearrange("(k p) t -> p k t", p=P)).then_inc(self.res.sem, 16)

            def vector(self, dve):
                dve.sem_inc(self.free.sem, self.ahead)
                if self.residual:
                    dve.wait_ge(*self.res(16))
                for t in range(KT):
                    dve.wait_ge(*self.full(t + 1))
                    ps = pair(t % self.ahead)
                    if self.residual:
                        dve.tensor_tensor(XT[:, t, :], ps, XT[:, t, :], ALU.add).then_inc(self.free.sem, 1)
                    else:
                        dve.tensor_copy(XT[:, t, :], ps).then_inc(self.free.sem, 1)
                    if t >= 1:
                        self.norm_after.accumulate(dve, t - 1)


        class FFN(Stage):
            def __init__(self, name, seg, second, norm_before):
                self.seg, self.second = seg, second
                self.norm_before, self.follows = norm_before, True
                super().__init__(name)

            def setup(self):
                s, n = self.count, 2 * FG
                self.g_full, self.u_full, self.y_full = s("g_full", n), s("u_full", n), s("y_full", FG * KT)
                self.ps_free, self.y_free = s("ps_free", 2 * n + 2), s("y_free", FG * KT + 2)
                self.tap, self.c1, self.c2, self.gate, self.prod = s("tap", n), s("c1", n), s("c2", n), s("gate", n), s("prod", n + 1)
                self.hi, self.a_ready = s("hi", n), s("a_ready", n + 1)
                self.utap, self.u1, self.u2 = (s(x, n * self.second) for x in ("utap", "u1", "u2"))
                self.g_free, self.cleared = s("g_free", n + 2), s("cleared", 1 * self.second)
                self.last_use = (0, self.u_full(n))
                self.AH = aH[:]
                self.AL = aL[:]
                self.g = [sc(0, T), sc(T, T)]
                self.t = sc(2 * T, T)
                self.p = sc(3 * T, T)

            def ready(self, k):
                return self.y_free(2 + (FG - 1) * KT + k + 1)

            def half_group(self, pe, g, slot, full, u_ready=None):
                pe.wait_ge(w_ready[slot], g + (bases[self.seg + "_head"][slot] + 2))
                H = wh[slot][:].rearrange("p (k n) -> p k n", k=KT)
                L = wl[slot][:].rearrange("p (k n) -> p k n", k=KT)
                if u_ready is not None:
                    pe.wait_ge(*self.ps_free(2))
                    for k in range(KT):
                        pe.wait_ge(*u_ready(k + 1))
                        for f in range(2):
                            for j, (w, u) in enumerate(((H, UH), (H, UL), (L, UH))):
                                for h in range(2):
                                    mm = pe.matmul(PS[:, 2 * f + h, :], w[:, k, f * P:(f + 1) * P], u[:, k, h * HALF:(h + 1) * HALF],
                                                   start=(k == 0 and j == 0), stop=(k == KT - 1 and j == 2))
                            if k == KT - 1:
                                mm.then_inc(full.sem, 1)
                    pe.drain().then_inc(w_free[slot], 1)
                    return
                for f in range(2):
                    pe.wait_ge(*self.ps_free(g * 4 + (slot * 2 + f + 1)))
                    for k in range(KT):
                        for j, (w, u) in enumerate(((H, UH), (H, UL), (L, UH))):
                            for h in range(2):
                                mm = pe.matmul(PS[:, 2 * f + h, :], w[:, k, f * P:(f + 1) * P], u[:, k, h * HALF:(h + 1) * HALF],
                                               start=(k == 0 and j == 0), stop=(k == KT - 1 and j == 2))
                    mm.then_inc(full.sem, 1)
                pe.drain().then_inc(w_free[slot], 1)

            def down(self, pe, g):
                pe.wait_ge(w_ready[2], g + (bases[self.seg][2] + 2))
                pe.wait_ge(*self.a_ready(g * 2 + 3))
                H = wh[2][:].rearrange("p (k n) -> p k n", k=2)
                L = wl[2][:].rearrange("p (k n) -> p k n", k=2)
                for m in range(KT):
                    pe.wait_ge(*self.y_free(g * KT + (m + 1)))
                    for k in range(2):
                        for j, (w, u) in enumerate(((H, self.AH), (H, self.AL), (L, self.AH))):
                            for h in range(2):
                                mm = pe.matmul(PS[:, 4 + 2 * (m % 2) + h, :], w[:, k, m * P:(m + 1) * P],
                                               u[:, k, h * HALF:(h + 1) * HALF],
                                               start=(k == 0 and j == 0), stop=(k == 1 and j == 2))
                    mm.then_inc(self.y_full.sem, 1)
                pe.drain().then_inc(w_free[2], 1)

            def tensor(self, pe):
                self.half_group(pe, 0, 0, self.g_full, self.norm_before.lo_ready)
                self.half_group(pe, 0, 1, self.u_full)
                with loop(pe, FG - 1) as g:
                    self.half_group(pe, g + 1, 0, self.g_full)
                    self.down(pe, g)
                    self.half_group(pe, g + 1, 1, self.u_full)
                self.down(pe, FG - 1)

            def taps(self, g, f, col0):
                def col(name, base):
                    t, at, _ = PCOL[name]
                    return prm[:, t, bass.ds(g * 2 + (at + base + f + col0), 1)]
                if self.second:
                    return col("conv_w_2a", 0), col("conv_w_2a", 44), col("conv_w_2b", 0), col("conv_b_2", 0)
                return col("conv_w", 0), col("conv_w", 22), col("conv_w", 44), col("conv_b", 0)

            def scalar(self, act):
                def gates(g):
                    for f in range(2):
                        n = g * 2 + f
                        _, _, w2, b = self.taps(g, f, 0)
                        act.wait_ge(*self.g_full(n + 1))
                        act.wait_ge(*self.g_free(n + 1))
                        apart(act)
                        act.activation(self.g[f], pair(f), ACT.Identity, bias=b, scale=w2).then_inc(self.tap.sem, 1)
                        act.wait_ge(*self.c2(n + 1))
                        act.activation(self.g[f], self.g[f], ACT.Gelu_apprx_tanh if self.second else ACT.Silu).then_inc(self.gate.sem, 1)

                def ups(g):
                    for f in range(2):
                        n = g * 2 + f
                        if self.second:
                            _, _, w2, b = self.taps(g, f, 22)
                            act.wait_ge(*self.u_full(n + 1))
                            act.wait_ge(*self.prod(n + 1))
                            apart(act)
                            act.activation(self.t, pair(f), ACT.Identity, bias=b, scale=w2).then_inc(self.utap.sem, 1)
                        act.wait_ge(*self.prod(n + 2))
                        act.activation(self.AH[:, f, :], self.p, ACT.Copy).then_inc(self.hi.sem, 1)

                with loop(act, FG) as g:
                    gates(g)
                    ups(g)

            def vector(self, dve):
                dve.wait_ge(*self.norm_before.lo_ready(KT))
                dve.sem_inc(self.ps_free.sem, 2)
                dve.sem_inc(self.y_free.sem, 2)
                dve.sem_inc(self.g_free.sem, 2)
                dve.sem_inc(self.prod.sem, 1)
                dve.sem_inc(self.a_ready.sem, 1)
                if self.second:
                    dve.wait_ge(*self.norm_before.stored(16))
                    dve.memset(XTf, 0.0).then_inc(self.cleared.sem, 1)
                    dve.wait_ge(*self.cleared(1))

                def older(o, ps, w0, w1, ready, n, s1, s2, free):
                    dve.wait_ge(*ready(n + 1))
                    dve.scalar_tensor_tensor(out=o[:, 1:T], in0=ps[:, 0:T - 1], scalar=w1, in1=o[:, 1:T],
                                             op0=ALU.mult, op1=ALU.add).then_inc(s1.sem, 1)
                    dve.wait_ge(*s1(n + 1))
                    dve.scalar_tensor_tensor(out=o[:, 2:T], in0=ps[:, 0:T - 2], scalar=w0, in1=o[:, 2:T],
                                             op0=ALU.mult, op1=ALU.add).then_inc(s2.sem, 1)
                    if free is not None:
                        dve.wait_ge(*s2(n + 1))
                        dve.sem_inc(free.sem, 1)

                def gates(g):
                    for f in range(2):
                        w0, w1, _, _ = self.taps(g, f, 0)
                        older(self.g[f], pair(f), w0, w1, self.tap, g * 2 + f, self.c1, self.c2, self.ps_free)

                def ups(g):
                    for f in range(2):
                        n = g * 2 + f
                        if self.second:
                            w0, w1, _, _ = self.taps(g, f, 22)
                            older(self.t, pair(f), w0, w1, self.utap, n, self.u1, self.u2, self.ps_free)
                            up = self.t
                        else:
                            dve.wait_ge(*self.u_full(n + 1))
                            up = pair(f)
                        dve.wait_ge(*self.gate(n + 1))
                        dve.wait_ge(*self.a_ready(n + 1))
                        dve.tensor_tensor(self.p, up, self.g[f], ALU.mult).then_inc(self.prod.sem, 1)
                        dve.wait_ge(*self.prod(n + 2))
                        if not self.second:
                            dve.sem_inc(self.ps_free.sem, 1)
                        dve.sem_inc(self.g_free.sem, 1)
                        dve.wait_ge(*self.hi(n + 1))
                        dve.tensor_tensor(self.AL[:, f, :], self.p, self.AH[:, f, :].bitcast(F32), ALU.subtract).then_inc(self.a_ready.sem, 1)

                def add(g, norm=None):
                    for m in range(KT):
                        dve.wait_ge(*self.y_full(g * KT + (m + 1)))
                        dve.tensor_tensor(XT[:, m, :], pair(2 + m % 2), XT[:, m, :], ALU.add).then_inc(self.y_free.sem, 1)
                        if norm is not None and m >= 1:
                            norm.accumulate(dve, m - 1)

                gates(0)
                ups(0)
                with loop(dve, FG - 1) as g:
                    gates(g + 1)
                    add(g)
                    ups(g + 1)
                add(FG - 1, self.norm_after)

        class Split(Stage):
            def setup(self):
                self.hi, self.lo_ready = self.count("hi", KT), self.count("lo", KT)

            def scalar(self, act):
                for k in range(KT):
                    act.activation(UH[:, k, :], XT[:, k, :], ACT.Copy).then_inc(self.hi.sem, 1)

            def vector(self, dve):
                for k in range(KT):
                    dve.wait_ge(*self.hi(k + 1))
                    dve.tensor_tensor(UL[:, k, :], XT[:, k, :], UH[:, k, :].bitcast(F32), ALU.subtract).then_inc(self.lo_ready.sem, 1)


        class Attend(Stage):
            def __init__(self, name, heads, rows, dv, scale, keys, loads, n_loads, sinks=False):
                self.heads, self.rows, self.dv, self.scale = heads, rows, dv, scale
                self.keys, self.loads, self.n_loads, self.sinks = keys, loads, n_loads, sinks
                super().__init__(name)

            def setup(self):
                s, n = self.count, self.heads * NBLK
                self.loaded = [s(f"loaded{j}", 16 * self.n_loads * self.heads // 2) for j in range(2)]
                self.s_full, self.exp_done = s("s_full", n), s("exp_done", n + 2)
                self.pt_full, self.pt_copied = s("pt_full", n + 2), s("pt_copied", n + 1)
                self.o_full, self.o_free = s("o_full", n + 16), s("o_free", n + 2)
                self.m_ready, self.mx, self.den, self.inv = s("m_ready", n), s("mx", n), s("den", n * self.sinks), s("inv", n)
                self.Q = [XTf[:, 0:T], sc(5120, T)]
                self.K = [XTf[:, 1024 + 1152 * j:1024 + 1152 * j + T] for j in range(2)]
                self.V = [sc(4096 + 512 * j, 512) for j in range(2)]
                self.O = XTf[:, 3328:3328 + 4096].rearrange("p (b n) -> p b n", b=NBLK)
                self.Pb = [sc(0, T), sc(T, T)]
                self.PT = [sc(2 * T, T), sc(3 * T, T)]

            preloads = None

            def sync(self, sp):
                self.after(sp)
                with loop(sp, self.heads // 2) as i:
                    for s in range(2):
                        sp.wait_ge(*self.o_full(i * 16 + 8 * (s + 1)))
                        apart(sp)
                        self.loads(sp, i * 2 + s, s, self)
                if self.preloads is not None:
                    self.preloads.preload(sp)

            def tensor(self, pe):
                pe.sem_inc(self.pt_full.sem, 2)
                pe.sem_inc(self.o_full.sem, 16)

                def scores(i, t):
                    s, b = t // 8, t % 8
                    k0, nk, masks = self.keys(b)
                    if b == 0:
                        pe.wait_ge(*self.loaded[s](i * (16 * self.n_loads) + 16 * self.n_loads))
                    pe.wait_ge(*self.exp_done(i * 16 + (t + 1)))
                    ps = pair(t % 2)
                    last = nk * P
                    for c in range(0, last, HALF):
                        e = min(c + HALF, last)
                        inside = [m for m in masks if c <= m[0] * P < e]
                        for j, (kb, m) in enumerate(inside):
                            pe.matmul(ps[:, kb * P:(kb + 1) * P], identb[:], bmask[:, m, :], start=j == 0,
                                      stop=False, skip_group_check=True)
                        mm = pe.matmul(ps[:, c:e], self.Q[s][0:self.rows, b * P:(b + 1) * P],
                                       self.K[s][0:self.rows, k0 * P + c:k0 * P + e], start=not inside, stop=True,
                                       skip_group_check=True)
                    mm.then_inc(self.s_full.sem, 1)

                def turn(i, u):
                    nk = self.keys(u % 8)[1]
                    pe.wait_ge(*self.exp_done(i * 16 + (u + 3)))
                    pe.wait_ge(*self.pt_copied(i * 16 + (u + 1)))
                    for j in range(nk):
                        tr = pe.transpose(pair(2)[:, j * P:(j + 1) * P], self.Pb[u % 2][:, j * P:(j + 1) * P], ident[:])
                    tr.then_inc(self.pt_full.sem, 1)

                def values(i, u):
                    s, b = u // 8, u % 8
                    k0, nk, _ = self.keys(b)
                    V = self.V[s].rearrange("p (b n) -> p b n", n=self.dv)
                    pe.wait_ge(*self.pt_copied(i * 16 + (u + 2)))
                    pe.wait_ge(*self.o_free(i * 16 + (u + 1)))
                    for j in range(nk):
                        mm = pe.matmul(PS[:, 6 + u % 2, 0:self.dv], self.PT[u % 2][:, j * P:(j + 1) * P],
                                       V[:, k0 + j, :], start=j == 0, stop=j == nk - 1)
                    mm.then_inc(self.o_full.sem, 1)

                warm_up(pe, 44)
                rotated(pe, self.heads // 2, 16, [(0, scores), (2, turn), (3, values)])

            def scalar(self, act):
                act.sem_inc(self.exp_done.sem, 2)
                act.sem_inc(self.pt_copied.sem, 1)

                def probs(i, t):
                    nk = self.keys(t % 8)[1]
                    act.wait_ge(*self.m_ready(i * 16 + (t + 1)))
                    act.wait_ge(*self.pt_full(i * 16 + (t + 1)))
                    apart(act)
                    if self.sinks:
                        act.activation(sm[:, 8 + t % 4:9 + t % 4], sm[:, 4 + t % 4:5 + t % 4], ACT.Exp,
                                       bias=psink[:, bass.ds(i * 2 + t // 8, 1)])
                    act.activation(self.Pb[t % 2][:, 0:nk * P], pair(t % 2)[:, 0:nk * P], ACT.Exp,
                                   bias=sm[:, 4 + t % 4:5 + t % 4], scale=self.scale,
                                   accum_out=sm[:, 12 + t % 4:13 + t % 4]).then_inc(self.exp_done.sem, 1)

                def turned(i, u):
                    nk = self.keys(u % 8)[1]
                    act.wait_ge(*self.pt_full(i * 16 + (u + 3)))
                    act.wait_ge(*self.o_full(i * 16 + (u + 15)))
                    act.activation(self.PT[u % 2][:, 0:nk * P], pair(2)[:, 0:nk * P], ACT.Copy)\
                       .then_inc(self.pt_copied.sem, 1)

                rotated(act, self.heads // 2, 16, [(2, turned), (0, probs)])

            def vector(self, dve):
                dve.sem_inc(self.o_free.sem, 2)

                def maximum(i, t):
                    nk = self.keys(t % 8)[1]
                    dve.wait_ge(*self.s_full(i * 16 + (t + 1)))
                    dve.reduce_max(sm[:, t % 4:t % 4 + 1], pair(t % 2)[:, 0:nk * P], AX.X).then_inc(self.mx.sem, 1)
                    dve.wait_ge(*self.mx(i * 16 + (t + 1)))
                    o, x = sm[:, 4 + t % 4:5 + t % 4], sm[:, t % 4:t % 4 + 1]
                    if self.sinks:
                        dve.tensor_scalar(o, x, -self.scale, nsink[:, bass.ds(i * 2 + t // 8, 1)], ALU.mult, ALU.min)\
                           .then_inc(self.m_ready.sem, 1)
                    else:
                        dve.tensor_scalar(o, x, -self.scale, None, ALU.mult).then_inc(self.m_ready.sem, 1)

                def output(i, u):
                    s, b = u // 8, u % 8
                    j = u % 4
                    den = sm[:, 12 + j:13 + j]
                    dve.wait_ge(*self.o_full(i * 16 + (u + 17)))
                    if self.sinks:
                        dve.tensor_tensor(sm[:, 16 + j:17 + j], den, sm[:, 8 + j:9 + j], ALU.add).then_inc(self.den.sem, 1)
                        dve.wait_ge(*self.den(i * 16 + (u + 1)))
                        den = sm[:, 16 + j:17 + j]
                    dve.reciprocal(sm[:, 20 + j:21 + j], den).then_inc(self.inv.sem, 1)
                    dve.wait_ge(*self.inv(i * 16 + (u + 1)))
                    dve.tensor_scalar(self.O[:, b, bass.ds(i * (2 * self.dv) + s * self.dv, self.dv)],
                                      PS[:, 6 + u % 2, 0:self.dv], sm[:, 20 + j:21 + j], None, ALU.mult)\
                       .then_inc(self.o_free.sem, 1)

                rotated(dve, self.heads // 2, 16, [(0, maximum), (3, output)])

        class TurnHeads(Stage):
            def __init__(self, name, src, u0):
                self.src, self.u0 = src, u0
                super().__init__(name)

            def setup(self):
                self.full, self.hi, self.free = self.count("full", 4), self.count("hi", 4), self.count("free", 4)

            def tensor(self, pe):
                for k in range(4):
                    if k >= 2:
                        pe.wait_ge(*self.free(k - 1))
                    for b in range(NBLK):
                        tr = pe.transpose(pair(k % 2)[:, b * P:(b + 1) * P], self.src[:, b, k * P:(k + 1) * P], ident[:])
                    tr.then_inc(self.full.sem, 1)

            def scalar(self, act):
                for k in range(4):
                    act.wait_ge(*self.full(k + 1))
                    act.activation(UH[:, self.u0 + k, :], pair(k % 2), ACT.Copy).then_inc(self.hi.sem, 1)

            def vector(self, dve):
                for k in range(4):
                    dve.wait_ge(*self.hi(k + 1))
                    dve.tensor_tensor(UL[:, self.u0 + k, :], pair(k % 2), UH[:, self.u0 + k, :].bitcast(F32),
                                      ALU.subtract).then_inc(self.free.sem, 1)


        class HGRN(Stage):
            def setup(self):
                def s(what):
                    return self.count(what, 0)
                self.f_loaded, self.q_loaded, self.v_loaded, self.g_loaded = s("f_loaded"), s("q_loaded"), s("v_loaded"), s("g_loaded")
                self.fk, self.lnf, self.scan = s("fk"), s("lnf"), s("scan")
                self.dd, self.ex, self.mr, self.pl, self.pr = s("dd"), s("ex"), s("mr"), s("pl"), s("pr")
                self.e0, self.q0, self.de, self.ke, self.ee = s("e0"), s("q0"), s("de"), s("ke"), s("ee")
                self.tk, self.kc, self.kv, self.st, self.oo = s("tk"), s("kc"), s("kv"), s("st"), s("oo")
                self.sq, self.ss, self.l2, self.r2, self.n1, self.n2, self.hi, self.lo = (
                    s(x) for x in ("sq", "ss", "l2", "r2", "n1", "n2", "hi", "lo"))

                def x(n):
                    return XTf[:, n * T:(n + 1) * T]
                self.q, self.v, self.b, self.k, self.KE, self.KET, self.o = (x(n) for n in range(7))
                self.E = [x(7), sc(T, T)]
                self.M = [sc(5 * T, T), sc(2 * T, T)]
                self.ST, self.Q0, self.S = sc(0, T), sc(3 * T, T), sc(4 * T, T)
                self.F = self.E[1]
                self.R = self.S
                self.ends = sm[:, 0:NBLK]
                self.g, self.f = aH[:, 0, :].bitcast(F32), aH[:, 1, :].bitcast(F32)

            def heads(self, e, head, finish):
                head(0, None)
                with loop(e, HG - 1) as i:
                    head(i + 1, i)
                finish(HG - 1)

            def sync(self, sp):
                self.after(sp, back=2)
                vd = self.v.rearrange("p (c n) -> p c n", c=NBLK)
                vs = v1.rearrange("(c p) n -> p c n", p=P)

                def load(dst, src, h, loaded):
                    sp.dma_start(dst, src[bass.ds(h * P, P), :]).then_inc(loaded.sem, 16)

                load(self.f, zf1, 0, self.f_loaded)
                load(self.q, zq1, 0, self.q_loaded)
                sp.dma_start(vd, vs[:, :, 0:P]).then_inc(self.v_loaded.sem, 16)
                load(self.g, zg1, 0, self.g_loaded)
                with loop(sp, HG - 1) as i:
                    sp.wait_ge(*self.fk(i * 2 + 2))
                    apart(sp)
                    load(self.f, zf1, i + 1, self.f_loaded)
                    sp.wait_ge(*self.mr(i * LEVELS + LEVELS))
                    sp.wait_ge(*self.q0(i + 1))
                    apart(sp)
                    load(self.q, zq1, i + 1, self.q_loaded)
                    sp.wait_ge(*self.oo(i + 1))
                    apart(sp)
                    sp.dma_start(vd, vs[:, :, bass.ds(i * P + P, P)]).then_inc(self.v_loaded.sem, 16)
                    sp.wait_ge(*self.n2(i + 1))
                    apart(sp)
                    load(self.g, zg1, i + 1, self.g_loaded)

            def tensor(self, pe):
                def c(t, n):
                    return t[:, n * P:(n + 1) * P]

                def sums(h):
                    pe.wait_ge(*self.sq(h + 1))
                    for x in range(2):
                        mm = pe.matmul(PS[:, 4 + x, :], ones[:], self.o[:, x * HALF:(x + 1) * HALF], start=True, stop=True)
                    mm.then_inc(self.ss.sem, 1)

                def head(h, prior):
                    pe.wait_ge(*self.fk(h * 2 + 2))
                    pe.wait_ge(*self.q_loaded(h * 16 + 16))
                    for n in range(NBLK):
                        mm = pe.matmul(c(pair(1), n), c(self.k, n), c(self.q, n), start=True, stop=True)
                    mm.then_inc(self.pl.sem, 1)
                    if prior is not None:
                        sums(prior)
                    for l in range(LEVELS):
                        m = 64 >> l
                        pe.wait_ge(*self.mr(h * LEVELS + (l + 1)))
                        if l >= 2:
                            pe.wait_ge(*self.pr(h * 8 + l))
                        for n in range(NBLK):
                            upper = c(self.M[l % 2], n).rearrange("p (g h m) -> p g h m", h=2, m=m)[:, :, 1, :]
                            mm = pe.matmul(PS[:, l % 2, n * 64:(n + 1) * 64], c(self.M[l % 2], n), upper, start=True, stop=True)
                        mm.then_inc(self.pl.sem, 1)
                        if l == 1:
                            pe.wait_ge(*self.ke(h + 1))
                            if prior is not None:
                                pe.wait_ge(*self.l2(prior + 1))
                            for n in range(NBLK):
                                mm = pe.transpose(c(pair(2), n), c(self.KE, n), ident[:])
                            mm.then_inc(self.tk.sem, 1)
                        if l == 2:
                            pe.wait_ge(*self.kc(h + 1))
                            pe.wait_ge(*self.v_loaded(h * 16 + 16))
                            if prior is not None:
                                pe.wait_ge(*self.n1(prior + 1))
                            for n in range(NBLK):
                                mm = pe.matmul(c(pair(3), n), c(self.KET, n), c(self.v, n), start=True, stop=True)
                            mm.then_inc(self.kv.sem, 1)
                    pe.wait_ge(*self.pr(h * 8 + 8))
                    pe.wait_ge(*self.st(h * 7 + 7))
                    pe.wait_ge(*self.q0(h + 1))
                    for n in range(NBLK):
                        mm = pe.matmul(c(pair(3), n), c(self.v, n), c(self.ST, n), start=True, stop=n == 0)
                        if n:
                            mm = pe.matmul(c(pair(3), n), c(self.S, n), c(self.Q0, n), start=False, stop=True)
                    mm.then_inc(self.oo.sem, 1)

                self.heads(pe, head, sums)

            def scalar(self, act):
                def squares(h):
                    act.wait_ge(*self.oo(h + 1))
                    act.wait_ge(*self.lo(h + 1))
                    act.activation(self.o, pair(3), ACT.Square).then_inc(self.sq.sem, 1)

                def rstd(h):
                    act.wait_ge(*self.ss(h + 1))
                    act.activation(self.R, pair(2), ACT.Ln, bias=eps, scale=1.0 / P).then_inc(self.l2.sem, 1)
                    act.wait_ge(*self.l2(h + 1))
                    act.activation(self.R, self.R, ACT.Exp, scale=-0.5).then_inc(self.r2.sem, 1)

                def split(h):
                    act.wait_ge(*self.n2(h + 1))
                    apart(act)
                    act.activation(UH[:, bass.ds(h, 1), :], self.o, ACT.Copy).then_inc(self.hi.sem, 1)

                def head(h, prior):
                    def decay(l):
                        act.wait_ge(*self.dd(h * 14 + 2 * (l + 1)))
                        act.activation(self.E[l % 2], self.E[l % 2], ACT.Exp).then_inc(self.ex.sem, 1)

                    act.wait_ge(*self.fk(h * 2 + 1))
                    if prior is not None:
                        act.wait_ge(*self.mr(h * LEVELS))
                    act.activation(self.E[0], self.F, ACT.Ln).then_inc(self.lnf.sem, 1)
                    if prior is not None:
                        squares(prior)
                    decay(0)
                    act.wait_ge(*self.scan(h * 8 + 8))
                    act.activation(self.ends.rearrange("p (n t) -> p n t", t=1),
                                   self.b.rearrange("p (n t) -> p n t", n=NBLK)[:, :, P - 1:P], ACT.Exp).then_inc(self.e0.sem, 1)
                    act.activation(self.Q0, self.b, ACT.Exp).then_inc(self.e0.sem, 1)
                    act.wait_ge(*self.de(h + 1))
                    act.activation(self.KE, self.KE, ACT.Exp).then_inc(self.ee.sem, 1)
                    decay(1)
                    if prior is not None:
                        rstd(prior)
                    decay(2)
                    act.wait_ge(*self.tk(h + 1))
                    act.activation(self.KET, pair(2), ACT.Copy).then_inc(self.kc.sem, 1)
                    decay(3)
                    decay(4)
                    if prior is not None:
                        split(prior)
                    decay(5)
                    decay(6)

                def finish(h):
                    squares(h)
                    rstd(h)
                    split(h)

                self.heads(act, head, finish)

            def vector(self, dve):
                dve.sem_inc(self.lo.sem, 1)

                def halves(t, m):
                    v = t.rearrange("p (n h m) -> p n h m", h=2, m=m)
                    return v[:, :, 0, :], v[:, :, 1, :]

                def normed(h):
                    dve.wait_ge(*self.r2(h + 1))
                    dve.scalar_tensor_tensor(out=self.o, in0=pair(3), scalar=pc("hg_norm_w"), in1=self.R,
                                             op0=ALU.mult, op1=ALU.mult).then_inc(self.n1.sem, 1)

                def gated(h):
                    dve.wait_ge(*self.n1(h + 1))
                    dve.wait_ge(*self.g_loaded(h * 16 + 16))
                    dve.tensor_tensor(self.o, self.o, self.g, ALU.mult).then_inc(self.n2.sem, 1)

                def split(h):
                    dve.wait_ge(*self.hi(h + 1))
                    dve.tensor_tensor(UL[:, bass.ds(h, 1), :], self.o, UH[:, bass.ds(h, 1), :].bitcast(F32), ALU.subtract)\
                       .then_inc(self.lo.sem, 1)

                def head(h, prior):
                    def exponents(l):
                        m = 64 >> l
                        b0, b1 = halves(self.b, m)
                        e0, e1 = halves(self.E[l % 2], m)
                        ref = b0[:, :, m - 1:m].to_broadcast([P, T // (2 * m), m])
                        if l >= 2:
                            dve.wait_ge(*self.mr(h * LEVELS + (l - 1)))
                        dve.tensor_tensor(e0, ref, b0, ALU.subtract).then_inc(self.dd.sem, 1)
                        dve.tensor_tensor(e1, b1, ref, ALU.subtract).then_inc(self.dd.sem, 1)

                    def decayed(l):
                        m = 64 >> l
                        e0, e1 = halves(self.E[l % 2], m)
                        m0, m1 = halves(self.M[l % 2], m)
                        k0, _ = halves(self.k, m)
                        _, q1 = halves(self.q, m)
                        dve.wait_ge(*self.ex(h * LEVELS + (l + 1)))
                        if l >= 2:
                            dve.wait_ge(*self.pl(h * 8 + l))
                        dve.tensor_tensor(m0, k0, e0, ALU.mult)
                        dve.tensor_tensor(m1, q1, e1, ALU.mult).then_inc(self.mr.sem, 1)

                    def placed(l):
                        m = 64 >> l
                        g = P // (2 * m)
                        dve.wait_ge(*self.pl(h * 8 + (l + 2)))
                        dve.wait_ge(*self.pr(h * 8 + (l + 1)))
                        mask = lvl[:, 6 - l:7 - l, :].rearrange("p o (g h m) -> p o g h m", h=2, m=m)[:, :, :, 1, :]
                        st = self.ST.rearrange("p (n g h m) -> p n g h m", n=NBLK, h=2, m=m)[:, :, :, 1, :]
                        apart(dve)
                        dve.copy_predicated(st, mask.to_broadcast([P, NBLK, g, m]),
                                            PS[:, l % 2, :].rearrange("p (n g m) -> p n g m", n=NBLK, m=m)).then_inc(self.pr.sem, 1)

                    dve.wait_ge(*self.f_loaded(h * 16 + 16))
                    if prior is not None:
                        dve.wait_ge(*self.mr(h * LEVELS))
                    dve.tensor_scalar(self.F, self.f, omlb[:, bass.ds(h, 1)], lb[:, bass.ds(h, 1)], ALU.mult, ALU.add)\
                       .then_inc(self.fk.sem, 1)
                    dve.wait_ge(*self.fk(h * 2 + 1))
                    dve.tensor_scalar(self.k, self.F, -1.0, 1.0, ALU.mult, ALU.add).then_inc(self.fk.sem, 1)
                    dve.wait_ge(*self.fk(h * 2 + 2))
                    dve.wait_ge(*self.lnf(h + 1))
                    for n in range(NBLK):
                        s = slice(n * P, (n + 1) * P)
                        dve.tensor_tensor_scan(self.b[:, s], ones[:], self.E[0][:, s], 0.0, ALU.mult, ALU.add).then_inc(self.scan.sem, 1)
                    dve.wait_ge(*self.scan(h * 8 + 8))
                    exponents(0)
                    bc = self.b.rearrange("p (n t) -> p n t", n=NBLK)
                    dve.tensor_tensor(self.KE.rearrange("p (n t) -> p n t", n=NBLK),
                                      bc[:, :, P - 1:P].to_broadcast([P, NBLK, P]), bc, ALU.subtract).then_inc(self.de.sem, 1)
                    exponents(1)
                    dve.wait_ge(*self.pl(h * 8 + 1))
                    if prior is not None:
                        dve.wait_ge(*self.oo(prior + 1))
                    dve.tensor_tensor(self.ST.rearrange("p (n t) -> p n t", n=NBLK),
                                      pair(1).rearrange("p (n t) -> p n t", n=NBLK),
                                      ident[:].rearrange("p (o t) -> p o t", o=1).to_broadcast([P, NBLK, P]), ALU.mult).then_inc(self.pr.sem, 1)
                    decayed(0)
                    exponents(2)
                    decayed(1)
                    placed(0)
                    dve.wait_ge(*self.ee(h + 1))
                    dve.tensor_tensor(self.KE, self.k, self.KE, ALU.mult).then_inc(self.ke.sem, 1)
                    dve.wait_ge(*self.e0(h * 2 + 2))
                    dve.tensor_tensor(self.Q0, self.q, self.Q0, ALU.mult).then_inc(self.q0.sem, 1)
                    exponents(3)
                    decayed(2)
                    placed(1)
                    if prior is not None:
                        normed(prior)
                    exponents(4)
                    decayed(3)
                    placed(2)
                    if prior is not None:
                        gated(prior)
                    exponents(5)
                    decayed(4)
                    placed(3)
                    if prior is not None:
                        split(prior)
                    exponents(6)
                    decayed(5)
                    placed(4)
                    decayed(6)
                    placed(5)
                    dve.wait_ge(*self.kv(h + 1))
                    for n in range(NBLK - 1):
                        s0, s1 = slice(n * P, (n + 1) * P), slice((n + 1) * P, (n + 2) * P)
                        if n == 0:
                            dve.tensor_copy(self.S[:, s1], pair(3)[:, s0]).then_inc(self.st.sem, 1)
                        else:
                            dve.wait_ge(*self.st(h * 7 + n))
                            dve.scalar_tensor_tensor(out=self.S[:, s1], in0=self.S[:, s0], scalar=self.ends[:, n:n + 1],
                                                     in1=pair(3)[:, s0], op0=ALU.mult, op1=ALU.add).then_inc(self.st.sem, 1)
                    placed(6)

                def finish(h):
                    normed(h)
                    gated(h)
                    split(h)

                self.heads(dve, head, finish)


        class Forget(Stage):
            def __init__(self, name, project):
                self.project, self.follows = project, True
                super().__init__(name)

            def setup(self):
                def s(what):
                    return self.count(what, 0)
                self.full, self.free, self.x, self.a1, self.st = s("full"), s("free"), s("x"), s("a1"), s("st")

            def tensor(self, pe):
                feature_tiles(pe, "in2_f", 0, 0, self.full, self.free, 0, nf=1)

            def scalar(self, act):
                x, t = sc(0, T)[0:8, :], sc(T, T)[0:8, :]
                act.wait_ge(*self.x(1))
                for n, (func, src, kw) in enumerate(((ACT.Abs, x, {}), (ACT.Exp, t, {"scale": -1.0}),
                                                     (ACT.Ln, t, {"bias": ones[0:8, 0:1]}))):
                    act.activation(t, src, func, **kw).then_inc(self.a1.sem, 1)
                    act.wait_ge(*self.a1(n + 1))
                act.wait_ge(*self.x(5))
                act.dma_start(fc, sc(2 * T, T)[0:8, :]).then_inc(self.st.sem, 16)
                act.dma_start(fnc, sc(3 * T, T)[0:8, :]).then_inc(self.st.sem, 16)
                act.dma_start(onesd, sc(4 * T, T)[0:1, :]).then_inc(self.st.sem, 16)
                act.wait_ge(*self.st(48))

            def vector(self, dve):
                dve.wait_ge(act_stage, self.project.index)
                dve.sem_inc(self.free.sem, 1)
                x, t, c = sc(0, T)[0:8, :], sc(T, T)[0:8, :], sc(2 * T, T)[0:8, :]
                one = sc(4 * T, T)[0:8, :]
                dve.memset(one, 1.0).then_inc(self.free.sem, 1)
                dve.wait_ge(*self.full(1))
                dve.tensor_scalar(x, pair(0)[0:8, :], binv[0:8, :], None, ALU.add).then_inc(self.x.sem, 1)
                dve.wait_ge(*self.a1(3))
                dve.wait_ge(*self.x(1))
                dve.scalar_tensor_tensor(out=t, in0=x, scalar=0.0, in1=t, op0=ALU.min, op1=ALU.subtract).then_inc(self.x.sem, 1)
                dve.wait_ge(*self.x(2))
                dve.wait_ge(*self.free(2))
                dve.tensor_tensor_scan(c, one, t, 0.0, ALU.mult, ALU.add).then_inc(self.x.sem, 1)
                dve.wait_ge(*self.x(3))
                dve.tensor_scalar(sc(3 * T, T)[0:8, :], c, -8.0, None, ALU.mult).then_inc(self.x.sem, 1)
                dve.wait_ge(*self.x(4))
                dve.tensor_scalar(c, c, 8.0, None, ALU.mult).then_inc(self.x.sem, 1)

        class Pooling(Stage):
            follows = True

            def preload(self, sp):
                for j, t in enumerate((aH, aL)):
                    sp.dma_start(t[:].bitcast(F32), zpqk[j * CH:(j + 1) * CH, :].rearrange("(k p) t -> p k t", p=P)).then_inc(self.loaded.sem, 16)
                sp.dma_start(self.w.rearrange("p (g n) -> p g n", g=4), a["pool_w_2"].rearrange("o g p n -> p (o g) n")).then_inc(self.loaded.sem, 16)

            def setup(self):
                self.w = XTf[:, 7424:7936]
                def s(what):
                    return self.count(what, 0)
                self.loaded, self.v, self.pooled, self.full, self.hi, self.free = (s(x) for x in ("loaded", "v", "pooled", "full", "hi", "free"))

            def scalar(self, act):
                for g in range(4):
                    act.wait_ge(*self.full(g + 1))
                    act.activation(UH[:, g, :], pair(2 + g % 2), ACT.Copy, scale=pc("pool_scale_2", g)).then_inc(self.hi.sem, 1)

            def tensor(self, pe):
                for g in range(4):
                    pe.wait_ge(*self.pooled(g + 1))
                    if g >= 2:
                        pe.wait_ge(*self.free(g - 1))
                    for h in range(2):
                        mm = pe.matmul(pair(2 + g % 2)[:, h * HALF:(h + 1) * HALF], self.w[:, g * P:(g + 1) * P],
                                       sc((2 + g % 2) * T + h * HALF, HALF), start=True, stop=True)
                    mm.then_inc(self.full.sem, 1)

            def vector(self, dve):
                n = [0]

                def done(ins):
                    n[0] += 1
                    ins.then_inc(self.v.sem, 1)
                    dve.wait_ge(*self.v(n[0]))

                def split(g):
                    dve.wait_ge(*self.hi(g + 1))
                    dve.scalar_tensor_tensor(out=UL[:, g, :], in0=pair(2 + g % 2), scalar=pc("pool_scale_2", g),
                                             in1=UH[:, g, :].bitcast(F32), op0=ALU.mult, op1=ALU.subtract).then_inc(self.free.sem, 1)

                dve.wait_ge(*self.loaded(48))
                for g in range(4):
                    w = 2 << g
                    u = (aH, aL)[g // 2][:, g % 2, :].bitcast(F32)
                    cur = u
                    for j in range(g + 1):
                        step, nxt = 1 << j, sc((j % 2) * T, T)
                        done(dve.tensor_copy(nxt[:, 0:step], cur[:, 0:step]))
                        done(dve.tensor_tensor(nxt[:, step:T], cur[:, step:T], cur[:, 0:T - step], ALU.add))
                        cur = nxt
                    o = sc((2 + g % 2) * T, T)
                    if g >= 2:
                        dve.wait_ge(*self.full(g - 1))
                    done(dve.scalar_tensor_tensor(out=o[:, w:T], in0=cur[:, w:T], scalar=1.0 / w, in1=u[:, w:T],
                                                  op0=ALU.mult, op1=ALU.subtract))
                    done(dve.tensor_tensor(o[:, 0:w], cur[:, 0:w], invt[:, 0:w], ALU.mult))
                    dve.tensor_tensor(o[:, 0:w], o[:, 0:w], u[:, 0:w], ALU.subtract).then_inc(self.pooled.sem, 1)
                    if g >= 1:
                        split(g - 1)
                split(3)

        class Branches(Stage):
            def setup(self):
                def s(what):
                    return self.count(what, 0)
                self.full, self.free, self.m, self.used = s("full"), s("free"), s("m"), s("used")
                self.loaded = [s(f"loaded{f}") for f in range(4)]

            def tensor(self, pe):
                with loop(pe, 2) as i:
                    for pos in range(2):
                        pe.wait_ge(w_ready[pos], use("branches", pos, i) + 2)
                        H = wh[pos][:].rearrange("p (k n) -> p k n", k=4)
                        L = wl[pos][:].rearrange("p (k n) -> p k n", k=4)
                        for f in range(4):
                            pe.wait_ge(*self.free(i * 8 + (pos * 4 + f + 1)))
                            for k in range(4):
                                for j, (w, u) in enumerate(((H, UH), (H, UL), (L, UH))):
                                    for h in range(2):
                                        mm = pe.matmul(PS[:, 2 * f + h, :], w[:, k, f * P:(f + 1) * P],
                                                       u[:, 4 * pos + k, h * HALF:(h + 1) * HALF],
                                                       start=(k == 0 and j == 0), stop=(k == 3 and j == 2))
                            mm.then_inc(self.full.sem, 1)
                        pe.drain().then_inc(w_free[pos], 1)

            def scalar(self, act):
                with loop(act, 2) as i:
                    for pos in range(2):
                        for f in range(4):
                            act.wait_ge(*self.used(i * 8 + (pos * 4 + f + 1)))
                            act.dma_start(sc(f * T, T), zgate[bass.ds(i * HALF + (pos * D + f * P), P), :])\
                               .then_inc(self.loaded[f].sem, 16)

            def vector(self, dve):
                dve.sem_inc(self.free.sem, 4)
                dve.sem_inc(self.used.sem, 4)
                with loop(dve, 2) as i:
                    for pos in range(2):
                        for f in range(4):
                            x, g = XTf[:, bass.ds(i * (4 * T) + f * T, T)], sc(f * T, T)
                            dve.wait_ge(*self.loaded[f](i * 32 + (pos * 16 + 16)))
                            dve.wait_ge(*self.full(i * 8 + (pos * 4 + f + 1)))
                            dve.tensor_tensor(g, pair(f), g, ALU.mult).then_inc(self.free.sem, 1)
                            dve.wait_ge(*self.free(i * 8 + (pos * 4 + f + 5)))
                            if pos == 0:
                                dve.tensor_copy(x, g).then_inc(self.used.sem, 1)
                            else:
                                dve.wait_ge(*self.used(i * 8 + (f + 5)))
                                dve.tensor_tensor(x, x, g, ALU.add).then_inc(self.used.sem, 1)

        class TurnOut(Stage):
            def setup(self):
                self.full, self.free = self.count("full", 0), self.count("free", 0)
                self.st = [self.count(f"st{j}", 0) for j in range(4)]

            def tensor(self, pe):
                for b in range(NBLK):
                    if b >= 2:
                        pe.wait_ge(*self.free(b - 1))
                    for k in range(KT):
                        tr = pe.transpose(pair(b % 2)[:, k * P:(k + 1) * P], XT[:, k, b * P:(b + 1) * P], ident[:])
                    tr.then_inc(self.full.sem, 1)

            def scalar(self, act):
                for b in range(NBLK):
                    act.wait_ge(*self.full(b + 1))
                    if b >= 4:
                        act.wait_ge(*self.st[b % 4](16))
                    act.activation(sc((b % 4) * T, T), pair(b % 2), ACT.Copy).then_inc(self.free.sem, 1)
                    act.wait_ge(*self.free(b + 1))
                    act.dma_start(out[b * P:(b + 1) * P, :], sc((b % 4) * T, T)).then_inc(self.st[b % 4].sem, 16)
                for j in range(4):
                    act.wait_ge(*self.st[j](32))

        pid, battn = ACT.Identity, PCOL["b_attn"][1]

        def attn_bias(i, f):
            return prm[:, 0, bass.ds(i * 2 + (battn + f), 1)]

        def copy(scale=1.0):
            return finish_with(ACT.Copy, scale=scale)

        def window_keys(b):
            return (0, 1, [(0, 1)]) if b == 0 else (b - 1, 2, [(0, 0), (1, 1)])

        def window_loads(sp, h, s, st):
            kv = h // 4
            sp.dma_start(st.Q[s][0:64, :], aq1[bass.ds(h * 64, 64), :]).then_inc(st.loaded[s].sem, 16)
            sp.dma_start(st.K[s][0:64, :], ak1[bass.ds(kv * 64, 64), :]).then_inc(st.loaded[s].sem, 16)
            sp.dma_start(st.V[s].rearrange("p (b n) -> p b n", n=64),
                         v1.rearrange("(b p) n -> p b n", p=P)[:, :, bass.ds(kv * 64 + 512, 64)]).then_inc(st.loaded[s].sem, 16)

        def fox_loads(sp, h, s, st):
            q, k, ld = st.Q[s], st.K[s], st.loaded[s]
            sp.dma_start(q[0:64, :], zpqk[bass.ds(h * 64 + 512, 64), :]).then_inc(ld.sem, 16)
            sp.dma_start(q[64:65, :], fc[bass.ds(h, 1), :]).then_inc(ld.sem, 16)
            sp.dma_start(q[65:66, :], onesd[:, :]).then_inc(ld.sem, 16)
            sp.dma_start(k[0:64, :], zpqk[bass.ds(h * 64 + 1024, 64), :]).then_inc(ld.sem, 16)
            sp.dma_start(k[64:65, :], onesd[:, :]).then_inc(ld.sem, 16)
            sp.dma_start(k[65:66, :], fnc[bass.ds(h, 1), :]).then_inc(ld.sem, 16)
            sp.dma_start(st.V[s].rearrange("p (b n) -> p b n", n=64),
                         v2.rearrange("(b p) n -> p b n", p=P)[:, :, bass.ds(h * 64, 64)]).then_inc(ld.sem, 16)

        def mem_loads(sp, h, s, st):
            sp.dma_start(st.Q[s], xq[bass.ds(h * P, P), :]).then_inc(st.loaded[s].sem, 16)
            sp.dma_start(st.K[s][:, 0:MEM], mk[bass.ds(h * P, P), :]).then_inc(st.loaded[s].sem, 16)
            sp.dma_start(st.V[s][:, 0:256].rearrange("p (b n) -> p b n", n=P),
                         mv.rearrange("(b p) n -> p b n", p=P)[:, :, bass.ds(h * P, P)]).then_inc(st.loaded[s].sem, 16)

        memT = XTf[:, 4096:6144].rearrange("p (k t) -> p k t", k=KT)
        Setup("setup")
        SetupBound("bound")
        turn = TurnIn("turn_mem", a["mem_2"].rearrange("o t n -> (o t) n"), memT, MEM)
        norm = Norm("norm_mem", "mem_g_2", "split", src=memT, n=MEM)
        mem_k = Project("mem_k", [("mem_k", [(copy(), rows_at(mk, 0, 0), 2), (copy(), rows_at(mk, 256, 0), 2)])], ntok=MEM, norm_before=norm)
        mem_v = ProjectTokens("mem_v", mv, [("mem_v", 0, 0, CH, 0, False), ("mem_v", 1, 0, CH, 256, False)], mem_k, ntt=2)
        turn = TurnIn("turn_x", a["x"].rearrange("o t n -> (o t) n"), XT, T)
        mem_v.turn_after = turn
        norm = Norm("norm_mix", "norm_mix_w", "split", before=turn, store=True)
        in1 = Project("in1", [("in1_gates", [(finish_with(ACT.Sigmoid), rows_at(zf1, 0, CH), 2), (finish_with(ACT.Silu), rows_at(zg1, 0, CH), 2)]),
                        ("in1_q", [(copy(HG_SCALE), rows_at(zq1, 0, CH), 2), (finish_with(pid, attn_bias), rows_at(aq1, 0, CH), 2)])],
                norm_before=norm)
        ProjectTokens("in1_v", v1, [("in1_v", 0, 0, CH, 0, False), ("in1_v", 1, P, P, 512, True), ("in1_v", 2, 0, CH, 256, False)], in1,
                      key=("in1_v", 1, ak1, pc("b_attn", 4)))
        window = Attend("window", 8, 64, 64, 0.125, window_keys, window_loads, 3, sinks=True)
        TurnHeads("turn_window", window.O, 4)
        hgrn = HGRN("hgrn")
        product = OutProduct("out1", "out1", 2, KT, True)
        norm = Norm("norm_ffn1", "norm_ffn_w", "split", before=product, fused=True)
        ffn = FFN("ffn1", "ffn1", False, norm)
        final = Norm("final", "final_norm_w", "inplace", before=ffn, fused=True)
        norm = Norm("norm_mix2", "mix_pre_g_2", "split", before=final, store=True)
        in2 = Project("in2", [("in2_pqk", [(copy(), rows_at(zpqk, 0, 512), 2), (copy(), rows_at(zpqk, 256, 512), 2)]),
                        ("in2_gates", [(finish_with(ACT.Sigmoid), rows_at(zgate, 0, 512), 2), (finish_with(ACT.Sigmoid), rows_at(zgate, 256, 512), 2)])],
                norm_before=norm)
        ProjectTokens("in2_v", v2, [("in2_v", 0, 0, CH, 0, False), ("in2_v", 1, 0, CH, 256, False)], in2)
        Forget("forget", in2)
        fox = Attend("fox", 8, 66, 64, 0.125, lambda b: (0, b + 1, [(b, 1)]), fox_loads, 7)
        TurnHeads("turn_fox", fox.O, 4)
        fox.preloads = Pooling("pooling")
        Branches("branches")
        split = Split("split_merged")
        product = OutProduct("mix", "mix", 2, KT, False, split_before=split)
        post = Norm("post_mix", "mix_post_g_2", "post", before=product, fused=True)
        norm = Norm("norm_xa", "xa_pre_g_2", "split", before=post, store=True)
        Project("xq", [("xq", [(copy(), rows_at(xq, 0, 0), 2), (copy(), rows_at(xq, 256, 0), 2)])], norm_before=norm)
        memory = Attend("memory", 4, P, P, P ** -0.5, lambda b: (0, 2, []), mem_loads, 3)
        TurnHeads("turn_memory", memory.O, 0)
        product = OutProduct("xo", "xo", 4, 4, False)
        post = Norm("post_xa", "xa_post_g_2", "post", before=product, fused=True)
        norm = Norm("norm_ffn2", "ffn_pre_g_2", "split", before=post, store=True)
        ffn = FFN("ffn2", "ffn2", True, norm)
        Norm("post_ffn", "ffn_post_g_2", "post", before=ffn, fused=True)
        TurnOut("turn_out")

        groups = [["mem_k", "mem_v", "in1_gates", "in1_q", "in1_v"], window, hgrn,
                  ["out1", "ffn1_head", "ffn1", "ffn1_tail", "in2_pqk", "in2_gates", "in2_v", "in2_f"], fox,
                  ["branches", "mix", "xq"], memory, ["xo", "ffn2_head", "ffn2", "ffn2_tail"]]
        assert [g for group in groups if isinstance(group, list) for g in group] == list(segments)

        block = ctx.enter_context(nc.Block())

        @block.sync
        def _(sp):
            for group in groups:
                if isinstance(group, Stage):
                    group.sync(sp)
                    continue
                for seg in group:
                    iters, chunks = segments[seg]

                    def body(i):
                        seen = set()
                        for slot, src in chunks:
                            for other in ((0, 2) if slot != 1 else (1,)):
                                used = bases[seg][other] + ((1 if other in seen else 0) if other in [c[0] for c in chunks] else 0)
                                if other in [c[0] for c in chunks]:
                                    sp.wait_ge(w_ready[other], i + (used + 1))
                                    apart(sp)
                                else:
                                    sp.wait_ge(w_ready[other], used + 1)
                            ap = src(i)
                            k, n = ap.shape[1], ap.shape[2]
                            sp.dma_start(raw[slot % 2][:, 0:k * n].rearrange("p (k n) -> p k n", k=k), ap)\
                              .then_inc(raw_loaded[slot], 16)
                            seen.add(slot)
                    iterate(sp, iters, body)

        @block.gpsimd
        def _(pool):
            n = 0

            def const(ins):
                ins.then_inc(consts_ready, 1)

            prow = XTf[:, 0:512]
            const(pool.memset(prow, 0.0))
            for s in range(3):
                pool.sem_inc(w_ready[s], 1)
            const(pool.memset(ident[:], 0.0))
            const(pool.memset(ones[:], 1.0))
            const(pool.memset(bmask[:].rearrange("p a n -> p (a n)"), 0.0))
            const(pool.memset(eps, EPS))
            for t in range(16):
                const(pool.memset(invt[:, t:t + 1], 1.0 / (t + 1)))
            const(pool.iota(SC[:, 0:P].bitcast(I32), pattern=[[0, P]], base=0, channel_multiplier=1))
            const(pool.iota(SC[:, P:2 * P].bitcast(I32), pattern=[[1, P]], base=0, channel_multiplier=0))
            pool.wait_ge(consts_ready, 23)
            const(pool.affine_select(out=ident[:], in_=ident[:], compare_op=ALU.not_equal, fill=1.0, base=0,
                                     pattern=[[-1, P]], channel_multiplier=1))
            const(pool.affine_select(out=bmask[:, 0, :], in_=bmask[:, 0, :], compare_op=ALU.is_gt, fill=NEG, base=0,
                                     pattern=[[1, P]], channel_multiplier=-1))
            const(pool.affine_select(out=bmask[:, 1, :], in_=bmask[:, 1, :], compare_op=ALU.is_ge, fill=NEG, base=0,
                                     pattern=[[-1, P]], channel_multiplier=1))
            pool.wait_ge(consts_ready, 26)
            const(pool.tensor_copy(identb[:], ident[:]))
            for seg, (iters, chunks) in segments.items():
                def body(i):
                    for pos, (slot, src) in enumerate(chunks):
                        ap = src(i)
                        m = ap.shape[1] * ap.shape[2]
                        u = use(seg, pos, i)
                        pool.wait_ge(raw_loaded[slot], u * 16 + 16)
                        pool.wait_ge(w_free[slot], u + 1)
                        apart(pool)
                        pool.tensor_copy(wh[slot][:, 0:m], raw[slot % 2][:, 0:m]).then_inc(hi_done[slot], 1)
                        pool.wait_ge(hi_done[slot], u + 1)
                        pool.tensor_tensor(wl[slot][:, 0:m], raw[slot % 2][:, 0:m], wh[slot][:, 0:m].bitcast(F32),
                                           ALU.subtract).then_inc(w_ready[slot], 1)
                iterate(pool, iters, body)

        def run(e, method, own):
            for stage in stages:
                stage.after(e)
                part = {"tensor": stage.tensor, "scalar": stage.scalar, "vector": stage.vector}[method]
                part(e)
                e.drain().then_inc(own, 1)

        @block.tensor
        def _(pe):
            run(pe, "tensor", pe_stage)

        @block.scalar
        def _(act):
            run(act, "scalar", act_stage)

        @block.vector
        def _(dve):
            run(dve, "vector", dve_stage)


def kernel(**inputs):
    import numpy as np
    import concourse.bacc as bacc
    from concourse.bass_utils import run_bass_kernel_spmd

    nc = bacc.Bacc("TRN2", target_bir_lowering=False, num_devices=1)
    arrays, aps = {}, {}
    for name, value in inputs.items():
        v = np.ascontiguousarray(value)
        arrays["in_" + name] = v
        aps[name] = nc.dram_tensor("in_" + name, v.shape, mybir.dt.from_np(v.dtype), kind="ExternalInput").ap()
    out = nc.dram_tensor("out", (1, T, D), F32, kind="ExternalOutput").ap()
    program(nc, aps, out.rearrange("o t n -> (o t) n"))
    r = run_bass_kernel_spmd(nc, [arrays], core_ids=[0])
    return r.results[0]["out"]
```
